# Optimizing a Trainium2 kernel written in Bass

```python
import jax, jax.numpy as jnp
from jax import lax
import numpy as np

D_MODEL = 1024
BATCH = 1
SEQ = 256
DEPTH = 4
DEC_BATCH = 1
DEC_SEQ = 32
PAST_LEN = 512

CHUNK = 64
N_MIXERS = 3
N_POOL_LAYERS = (DEPTH + 2) // 3
N_ATTN_LAYERS = (DEPTH + 1) // 3
N_RWKV_LAYERS = DEPTH // 3
D_FF = 4 * D_MODEL
RMS_EPS = 1e-6
POOL_WINDOWS = (2, 4, 8, 16)
POOL_GROUPS = 4
POOL_GW = D_MODEL // POOL_GROUPS
POOL_HIST = max(POOL_WINDOWS) - 1
ATTN_HEADS = 8
ATTN_HEAD_DIM = D_MODEL // ATTN_HEADS
IDX_HEADS = 8
IDX_DIM = 64
TOPK_MAX = 256
ROPE_THETA = 500000.0
ROPE_FRACTION = 4
Q_BLOCK = 128
NEG_INF = -1e30
Q_W = ATTN_HEADS * ATTN_HEAD_DIM
OFF_K = Q_W
OFF_V = OFF_K + ATTN_HEAD_DIM
OFF_QI = OFF_V + ATTN_HEAD_DIM
OFF_KI = OFF_QI + IDX_HEADS * IDX_DIM
OFF_WI = OFF_KI + IDX_DIM
ATTN_IN_W = OFF_WI + IDX_HEADS
RWKV_HEAD = 64
RWKV_HEADS = D_MODEL // RWKV_HEAD
DECAY_LORA = 64
AAA_LORA = 64
GATE_LORA = 128
LNX_EPS = 64e-5

kernel_name = 'hybrid_pool_dsa_rwkv7_stream_step'

def rms_norm(x, g):
    xf = x.astype(jnp.float32)
    y = xf * lax.rsqrt(jnp.mean(xf * xf, axis=-1, keepdims=True) + RMS_EPS)
    return (y * g.astype(jnp.float32)).astype(x.dtype)

def squared_relu_mlp(h, w_up, w_down):
    return jnp.square(jax.nn.relu(h @ w_up)) @ w_down

def pool_mixer(h, hist, n_hist, w, scale):
    B, T, D = h.shape
    xp = jnp.concatenate([hist.astype(h.dtype), h], axis=1)
    csum = jnp.concatenate([jnp.zeros((B, 1, D), jnp.float32),
                            jnp.cumsum(xp.astype(jnp.float32), axis=1)], axis=1)
    t = jnp.arange(T)
    hi = csum[:, POOL_HIST + 1:POOL_HIST + 1 + T]
    groups = []
    for gi, win in enumerate(POOL_WINDOWS):
        cs = slice(gi * POOL_GW, (gi + 1) * POOL_GW)
        lo = csum[:, POOL_HIST + 1 - win:POOL_HIST + 1 - win + T, cs]
        cnt = jnp.minimum(t + 1 + n_hist, win).astype(jnp.float32)[None, :, None]
        groups.append((hi[..., cs] - lo) / cnt)
    pooled = jnp.concatenate(groups, axis=-1) - h.astype(jnp.float32)
    mixed = jnp.einsum('btgc,gcd->btgd', pooled.reshape(B, T, POOL_GROUPS, POOL_GW), w.astype(jnp.float32))
    out = mixed.reshape(B, T, D) * scale.astype(jnp.float32)
    return out.astype(h.dtype), xp[:, -POOL_HIST:]

def partial_rope(x, pos):
    d = x.shape[-1]
    rd = d // ROPE_FRACTION
    half = rd // 2
    inv = ROPE_THETA ** (-jnp.arange(half, dtype=jnp.float32) / half)
    ang = pos.astype(jnp.float32)[:, None] * inv[None, :]
    cos = jnp.cos(ang)[:, None, :]
    sin = jnp.sin(ang)[:, None, :]
    xf = x.astype(jnp.float32)
    x1, x2 = xf[..., :half], xf[..., half:rd]
    out = jnp.concatenate([x1 * cos - x2 * sin, x2 * cos + x1 * sin, xf[..., rd:]], axis=-1)
    return out.astype(x.dtype)

def dsa_project(h, w_in, pos):
    B, T, _ = h.shape
    p = h @ w_in
    q = partial_rope(p[..., :OFF_K].reshape(B, T, ATTN_HEADS, ATTN_HEAD_DIM), pos)
    k = partial_rope(p[..., OFF_K:OFF_V][:, :, None], pos)[:, :, 0]
    v = p[..., OFF_V:OFF_QI]
    qi = partial_rope(p[..., OFF_QI:OFF_KI].reshape(B, T, IDX_HEADS, IDX_DIM), pos)
    ki = partial_rope(p[..., OFF_KI:OFF_WI][:, :, None], pos)[:, :, 0]
    wi = p[..., OFF_WI:]
    return q, k, v, qi, ki, wi

def dsa_attend(q, qi, wi, q_pos, keys_k, keys_v, keys_i, k_pos, topk):
    admissible = (k_pos[None, :] // CHUNK) <= (q_pos[:, None] // CHUNK)
    dots = jnp.einsum('bqhd,bld->bhql', qi.astype(jnp.float32), keys_i.astype(jnp.float32)) * IDX_DIM ** -0.5
    score = jnp.einsum('bhql,bqh->bql', jax.nn.relu(dots), wi.astype(jnp.float32) * IDX_HEADS ** -0.5)
    score = jnp.where(admissible[None], score, NEG_INF)
    top_score, idx = lax.top_k(score, topk)
    valid = top_score > 0.5 * NEG_INF
    take = jax.vmap(lambda rows, ix: rows[ix])
    k_sel = take(keys_k, idx).astype(jnp.float32)
    v_sel = take(keys_v, idx).astype(jnp.float32)
    logits = jnp.einsum('bqhd,bqkd->bhqk', q.astype(jnp.float32), k_sel) * ATTN_HEAD_DIM ** -0.5
    logits = jnp.where(valid[:, None], logits, NEG_INF)
    probs = jax.nn.softmax(logits, axis=-1)
    return jnp.einsum('bhqk,bqkd->bqhd', probs, v_sel).astype(q.dtype)

def dsa_prompt(h, w_in, w_out):
    B, S, _ = h.shape
    pos = jnp.arange(S)
    q, k, v, qi, ki, wi = dsa_project(h, w_in, pos)
    topk = min(TOPK_MAX, S // 4)

    def block(b0):
        sl = lambda a: lax.dynamic_slice_in_dim(a, b0, Q_BLOCK, axis=1)
        return dsa_attend(sl(q), sl(qi), sl(wi), b0 + jnp.arange(Q_BLOCK), k, v, ki, pos, topk)

    o = lax.map(block, jnp.arange(0, S, Q_BLOCK))
    o = jnp.moveaxis(o, 0, 1).reshape(B, S, Q_W)
    return o @ w_out, k, v, ki

def dsa_sample(h, ck, cv, cki, w_in, w_out):
    B, T, _ = h.shape
    P = ck.shape[1]
    q_pos = P + jnp.arange(T)
    q, k, v, qi, ki, wi = dsa_project(h, w_in, q_pos)
    keys_k = jnp.concatenate([ck.astype(k.dtype), k], axis=1)
    keys_v = jnp.concatenate([cv.astype(v.dtype), v], axis=1)
    keys_i = jnp.concatenate([cki.astype(ki.dtype), ki], axis=1)
    topk = min(TOPK_MAX, (P + T) // 4)
    o = dsa_attend(q, qi, wi, q_pos, keys_k, keys_v, keys_i, jnp.arange(P + T), topk)
    return o.reshape(B, T, Q_W) @ w_out, k, v, ki

def rwkv7_mixer(h, shift_prev, wkv0, mix, w0, w1, w2, a0, a1, a2, g1, g2,
                k_k, k_a, r_k, w_r, w_k, w_v, w_o, lnx_g, lnx_b):
    B, T, D = h.shape
    H, N = RWKV_HEADS, RWKV_HEAD
    f32 = jnp.float32
    hf = h.astype(f32)
    xx = jnp.concatenate([shift_prev.astype(f32), hf[:, :-1]], axis=1) - hf
    mix = mix.astype(f32)
    lerp = lambda j: hf + xx * mix[j]
    r = lerp(0) @ w_r
    wl = w0 + jnp.tanh(lerp(1) @ w1) @ w2
    decay = jnp.exp(-jnp.exp(-jax.nn.softplus(-wl) - 0.5))
    k = lerp(2) @ w_k
    v = lerp(3) @ w_v
    a = jax.nn.sigmoid(a0 + (lerp(4) @ a1) @ a2)
    g = jax.nn.sigmoid(lerp(5) @ g1) @ g2
    kk = (k * k_k).reshape(B, T, H, N)
    kk = kk * lax.rsqrt(jnp.maximum(jnp.sum(kk * kk, axis=-1, keepdims=True), 1e-24))
    k = k * (1.0 + (a - 1.0) * k_a)
    r, decay, k, v, a = tuple(z.reshape(B, T, H, N).astype(f32) for z in (r, decay, k, v, a))
    neg_kk, b = -kk, kk * a

    def step(state, inp):
        r_t, w_t, k_t, v_t, a_t, b_t = inp
        sa = jnp.einsum('bhvk,bhk->bhv', state, a_t)
        state = (state * w_t[:, :, None, :] + sa[..., None] * b_t[:, :, None, :]
                 + v_t[..., None] * k_t[:, :, None, :])
        return state, jnp.einsum('bhvk,bhk->bhv', state, r_t)

    seq = tuple(jnp.moveaxis(z, 1, 0) for z in (r, decay, k, v, neg_kk, b))
    wkv_t, ys = lax.scan(step, wkv0.astype(f32), seq)
    y = jnp.moveaxis(ys, 0, 1)
    mu = jnp.mean(y, axis=-1, keepdims=True)
    var = jnp.mean(jnp.square(y - mu), axis=-1, keepdims=True)
    yn = ((y - mu) * lax.rsqrt(var + LNX_EPS)).reshape(B, T, D) * lnx_g + lnx_b
    bonus = (jnp.sum(r * k * r_k, axis=-1, keepdims=True) * v).reshape(B, T, D)
    out = ((yn + bonus) * g) @ w_o
    return out.astype(h.dtype), h[:, -1:], wkv_t

def setup_inputs(seed: int = 0) -> dict:
    key = jax.random.key(seed)
    ks = iter(jax.random.split(key, 48))
    nrm = lambda shape, s: jax.random.normal(next(ks), shape, jnp.float32) * s
    D = D_MODEL
    H, N = RWKV_HEADS, RWKV_HEAD
    return {
        'x_prompt': nrm((BATCH, SEQ, D), 1.0),
        'x_sample': nrm((DEC_BATCH, DEC_SEQ, D), 1.0),
        'state_pool': nrm((N_POOL_LAYERS, DEC_BATCH, POOL_HIST, D), 1.0),
        'cache_k': nrm((N_ATTN_LAYERS, DEC_BATCH, PAST_LEN, ATTN_HEAD_DIM), 1.0),
        'cache_v': nrm((N_ATTN_LAYERS, DEC_BATCH, PAST_LEN, ATTN_HEAD_DIM), 1.0),
        'cache_kidx': nrm((N_ATTN_LAYERS, DEC_BATCH, PAST_LEN, IDX_DIM), 1.0),
        'state_shift': nrm((N_RWKV_LAYERS, DEC_BATCH, 1, D), 1.0),
        'state_wkv': nrm((N_RWKV_LAYERS, DEC_BATCH, H, N, N), 0.3),
        'ln1_g': 1.0 + nrm((DEPTH, D), 0.05),
        'ln2_g': 1.0 + nrm((DEPTH, D), 0.05),
        'w_up': nrm((DEPTH, D, D_FF), D ** -0.5),
        'w_down': nrm((DEPTH, D_FF, D), 0.5 * D_FF ** -0.5),
        'ln_f_g': 1.0 + nrm((D,), 0.05),
        'pool_w': nrm((N_POOL_LAYERS, POOL_GROUPS, POOL_GW, POOL_GW), POOL_GW ** -0.5),
        'pool_scale': 0.5 + nrm((N_POOL_LAYERS, D), 0.1),
        'attn_w_in': nrm((N_ATTN_LAYERS, D, ATTN_IN_W), D ** -0.5),
        'attn_w_out': nrm((N_ATTN_LAYERS, Q_W, D), Q_W ** -0.5),
        'rwkv_mix': jax.random.uniform(next(ks), (N_RWKV_LAYERS, 6, D), jnp.float32),
        'rwkv_w0': nrm((N_RWKV_LAYERS, D), 1.5) - 1.0,
        'rwkv_w1': nrm((N_RWKV_LAYERS, D, DECAY_LORA), 0.5 * D ** -0.5),
        'rwkv_w2': nrm((N_RWKV_LAYERS, DECAY_LORA, D), 0.5 * DECAY_LORA ** -0.5),
        'rwkv_a0': nrm((N_RWKV_LAYERS, D), 0.3),
        'rwkv_a1': nrm((N_RWKV_LAYERS, D, AAA_LORA), 0.5 * D ** -0.5),
        'rwkv_a2': nrm((N_RWKV_LAYERS, AAA_LORA, D), 0.5 * AAA_LORA ** -0.5),
        'rwkv_g1': nrm((N_RWKV_LAYERS, D, GATE_LORA), D ** -0.5),
        'rwkv_g2': nrm((N_RWKV_LAYERS, GATE_LORA, D), GATE_LORA ** -0.5),
        'rwkv_k_k': 0.85 + nrm((N_RWKV_LAYERS, D), 0.05),
        'rwkv_k_a': 1.0 + nrm((N_RWKV_LAYERS, D), 0.05),
        'rwkv_r_k': nrm((N_RWKV_LAYERS, H, N), 0.3),
        'rwkv_w_r': nrm((N_RWKV_LAYERS, D, D), D ** -0.5),
        'rwkv_w_k': nrm((N_RWKV_LAYERS, D, D), D ** -0.5),
        'rwkv_w_v': nrm((N_RWKV_LAYERS, D, D), D ** -0.5),
        'rwkv_w_o': nrm((N_RWKV_LAYERS, D, D), D ** -0.5),
        'rwkv_lnx_g': 1.0 + nrm((N_RWKV_LAYERS, D), 0.05),
        'rwkv_lnx_b': nrm((N_RWKV_LAYERS, D), 0.01),
    }

def reference(x_prompt, x_sample, state_pool, cache_k, cache_v, cache_kidx, state_shift, state_wkv,
              ln1_g, ln2_g, w_up, w_down, ln_f_g, pool_w, pool_scale, attn_w_in, attn_w_out,
              rwkv_mix, rwkv_w0, rwkv_w1, rwkv_w2, rwkv_a0, rwkv_a1, rwkv_a2, rwkv_g1, rwkv_g2,
              rwkv_k_k, rwkv_k_a, rwkv_r_k, rwkv_w_r, rwkv_w_k, rwkv_w_v, rwkv_w_o, rwkv_lnx_g, rwkv_lnx_b):
    xp, xs = x_prompt, x_sample
    bp = xp.shape[0]
    (pool_pl, pool_sl, k_pl, k_sl, v_pl, v_sl, ki_pl, ki_sl,
     sh_pl, sh_sl, wkv_pl, wkv_sl) = ([] for _ in range(12))
    for i in range(DEPTH):
        j = i // N_MIXERS
        hp = rms_norm(xp, ln1_g[i])
        hs = rms_norm(xs, ln1_g[i])
        if i % N_MIXERS == 0:
            zero_hist = jnp.zeros((bp, POOL_HIST, D_MODEL), hp.dtype)
            mp, sp = pool_mixer(hp, zero_hist, 0, pool_w[j], pool_scale[j])
            ms, ss = pool_mixer(hs, state_pool[j], PAST_LEN, pool_w[j], pool_scale[j])
            pool_pl.append(sp)
            pool_sl.append(ss)
        elif i % N_MIXERS == 1:
            mp, kp, vp, kip = dsa_prompt(hp, attn_w_in[j], attn_w_out[j])
            ms, kn, vn, kin = dsa_sample(hs, cache_k[j], cache_v[j], cache_kidx[j], attn_w_in[j], attn_w_out[j])
            k_pl.append(kp); v_pl.append(vp); ki_pl.append(kip)
            k_sl.append(kn); v_sl.append(vn); ki_sl.append(kin)
        else:
            rw = (rwkv_mix[j], rwkv_w0[j], rwkv_w1[j], rwkv_w2[j], rwkv_a0[j], rwkv_a1[j], rwkv_a2[j],
                  rwkv_g1[j], rwkv_g2[j], rwkv_k_k[j], rwkv_k_a[j], rwkv_r_k[j], rwkv_w_r[j], rwkv_w_k[j],
                  rwkv_w_v[j], rwkv_w_o[j], rwkv_lnx_g[j], rwkv_lnx_b[j])
            zero_shift = jnp.zeros((bp, 1, D_MODEL), hp.dtype)
            zero_wkv = jnp.zeros((bp, RWKV_HEADS, RWKV_HEAD, RWKV_HEAD), jnp.float32)
            mp, shp, wp = rwkv7_mixer(hp, zero_shift, zero_wkv, *rw)
            ms, shs, wsn = rwkv7_mixer(hs, state_shift[j], state_wkv[j], *rw)
            sh_pl.append(shp); wkv_pl.append(wp)
            sh_sl.append(shs); wkv_sl.append(wsn)
        xp = xp + mp
        xs = xs + ms
        xp = xp + squared_relu_mlp(rms_norm(xp, ln2_g[i]), w_up[i], w_down[i])
        xs = xs + squared_relu_mlp(rms_norm(xs, ln2_g[i]), w_up[i], w_down[i])
    y_prompt = rms_norm(xp, ln_f_g)
    y_sample = rms_norm(xs, ln_f_g)
    pool_p = jnp.stack(pool_pl, 0)
    pool_s = jnp.stack(pool_sl, 0)
    k_p = jnp.stack(k_pl, 0)
    k_s = jnp.stack(k_sl, 0)
    v_p = jnp.stack(v_pl, 0)
    v_s = jnp.stack(v_sl, 0)
    kidx_p = jnp.stack(ki_pl, 0)
    kidx_s = jnp.stack(ki_sl, 0)
    shift_p = jnp.stack(sh_pl, 0)
    shift_s = jnp.stack(sh_sl, 0)
    wkv_p = jnp.stack(wkv_pl, 0)
    wkv_s = jnp.stack(wkv_sl, 0)
    return (y_prompt, y_sample, pool_p, pool_s, k_p, k_s, v_p, v_s, kidx_p, kidx_s, shift_p, shift_s, wkv_p, wkv_s)


_drawn_inputs = setup_inputs


def setup_inputs(seed=0):
    import zlib

    import numpy as np

    out = dict(_drawn_inputs(seed))
    spreads = {}
    factors = {'rwkv_lnx_g': 3.105, 'rwkv_lnx_b': 23.345}
    for name, (base, spread) in spreads.items():
        noise = np.random.default_rng([zlib.crc32(name.encode()), seed]).standard_normal(out[name].shape)
        drawn = base * np.exp(spread * noise) if base else spread * noise
        out[name] = __import__('jax').numpy.asarray(drawn.astype(out[name].dtype))
    for name, factor in factors.items():
        out[name] = (out[name] * factor).astype(out[name].dtype)
    return out
```

```python
import concourse.bass as bass
from concourse import mybir
import numpy as np

F32, F32R = mybir.dt.float32, mybir.dt.float32r
ALU, ACT, AX = mybir.AluOpType, mybir.ActivationFunctionType, mybir.AxisListType

P = 128
D = 1024
C = D // P
SEQ, DEC = 256, 32
T = SEQ + DEC
PAST = 512
DEPTH = 4
FF = 4 * D
KT = 4
CW = 512
RAWS, SPLITS = 4, 2
EPS = 1e-6
WINDOWS = (2, 4, 8, 16)
HIST = 15
HEADS, DH = 8, 128
IHEADS, DI = 8, 64
CHUNK = 64
TOPK_P = SEQ // 4
TOPK_S = (PAST + DEC) // 4
LS = PAST + DEC
NEG = -1e30
TAKEN = -3e30
ATTN_IN = 1864
OFF_K, OFF_WI = 1024, 1856
THETA = 500000.0
N = 64
CH = 32
NCH = T // CH
TT = 96
NT = T // TT
LNX_EPS = 64e-5
TOK_TILES = ((0, 128), (128, 128), (256, 32))

VEC_SOURCES = (("ln1_g", 4), ("ln2_g", 4), ("ln_f_g", 1), ("pool_scale", 2), ("rwkv_mix", 6), ("rwkv_w0", 1),
               ("rwkv_a0", 1), ("rwkv_k_k", 1), ("rwkv_k_a", 1), ("rwkv_r_k", 1), ("rwkv_lnx_g", 1),
               ("rwkv_lnx_b", 1))
VEC = {}
_n = 0
for _name, _rows in VEC_SOURCES:
    VEC[_name] = _n
    _n += _rows
NVEC = _n


STAGES = ("input", "pool0", "mlp0", "attn", "mlp1", "rwkv", "mlp2", "pool1", "mlp3", "output")


def shape_constants():
    pos = np.concatenate([np.arange(SEQ), PAST + np.arange(DEC)]).astype(np.float32)
    parts = {}
    parts["ident"] = np.eye(P)
    parts["ones"] = np.ones((P, P))
    head_of = np.arange(P) // N
    parts["head_ones"] = (head_of[:, None] == head_of[None, :]) * 1.0

    def rope(dim, block):
        half = dim // 4 // 2
        inv = np.float32(THETA) ** (-np.arange(half, dtype=np.float32) / np.float32(half))
        ang = (pos[:, None] * inv[None, :].astype(np.float32)).astype(np.float32)
        cos, sin = np.ones((P, T)), np.zeros((P, T))
        swap = np.zeros((P, P))
        for b in range(0, P, block):
            cos[b:b + half] = cos[b + half:b + 2 * half] = np.cos(ang).T
            sin[b:b + half] = sin[b + half:b + 2 * half] = np.sin(ang).T
            for i in range(half):
                swap[b + i, b + half + i] = -1.0
                swap[b + half + i, b + i] = 1.0
        return cos, sin, swap.T

    parts["cos_q"], parts["sin_q"], parts["swap_q"] = rope(DH, DH)
    parts["cos_i"], parts["sin_i"], parts["swap_i"] = rope(DI, DI)
    count = np.stack([np.minimum(np.concatenate([np.arange(SEQ) + 1, np.full(DEC, HIST + 1)]), w) for w in WINDOWS])
    parts["inv_count"] = np.broadcast_to((1.0 / count).reshape(1, -1), (P, 4 * T))
    parts["scan_keep"] = np.broadcast_to((np.arange(T) % CH != 0) * 1.0, (P, T))
    i, j = np.arange(P)[:, None], np.arange(TT)[None, :]
    same = (i // CH == j // CH)
    parts["row_after_col"] = (same & (j < i)) * 1.0
    parts["col_after_row"] = (same & (i < j)) * 1.0
    parts["col_after_row_2"] = parts["col_after_row"]
    parts["col_from_row"] = (same & (i <= j)) * 1.0
    rep = np.zeros((P, P))
    for g in range(4):
        rep[:DEC, g * DEC:(g + 1) * DEC] = np.eye(DEC)
    parts["repeat4"] = rep
    order, at = {}, 0
    for k, v in parts.items():
        order[k] = (at, v.shape[1])
        at += v.shape[1]
    return np.concatenate([v for v in parts.values()], axis=1).astype(np.float32), order


class Signal:

    def __init__(self, nc, name):
        self.sem, self.base = nc.alloc_semaphore(name), 0

    def at(self, k):
        return self.base + k

    def close(self, total):
        self.base += total


class Own:

    def __init__(self, nc, name):
        self.sem, self.n = nc.alloc_semaphore(name), 0

    def step(self, eng, ins):
        self.n += 1
        ins.then_inc(self.sem, 1)
        eng.wait_ge(self.sem, self.n)


def build(nc, A, O, const_order):
    UNIT = C * T * 4
    base0 = (nc.sbuf_base + 63) // 64 * 64
    small = base0 + UNIT
    raw_at = small + 5120
    hi_at = raw_at + RAWS * KT * CW * 4
    lo_at = hi_at + SPLITS * KT * CW * 4
    work = lo_at + SPLITS * KT * CW * 4

    def at(name, offset, shape, dt=F32):
        return nc.alloc_sbuf_tensor_at(name, shape, dt, offset=offset)

    def unit(k):
        return work + k * UNIT

    class Area:
        def __init__(self, start):
            self.next = start

        def take(self, name, shape, dt=F32):
            size = int(np.prod(shape[1:])) * 4
            t = at(name, self.next, shape, dt)
            self.next += (size + 31) // 32 * 32
            return t

    X = at("X", base0, [P, C, T])
    sm = Area(small)
    vecs = sm.take("vecs", [P, NVEC * C])
    fixed = sm.take("fixed", [P, 3 * P])
    var = sm.take("var", [P, T])
    rstd = sm.take("rstd", [P, T])
    ident, ones, head_ones = (fixed[:, k * P:(k + 1) * P] for k in range(3))
    raw = at("raw", raw_at, [P, RAWS, KT, CW])
    w_hi = at("w_hi", hi_at, [P, SPLITS, KT, CW], F32R)
    w_lo = at("w_lo", lo_at, [P, SPLITS, KT, CW], F32R)
    x_hi = at("x_hi", unit(0), [P, C, T], F32R)
    x_lo = at("x_lo", unit(1), [P, C, T], F32R)
    PS = nc.alloc_psum_tensor("PS", [P, 8, 512], F32)

    def vec(name, row, c):
        k = (VEC[name] + row) * C + c
        return vecs[:, k:k + 1]

    consts = A["shape_constants"]

    def const_dram(name, rows=P):
        o, w = const_order[name]
        return consts[0:rows, o:o + w]

    raw_loaded = [nc.alloc_semaphore(f"raw_loaded{s}") for s in range(RAWS)]
    hi_made = nc.alloc_semaphore("hi_made")
    lo_made = nc.alloc_semaphore("lo_made")
    chunk_used = nc.alloc_semaphore("chunk_used")
    S = {n: Signal(nc, n) for n in (
        "squares", "sum_ready", "var_ready", "rstd_ready", "h_ready", "xhi_ready", "xlo_ready",
        "group_done", "group_out", "relu_ready", "ff_hi", "stage_load", "stage_pe", "stage_act", "stage_dve",
        "stage_pool", "store", "pe2", "act2", "dve2", "load2")}
    dve_own, act_own, pool_own = Own(nc, "dve_own"), Own(nc, "act_own"), Own(nc, "pool_own")

    def rows4(w, r0, c0, width=CW):
        return w[r0:r0 + KT * P, c0:c0 + width].rearrange("(k p) n -> p k n", p=P)

    chunks = []
    first_chunk = {}

    def plan_matrix(key, w, cols):
        first_chunk.setdefault(key, len(chunks))
        for c0 in range(0, cols, CW):
            width = min(CW, cols - c0)
            for r0 in range(0, D, KT * P):
                chunks.append((rows4(w, r0, c0, width), width))

    def plan_mlp(i):
        first_chunk[f"mlp{i}"] = len(chunks)
        for g in range(FF // CW):
            for half in range(2):
                chunks.append((rows4(A["w_up"][i], half * KT * P, g * CW), CW))
        for g in range(D // CW):
            for q in range(FF // (KT * P)):
                chunks.append((rows4(A["w_down"][i], q * KT * P, g * CW), CW))

    for stage in STAGES:
        if stage.startswith("mlp"):
            plan_mlp(int(stage[3:]))
        if stage == "attn":
            plan_matrix("attn_in", A["attn_w_in"][0], OFF_WI)
            plan_matrix("attn_out", A["attn_w_out"][0], D)
        if stage == "rwkv":
            for key in ("rwkv_w_r", "rwkv_w_k", "rwkv_w_v", "rwkv_w_o"):
                plan_matrix(key, A[key][0], D)
    first_chunk["end"] = len(chunks)

    def load_chunk(sp, n):
        src, width = chunks[n]
        if n >= RAWS:
            sp.wait_ge(lo_made, n - RAWS + 1)
        sp.dma_start(raw[:, n % RAWS, :, 0:width], src).then_inc(raw_loaded[n % RAWS], 16)

    def load_ahead(sp, start, end):
        for n in range(start + RAWS, min(end + RAWS, len(chunks))):
            load_chunk(sp, n)

    def make_hi(act, n, repeat=0):
        width = chunks[n][1]
        act.wait_ge(raw_loaded[n % RAWS], 16 * (n // RAWS + 1))
        if n >= SPLITS:
            act.wait_ge(chunk_used, n - SPLITS + 1)
        if repeat:
            nc.scalar.activation(w_hi[:, n % SPLITS, :, width:width + repeat],
                                 raw[:, n % RAWS, :, width - repeat:width], ACT.Copy)
        nc.scalar.activation(w_hi[:, n % SPLITS, :, 0:width], raw[:, n % RAWS, :, 0:width], ACT.Copy) \
            .then_inc(hi_made, 1)

    def make_lo(dve, n, repeat=0):
        width = chunks[n][1]
        dve.wait_ge(hi_made, n + 1)
        if repeat:
            nc.vector.tensor_tensor(w_lo[:, n % SPLITS, :, width:width + repeat],
                                    raw[:, n % RAWS, :, width - repeat:width],
                                    w_hi[:, n % SPLITS, :, width:width + repeat].bitcast(F32), ALU.subtract)
        nc.vector.tensor_tensor(w_lo[:, n % SPLITS, :, 0:width], raw[:, n % RAWS, :, 0:width],
                                w_hi[:, n % SPLITS, :, 0:width].bitcast(F32), ALU.subtract).then_inc(lo_made, 1)

    def use_chunk(slot, rhs_hi, rhs_lo, bank, first, last, width=CW):
        for m in range((width + P - 1) // P):
            w = min(P, width - m * P)
            out = PS[0:w, bank + m, 0:T] if isinstance(bank, int) else PS[0:w, bass.ds(bank + m, 1), 0:T]
            for k in range(KT):
                hi = w_hi[:, slot, k, m * P:m * P + w]
                lo = w_lo[:, slot, k, m * P:m * P + w]
                nc.tensor.matmul(out, hi, rhs_hi(k), start=first and k == 0, stop=False)
                nc.tensor.matmul(out, lo, rhs_hi(k), start=False, stop=False)
                mm = nc.tensor.matmul(out, hi, rhs_lo(k), start=False, stop=last and k == KT - 1)
        return mm

    def project(pe, a, g0, widths, hi=None, lo=None):
        hi, lo = hi or x_hi, lo or x_lo
        for g, width in enumerate(widths, g0):
            for half in range(2):
                n = a + 2 * g + half
                pe.wait_ge(lo_made, n + 1)
                use_chunk(n % 2, lambda k: hi[:, half * KT + k, :], lambda k: lo[:, half * KT + k, :],
                          4 * (g % 2), half == 0, half == 1, width).then_inc(chunk_used, 1)

    def norm_act(act, sq, h, split=True):
        for c in range(C):
            nc.scalar.activation(sq[:, c, :], X[:, c, :], ACT.Square).then_inc(S["squares"].sem, 1)
        act.wait_ge(S["var_ready"].sem, S["var_ready"].at(1))
        nc.scalar.activation(rstd[:, :], var[:, :], ACT.Sqrt).then_inc(S["rstd_ready"].sem, 1)
        if split:
            for c in range(C):
                act.wait_ge(S["h_ready"].sem, S["h_ready"].at(c + 1))
                nc.scalar.activation(x_hi[:, c, :], h[:, c, :], ACT.Copy).then_inc(S["xhi_ready"].sem, 1)

    def norm_pe(pe, sq, bank=7):
        for c in range(C):
            pe.wait_ge(S["squares"].sem, S["squares"].at(c + 1))
            mm = nc.tensor.matmul(PS[:, bank, 0:T], ones, sq[:, c, :], start=c == 0, stop=c == C - 1)
        mm.then_inc(S["sum_ready"].sem, 1)

    def norm_dve(dve, gain, row, outs, split=True, bank=7):
        dve.wait_ge(S["sum_ready"].sem, S["sum_ready"].at(1))
        dve_own.step(dve, nc.vector.tensor_scalar(var[:, :], PS[:, bank, 0:T], 1.0 / D, EPS, ALU.mult, ALU.add))
        nc.vector.reciprocal(var[:, :], var[:, :]).then_inc(S["var_ready"].sem, 1)
        dve.wait_ge(S["rstd_ready"].sem, S["rstd_ready"].at(1))
        for c in range(C):
            for dst, (t0, t1) in outs(c):
                ins = nc.vector.scalar_tensor_tensor(dst, X[:, c, t0:t1], vec(gain, row, c), rstd[:, t0:t1],
                                                     ALU.mult, ALU.mult)
                last = ins
                if (t0, t1) != outs(c)[-1][1]:
                    ins.then_inc(dve_own.sem, 1)
                    dve_own.n += 1
            last.then_inc(S["h_ready"].sem, 1)
        if split:
            for c in range(C):
                dve.wait_ge(S["xhi_ready"].sem, S["xhi_ready"].at(c + 1))
                nc.vector.tensor_tensor(x_lo[:, c, :], outs(c)[0][0], x_hi[:, c, :].bitcast(F32), ALU.subtract) \
                    .then_inc(S["xlo_ready"].sem, 1)

    def norm_close(split=True):
        for name, n in (("squares", C), ("sum_ready", 1), ("var_ready", 1), ("rstd_ready", 1), ("h_ready", C)):
            S[name].close(n)
        if split:
            S["xhi_ready"].close(C)
            S["xlo_ready"].close(C)

    def stage_input():
        x_tok = at("x_tok", unit(2), [P, 3, D])
        rows = at("vec_rows", unit(4), [P, 2, P])
        load, pe_s, dve_s = S["stage_load"], S["stage_pe"], S["stage_dve"]
        with nc.Block() as block:
            @block.sync
            def _(sp):
                sp.dma_start(fixed[:, :], consts[:, 0:3 * P]).then_inc(load.sem, 16)
                sp.dma_start(x_tok[:, 0:2, :], A["x_prompt"][0].rearrange("(t p) d -> p t d", p=P)) \
                    .then_inc(load.sem, 16)
                sp.dma_start(x_tok[0:DEC, 2, :], A["x_sample"][0]).then_inc(load.sem, 16)
                for n in range(min(RAWS, len(chunks))):
                    load_chunk(sp, n)

            @block.scalar
            def _(act):
                for name, count in VEC_SOURCES:
                    src = A[name]
                    src = src.rearrange("a h n -> a (h n)") if name == "rwkv_r_k" else src
                    src = src.rearrange("(a d) -> a d", a=1) if name == "ln_f_g" else src
                    src = src[0] if name == "rwkv_mix" else src
                    src = src.rearrange("a (c p) -> (a c) p", p=P)
                    r0, n = VEC[name] * C, count * C
                    while n:
                        here = min(n, P - r0 % P)
                        act.dma_start(rows[r0 % P:r0 % P + here, r0 // P, :], src[0:here, :]) \
                            .then_inc(S["load2"].sem, 16)
                        src = src[here:, :] if n > here else src
                        r0, n = r0 + here, n - here

            @block.tensor
            def _(pe):
                pe.wait_ge(load.sem, load.at(48))
                for c in range(C):
                    for t, (t0, n) in enumerate(TOK_TILES):
                        mm = nc.tensor.transpose(PS[:, c, t0:t0 + n], x_tok[0:n, t, c * P:(c + 1) * P],
                                                 ident[0:n, 0:n])
                    mm.then_inc(pe_s.sem, 1)
                pe.wait_ge(S["load2"].sem, S["load2"].at(16 * (len(VEC_SOURCES) + 1)))
                pe.wait_ge(dve_s.sem, dve_s.at(1))
                nc.tensor.transpose(PS[:, 0, 0:P], rows[:, 0, :], ident)
                rest = NVEC * C - P
                nc.tensor.transpose(PS[:, 0, P:P + rest], rows[0:rest, 1, :], ident[0:rest, 0:rest]) \
                    .then_inc(pe_s.sem, 1)

            @block.vector
            def _(dve):
                for c in range(C):
                    dve.wait_ge(pe_s.sem, pe_s.at(c + 1))
                    nc.vector.tensor_copy(X[:, c, :], PS[:, c, 0:T]).then_inc(dve_s.sem, 1)
                dve.wait_ge(pe_s.sem, pe_s.at(C + 1))
                nc.vector.tensor_copy(vecs[:, :], PS[:, 0, 0:NVEC * C]).then_inc(dve_s.sem, 1)
        load.close(48)
        S["load2"].close(16 * (len(VEC_SOURCES) + 1))
        pe_s.close(C + 1)
        dve_s.close(C + 1)

    def stage_mlp(i):
        a = first_chunk[f"mlp{i}"]
        GROUPS = FF // CW
        f_hi = at(f"ff_hi{i}", unit(2), [P, FF // P, T], F32R)
        f_lo = at(f"ff_lo{i}", unit(6), [P, FF // P, T], F32R)
        relu = at(f"relu{i}", unit(10), [P, 4, T])
        squared = at(f"squared{i}", unit(10) + UNIT // 2, [P, 4, T])
        h = at(f"mlp_h{i}", unit(11), [P, C, T])
        sq = at(f"mlp_sq{i}", unit(12), [P, C, T])
        out, relu_s, ffhi_s, fflo_s = (S[k] for k in ("group_out", "relu_ready", "ff_hi", "dve2"))
        up_dram = A["w_up"][i]

        with nc.Block() as block:
            @block.sync
            def _(sp):
                with sp.Fori(0, GROUPS // 2 - 1) as it:
                    for j in range(4):
                        half, dg = j % 2, 2 + j // 2
                        src = up_dram[half * KT * P:(half + 1) * KT * P, bass.ds((2 * it + dg) * CW, CW)] \
                            .rearrange("(k p) n -> p k n", p=P)
                        sp.wait_ge(lo_made, a + 1 + j + 4 * it)
                        sp.dma_start(raw[:, j, :, :], src).then_inc(raw_loaded[j], 16)
                load_ahead(sp, a + 2 * GROUPS - RAWS, a + 4 * GROUPS)

            @block.scalar
            def _(act):
                norm_act(act, sq, h)

                def hi(it, j):
                    act.wait_ge(raw_loaded[j], 16 * (a // RAWS + 1) + 16 * it)
                    if not isinstance(it, int) or a + j + 4 * it >= SPLITS:
                        act.wait_ge(chunk_used, a + j - SPLITS + 1 + 4 * it)
                    nc.scalar.activation(w_hi[:, j % 2, :, :], raw[:, j, :, :], ACT.Copy).then_inc(hi_made, 1)

                def evict(g, half):
                    act.wait_ge(chunk_used, a + 2 + 2 * g)
                    if not isinstance(g, int) or g >= 1:
                        act.wait_ge(fflo_s.sem, fflo_s.at(0) + g)
                    nc.scalar.activation(relu[:, :, :], PS[:, 4 * half:4 * half + 4, 0:T], ACT.Relu) \
                        .then_inc(relu_s.sem, 1)
                    act.wait_ge(relu_s.sem, relu_s.at(1) + g)
                    nc.scalar.activation(f_hi[:, bass.ds(4 * g, 4), :], relu[:, :, :], ACT.Square) \
                        .then_inc(ffhi_s.sem, 1)

                for j in range(4):
                    hi(0, j)
                evict(0, 0)
                with act.Fori(1, GROUPS // 2) as it:
                    hi(it, 0)
                    hi(it, 1)
                    evict(2 * it - 1, 1)
                    hi(it, 2)
                    hi(it, 3)
                    evict(2 * it, 0)
                down = a + 2 * GROUPS
                make_hi(act, down)
                make_hi(act, down + 1)
                evict(GROUPS - 1, 1)
                for n in range(down + 2, down + 2 * GROUPS):
                    make_hi(act, n)

            @block.vector
            def _(dve):
                norm_dve(dve, "ln2_g", i, lambda c: [(h[:, c, :], (0, T))])

                def lo(it, j):
                    dve.wait_ge(hi_made, a + j + 1 + 4 * it)
                    nc.vector.tensor_tensor(w_lo[:, j % 2, :, :], raw[:, j, :, :], w_hi[:, j % 2, :, :].bitcast(F32),
                                            ALU.subtract).then_inc(lo_made, 1)

                def evict(g):
                    dve.wait_ge(relu_s.sem, relu_s.at(1) + g)
                    nc.vector.tensor_tensor(squared[:, :, :], relu[:, :, :], relu[:, :, :], ALU.mult) \
                        .then_inc(out.sem, 1)
                    dve.wait_ge(out.sem, out.at(1) + g)
                    dve.wait_ge(ffhi_s.sem, ffhi_s.at(1) + g)
                    nc.vector.tensor_tensor(f_lo[:, bass.ds(4 * g, 4), :], squared[:, :, :],
                                            f_hi[:, bass.ds(4 * g, 4), :].bitcast(F32), ALU.subtract) \
                        .then_inc(fflo_s.sem, 1)

                for j in range(4):
                    lo(0, j)
                evict(0)
                with dve.Fori(1, GROUPS // 2) as it:
                    lo(it, 0)
                    lo(it, 1)
                    evict(2 * it - 1)
                    lo(it, 2)
                    lo(it, 3)
                    evict(2 * it)
                down = a + 2 * GROUPS
                make_lo(dve, down)
                make_lo(dve, down + 1)
                evict(GROUPS - 1)
                for n in range(down + 2, down + 2 * GROUPS):
                    make_lo(dve, n)
                for g in range(2):
                    dve.wait_ge(chunk_used, a + 2 * GROUPS + (g + 1) * GROUPS)
                    nc.vector.tensor_tensor(X[:, 4 * g:4 * g + 4, :], X[:, 4 * g:4 * g + 4, :],
                                            PS[:, 4 * g:4 * g + 4, 0:T], ALU.add).then_inc(out.sem, 1)

            @block.tensor
            def _(pe):
                norm_pe(pe, sq)
                pe.wait_ge(S["xlo_ready"].sem, S["xlo_ready"].at(C))

                def up_group(it, half, peeled):
                    for kh in range(2):
                        j = 2 * half + kh
                        pe.wait_ge(lo_made, a + j + 1 + 4 * it)
                        if kh == 0 and not peeled:
                            pe.wait_ge(relu_s.sem, relu_s.at(half - 1) + 2 * it)
                        mm = use_chunk(j % 2, lambda k: x_hi[:, kh * KT + k, :], lambda k: x_lo[:, kh * KT + k, :],
                                       4 * half, kh == 0, kh == 1)
                        mm.then_inc(chunk_used, 1)

                up_group(0, 0, True)
                up_group(0, 1, True)
                with pe.Fori(1, GROUPS // 2) as it:
                    up_group(it, 0, False)
                    up_group(it, 1, False)
                down = a + 2 * GROUPS
                for g in range(2):
                    pe.wait_ge(relu_s.sem, relu_s.at(GROUPS - 1 + g))
                    for q in range(GROUPS):
                        n = down + g * GROUPS + q
                        pe.wait_ge(lo_made, n + 1)
                        if g == 0:
                            pe.wait_ge(fflo_s.sem, fflo_s.at(q + 1))
                        mm = use_chunk(n % 2, lambda k: f_hi[:, 4 * q + k, :], lambda k: f_lo[:, 4 * q + k, :],
                                       4 * g, q == 0, q == GROUPS - 1)
                        mm.then_inc(chunk_used, 1)
        norm_close()
        out.close(GROUPS + 2)
        relu_s.close(GROUPS)
        ffhi_s.close(GROUPS)
        fflo_s.close(GROUPS)

    def project_residual(key, src):
        a = first_chunk[key]
        act_s, dve_s = S["act2"], S["dve2"]
        with nc.Block() as block:
            @block.sync
            def _(sp):
                load_ahead(sp, a, a + 4)

            @block.scalar
            def _(act):
                nc.scalar.activation(x_hi[:, :, :], src[:, :, :], ACT.Copy).then_inc(act_s.sem, 1)
                for n in range(a, a + 4):
                    make_hi(act, n)

            @block.vector
            def _(dve):
                dve.wait_ge(act_s.sem, act_s.at(1))
                nc.vector.tensor_tensor(x_lo[:, :, :], src[:, :, :], x_hi[:, :, :].bitcast(F32), ALU.subtract) \
                    .then_inc(dve_s.sem, 1)
                for n in range(a, a + 4):
                    make_lo(dve, n)
                for g in range(2):
                    dve.wait_ge(chunk_used, a + 2 * g + 2)
                    nc.vector.tensor_tensor(X[:, 4 * g:4 * g + 4, :], X[:, 4 * g:4 * g + 4, :],
                                            PS[:, 4 * g:4 * g + 4, 0:T], ALU.add)

            @block.tensor
            def _(pe):
                pe.wait_ge(dve_s.sem, dve_s.at(1))
                project(pe, a, 0, [CW, CW])
        act_s.close(1)
        dve_s.close(1)

    def tokens_out(block, src, tok, dsts, start_wait):
        pe_s, act_s = S["pe2"], S["act2"]

        @block.tensor
        def _(pe):
            start_wait(pe)
            for t, (t0, n) in enumerate(TOK_TILES):
                for c in range(C):
                    mm = nc.tensor.transpose(PS[0:n, 2 * t + c // 4, (c % 4) * P:(c % 4 + 1) * P],
                                             src[:, c, t0:t0 + n], ident)
                mm.then_inc(pe_s.sem, 1)

        @block.scalar
        def _(act):
            for t, (t0, n) in enumerate(TOK_TILES):
                act.wait_ge(pe_s.sem, pe_s.at(t + 1))
                nc.scalar.activation(tok[0:n, t, :].rearrange("p (b n) -> p b n", b=2),
                                     PS[0:n, 2 * t:2 * t + 2, :], ACT.Copy).then_inc(act_s.sem, 1)

        @block.sync
        def _(sp):
            for t, (t0, n) in enumerate(TOK_TILES):
                sp.wait_ge(act_s.sem, act_s.at(t + 1))
                sp.dma_start(dsts[t], tok[0:n, t, :]).then_inc(S["store"].sem, 16)
        pe_s.close(3)
        act_s.close(3)
        S["store"].close(48)

    def stage_output():
        h = at("out_h", unit(2), [P, C, T])
        sq = at("out_sq", unit(4), [P, C, T])
        tok = at("out_tok", unit(6), [P, 3, D])
        with nc.Block() as block:
            @block.scalar
            def _(act):
                norm_act(act, sq, h, split=False)

            @block.tensor
            def _(pe):
                norm_pe(pe, sq)

            @block.vector
            def _(dve):
                norm_dve(dve, "ln_f_g", 0, lambda c: [(h[:, c, :], (0, T))], split=False)
        norm_close(split=False)
        with nc.Block() as block:
            tokens_out(block, h, tok, (O[0][0, 0:P, :], O[0][0, P:SEQ, :], O[1][0]), lambda pe: None)
        with nc.Block() as block:
            @block.sync
            def _(sp):
                sp.wait_ge(S["store"].sem, S["store"].at(0))

    def stage_pool(j):
        layer = 3 * j
        G = HIST + SEQ + HIST + DEC
        P0, S0 = HIST, HIST + SEQ + HIST
        area = Area(unit(2))
        h = area.take(f"pool_h{j}", [P, C, G])
        even = area.take(f"pool_even{j}", [P, C, G])
        odd = area.take(f"pool_odd{j}", [P, C, G])
        pooled = area.take(f"pooled{j}", [P, C, T])
        inv_count = area.take(f"inv_count{j}", [P, 4, T])
        pw = area.take(f"pool_w_raw{j}", [P, C, 256])
        pw_hi = area.take(f"pool_w_hi{j}", [P, C, 256], F32R)
        pw_lo = area.take(f"pool_w_lo{j}", [P, C, 256], F32R)
        sq = area.take(f"pool_sq{j}", [P, C, T])
        hist = area.take(f"pool_hist{j}", [P, D])
        rows = area.take(f"pool_rows{j}", [P, 2, D])
        load, pe_s, dve_s, act_s, pool_s = (S[k] for k in ("stage_load", "stage_pe", "stage_dve", "stage_act",
                                                           "stage_pool"))
        parts = ((P0, 0, SEQ), (S0, SEQ, DEC))

        with nc.Block() as block:
            @block.sync
            def _(sp):
                sp.dma_start(hist[0:HIST, :], A["state_pool"][j, 0]).then_inc(load.sem, 16)
                sp.dma_start(inv_count[:, :, :].rearrange("p a b -> p (a b)"), const_dram("inv_count")) \
                    .then_inc(load.sem, 16)
                sp.dma_start(pw[:, :, :], A["pool_w"][j].rearrange("g (k p) n -> p (g k) n", p=P)) \
                    .then_inc(load.sem, 16)

            @block.gpsimd
            def _(pool):
                nc.gpsimd.memset(h[:, :, 0:HIST], 0.0).then_inc(pool_s.sem, 1)

            @block.tensor
            def _(pe):
                pe.wait_ge(load.sem, load.at(48))
                for c in range(C):
                    mm = nc.tensor.transpose(PS[:, 0, c * 16:c * 16 + HIST], hist[0:HIST, c * P:(c + 1) * P],
                                             ident[0:HIST, 0:HIST])
                mm.then_inc(pe_s.sem, 1)
                norm_pe(pe, sq)

            @block.scalar
            def _(act):
                norm_act(act, sq, h, split=False)
                act.wait_ge(load.sem, load.at(48))
                nc.scalar.activation(pw_hi[:, :, :], pw[:, :, :], ACT.Copy).then_inc(act_s.sem, 1)

            @block.vector
            def _(dve):
                dve.wait_ge(pe_s.sem, pe_s.at(1))
                nc.vector.tensor_copy(h[:, :, HIST + SEQ:S0],
                                      PS[:, 0, 0:16 * C].rearrange("p (c t) -> p c t", c=C)[:, :, 0:HIST]) \
                    .then_inc(dve_s.sem, 1)
                norm_dve(dve, "ln1_g", layer, lambda c: [(h[:, c, P0:P0 + SEQ], (0, SEQ)),
                                                         (h[:, c, S0:G], (SEQ, T))], split=False)
                dve.wait_ge(act_s.sem, act_s.at(1))
                nc.vector.tensor_tensor(pw_lo[:, :, :], pw[:, :, :], pw_hi[:, :, :].bitcast(F32), ALU.subtract) \
                    .then_inc(dve_s.sem, 1)
        load.close(48)
        pe_s.close(1)
        act_s.close(1)
        dve_s.close(2)
        pool_s.close(1)
        norm_close(split=False)

        with nc.Block() as block:
            @block.vector
            def _(dve):
                cur, step = h, 1
                for g in range(4):
                    dst = (even, odd)[g % 2]
                    lo, skip = 2 * g, 2 * step - 1
                    dve_own.step(dve, nc.vector.tensor_tensor(
                        dst[:, lo:C, skip:G], cur[:, lo:C, skip:G], cur[:, lo:C, skip - step:G - step], ALU.add))
                    cur, step = dst, 2 * step
                for g in range(4):
                    src = (even, odd)[g % 2]
                    for col, t, n in parts:
                        nc.vector.tensor_tensor(pooled[:, 2 * g:2 * g + 2, t:t + n], src[:, 2 * g:2 * g + 2, col:col + n],
                                                inv_count[:, g:g + 1, t:t + n].to_broadcast([P, 2, n]), ALU.mult) \
                            .then_inc(dve_s.sem, 1)
                dve.wait_ge(dve_s.sem, dve_s.at(8))
                for col, t, n in parts:
                    nc.vector.tensor_tensor(pooled[:, :, t:t + n], pooled[:, :, t:t + n], h[:, :, col:col + n],
                                            ALU.subtract).then_inc(dve_s.sem, 1)
                dve.wait_ge(act_s.sem, act_s.at(1))
                nc.vector.tensor_tensor(x_lo[:, :, :], pooled[:, :, :], x_hi[:, :, :].bitcast(F32), ALU.subtract) \
                    .then_inc(dve_s.sem, 1)
                for c in range(C):
                    dve.wait_ge(pe_s.sem, pe_s.at(c + 1))
                    nc.vector.scalar_tensor_tensor(X[:, c, :], PS[:, c, 0:T], vec("pool_scale", j, c), X[:, c, :],
                                                   ALU.mult, ALU.add).then_inc(dve_s.sem, 1)

            @block.scalar
            def _(act):
                act.wait_ge(dve_s.sem, dve_s.at(10))
                nc.scalar.activation(x_hi[:, :, :], pooled[:, :, :], ACT.Copy).then_inc(act_s.sem, 1)

            @block.tensor
            def _(pe):
                pe.wait_ge(dve_s.sem, dve_s.at(11))
                for c in range(C):
                    g, m = c // 2, c % 2
                    for k in range(2):
                        hi = pw_hi[:, 2 * g + k, m * P:(m + 1) * P]
                        lo = pw_lo[:, 2 * g + k, m * P:(m + 1) * P]
                        nc.tensor.matmul(PS[:, c, 0:T], hi, x_hi[:, 2 * g + k, :], start=k == 0, stop=False)
                        nc.tensor.matmul(PS[:, c, 0:T], lo, x_hi[:, 2 * g + k, :], start=False, stop=False)
                        mm = nc.tensor.matmul(PS[:, c, 0:T], hi, x_lo[:, 2 * g + k, :], start=False, stop=k == 1)
                    mm.then_inc(pe_s.sem, 1)
        dve_s.close(11 + C)
        act_s.close(1)
        pe_s.close(C)

        with nc.Block() as block:
            @block.tensor
            def _(pe):
                for g, col in enumerate((P0 + SEQ - HIST, G - HIST)):
                    for c in range(C):
                        mm = nc.tensor.transpose(PS[0:HIST, 2 * g + c // 4, (c % 4) * P:(c % 4 + 1) * P],
                                                 h[:, c, col:col + HIST], ident)
                    mm.then_inc(pe_s.sem, 1)

            @block.scalar
            def _(act):
                for g in range(2):
                    act.wait_ge(pe_s.sem, pe_s.at(g + 1))
                    nc.scalar.activation(rows[0:HIST, g, :].rearrange("p (b n) -> p b n", b=2),
                                         PS[0:HIST, 2 * g:2 * g + 2, :], ACT.Copy).then_inc(act_s.sem, 1)

            @block.sync
            def _(sp):
                for g in range(2):
                    sp.wait_ge(act_s.sem, act_s.at(g + 1))
                    sp.dma_start(O[2 + g][j, 0], rows[0:HIST, g, :]).then_inc(S["store"].sem, 16)
                sp.wait_ge(S["store"].sem, S["store"].at(32))
        pe_s.close(2)
        act_s.close(2)
        S["store"].close(32)

    def stage_attn():
        a = first_chunk["attn_in"]
        area = Area(unit(2))
        qk = area.take("qk", [P, HEADS + 1, T])
        vt = area.take("vt", [P, T])
        ix = area.take("ix", [P, 5, T])
        h = area.take("attn_h", [P, C, T])
        sq = area.take("attn_sq", [P, C, T])
        rot = area.take("rot", [P, HEADS, T])
        tables = area.take("rope_tables", [P, 4, T])
        swaps = area.take("rope_swaps", [P, 2, P])
        rep4 = area.take("repeat4", [P, P])
        w_wi = area.take("w_wi", [P, C, IHEADS])
        wi = area.take("wi", [P, 3, IHEADS])
        kc = area.take("cache_k_rows", [P, 4, DH])
        vc = area.take("cache_v_rows", [P, 4, DH])
        kic = area.take("cache_ki_rows", [P, 4, 2, DI])
        keys_s = area.take("keys_s", [P, LS])
        ikeys_s = area.take("ikeys_s", [P, LS])
        q_s = area.take("q_s", [P, HEADS, DEC])
        k_tok = area.take("k_tok", [P, 3, DH])
        v_tok = area.take("v_tok", [P, 3, DH])
        ki_tok = area.take("ki_tok", [P, 3, DI])
        score = [area.take(f"score{q}", [P, L]) for q, L in enumerate((P, SEQ, LS))]
        dots = area.take("dots", [P, 2, LS])
        best = area.take("best", [P, 8])
        hidden = area.take("hidden", [P, LS])
        logit = area.take("logit", [P, 2, LS])
        prob = area.take("prob", [P, 2, LS])
        prob_t = area.take("prob_t", [P, 2, 5, P])
        stat = area.take("stat", [P, 18, 5])
        o = at("attn_o", unit(2) + 10400 + 1152 + 5760, [P, C, T])
        load, pe_s, dve_s, act_s, pool_s = (S[k] for k in ("stage_load", "stage_pe", "stage_dve", "stage_act",
                                                           "stage_pool"))
        WIDTHS = [CW, CW, CW, OFF_WI - 3 * CW + DI]

        with nc.Block() as block:
            @block.sync
            def _(sp):
                def get(dst, src):
                    sp.dma_start(dst, src).then_inc(load.sem, 16)
                get(tables[:, 0, :], const_dram("cos_q"))
                get(tables[:, 1, :], const_dram("sin_q"))
                get(tables[:, 2, :], const_dram("cos_i"))
                get(tables[:, 3, :], const_dram("sin_i"))
                get(swaps[:, 0, :], const_dram("swap_q"))
                get(swaps[:, 1, :], const_dram("swap_i"))
                get(rep4[:, :], const_dram("repeat4"))
                get(w_wi[:, :, :], A["attn_w_in"][0][:, OFF_WI:ATTN_IN].rearrange("(c p) n -> p c n", p=P))
                get(kc[:, :, :], A["cache_k"][0, 0].rearrange("(j p) d -> p j d", p=P))
                get(vc[:, :, :], A["cache_v"][0, 0].rearrange("(j p) d -> p j d", p=P))
                for twice in range(2):
                    get(kic[:, :, twice, :], A["cache_kidx"][0, 0].rearrange("(j p) d -> p j d", p=P))
                load_ahead(sp, a, a + 8)

            @block.scalar
            def _(act):
                norm_act(act, sq, h)

                def evict(g):
                    act.wait_ge(chunk_used, a + 2 * g + 2)
                    b = 4 * (g % 2)
                    if g < 2:
                        nc.scalar.activation(qk[:, 4 * g:4 * g + 4, :], PS[:, b:b + 4, 0:T], ACT.Copy) \
                            .then_inc(act_s.sem, 1)
                    elif g == 2:
                        nc.scalar.activation(qk[:, HEADS, :], PS[:, b, 0:T], ACT.Copy)
                        nc.scalar.activation(vt[:, :], PS[:, b + 1, 0:T], ACT.Copy)
                        nc.scalar.activation(ix[:, 0:2, :], PS[:, b + 2:b + 4, 0:T], ACT.Copy).then_inc(act_s.sem, 1)
                    else:
                        nc.scalar.activation(ix[:, 2:5, :], PS[:, b:b + 3, 0:T], ACT.Copy).then_inc(act_s.sem, 1)

                for g in range(4):
                    for n in (a + 2 * g, a + 2 * g + 1):
                        make_hi(act, n, repeat=DI if g == 3 else 0)
                    if g >= 1:
                        evict(g - 1)
                evict(3)

            @block.vector
            def _(dve):
                norm_dve(dve, "ln1_g", 1, lambda c: [(h[:, c, :], (0, T))])
                for n in range(a, a + 8):
                    make_lo(dve, n, repeat=DI if n >= a + 6 else 0)

            @block.tensor
            def _(pe):
                norm_pe(pe, sq)
                pe.wait_ge(S["xlo_ready"].sem, S["xlo_ready"].at(C))
                for g, width in enumerate(WIDTHS):
                    if g >= 2:
                        pe.wait_ge(act_s.sem, act_s.at(g - 1))
                    project(pe, a, g, [width])
        norm_close()
        act_s.close(4)

        with nc.Block() as block:
            @block.tensor
            def _(pe):
                pe.wait_ge(load.sem, load.at(16 * 12))
                for c in range(HEADS):
                    mm = nc.tensor.matmul(PS[0:32, c, 0:T], swaps[0:32, 0, 0:32], qk[0:32, c, :], start=True,
                                          stop=True)
                mm.then_inc(pe_s.sem, 1)
                pe.wait_ge(dve_s.sem, dve_s.at(1))
                nc.tensor.matmul(PS[0:32, 0, 0:T], swaps[0:32, 0, 0:32], qk[0:32, HEADS, :], start=True, stop=True)
                for c in range(5):
                    mm = nc.tensor.matmul(PS[:, 1 + c, 0:T], swaps[:, 1, :], ix[:, c, :], start=True, stop=True)
                mm.then_inc(pe_s.sem, 1)
                for t, (t0, n) in enumerate(TOK_TILES):
                    for c in range(C):
                        mm = nc.tensor.matmul(PS[0:n, 6, t * 8:t * 8 + 8], h[:, c, t0:t0 + n], w_wi[:, c, :],
                                              start=c == 0, stop=c == C - 1)
                mm.then_inc(pe_s.sem, 1)

            @block.vector
            def _(dve):
                def rotate(x, rotated, bank, cos, sin, done):
                    n, shape = x.shape[1], list(x.shape)
                    nc.vector.tensor_tensor(rot[0:shape[0], 0:n, :], PS[0:shape[0], bank:bank + n, 0:T],
                                            sin.to_broadcast(shape), ALU.mult).then_inc(dve_s.sem, 1)
                    dve_own.step(dve, nc.vector.tensor_tensor(x, x, cos.to_broadcast(shape), ALU.mult))
                    dve.wait_ge(dve_s.sem, dve_s.at(done))
                    dve_own.step(dve, nc.vector.tensor_tensor(x, x, rot[0:shape[0], 0:n, :], ALU.add))

                dve.wait_ge(load.sem, load.at(16 * 12))
                dve.wait_ge(pe_s.sem, pe_s.at(1))
                rotate(qk[0:32, 0:HEADS, :], rot, 0, tables[0:32, 0:1, :], tables[0:32, 1:2, :], 1)
                dve.wait_ge(pe_s.sem, pe_s.at(2))
                rotate(qk[0:32, HEADS:HEADS + 1, :], rot, 0, tables[0:32, 0:1, :], tables[0:32, 1:2, :], 2)
                rotate(ix[:, :, :], rot, 1, tables[:, 2:3, :], tables[:, 3:4, :], 3)
                dve.wait_ge(pe_s.sem, pe_s.at(3))
                for t, (t0, n) in enumerate(TOK_TILES):
                    nc.vector.tensor_scalar(wi[0:n, t, :], PS[0:n, 6, t * 8:t * 8 + 8], IHEADS ** -0.5, None,
                                            ALU.mult)
        load.close(16 * 12)
        pe_s.close(3)
        dve_s.close(3)

        with nc.Block() as block:
            @block.tensor
            def _(pe):
                for t, (t0, n) in enumerate(TOK_TILES):
                    nc.tensor.transpose(PS[0:n, 0, t * DH:(t + 1) * DH], qk[:, HEADS, t0:t0 + n], ident)
                    nc.tensor.transpose(PS[0:n, 1, t * DH:(t + 1) * DH], vt[:, t0:t0 + n], ident)
                    mm = nc.tensor.transpose(PS[0:n, 2, t * DI:(t + 1) * DI], ix[0:DI, 4, t0:t0 + n],
                                             ident[0:DI, 0:DI])
                mm.then_inc(pe_s.sem, 1)
                for j in range(4):
                    nc.tensor.transpose(PS[:, 3, j * P:(j + 1) * P], kc[:, j, :], ident)
                    mm = nc.tensor.transpose(PS[:, 4, j * P:(j + 1) * P],
                                             kic[:, j, :, :].rearrange("p a d -> p (a d)"), ident)
                mm.then_inc(pe_s.sem, 1)

            @block.vector
            def _(dve):
                dve.wait_ge(pe_s.sem, pe_s.at(1))
                for rows, t0, t1 in ((P, 0, 2), (DEC, 2, 3)):
                    for b, (dst, w) in enumerate(((k_tok, DH), (v_tok, DH), (ki_tok, DI))):
                        ins = nc.vector.tensor_copy(
                            dst[0:rows, t0:t1, :],
                            PS[0:rows, b, t0 * w:t1 * w].rearrange("p (t d) -> p t d", d=w))
                ins.then_inc(dve_s.sem, 1)

            @block.scalar
            def _(act):
                act.wait_ge(pe_s.sem, pe_s.at(2))
                nc.scalar.activation(keys_s[:, 0:PAST], PS[:, 3, :], ACT.Copy)
                nc.scalar.activation(ikeys_s[:, 0:PAST], PS[:, 4, :], ACT.Copy)
                nc.scalar.activation(q_s[:, :, :], qk[:, 0:HEADS, SEQ:T], ACT.Copy)
                nc.scalar.activation(keys_s[:, PAST:LS], qk[:, HEADS, SEQ:T], ACT.Copy)
                nc.scalar.activation(ikeys_s[:, PAST:LS], ix[:, 4, SEQ:T], ACT.Copy)

            @block.sync
            def _(sp):
                sp.wait_ge(dve_s.sem, dve_s.at(1))
                for k, tok in enumerate((k_tok, v_tok, ki_tok)):
                    sp.dma_start(O[4 + 2 * k][0, 0].rearrange("(t p) d -> p t d", p=P), tok[:, 0:2, :]) \
                        .then_inc(S["store"].sem, 16)
                    sp.dma_start(O[5 + 2 * k][0, 0], tok[0:DEC, 2, :]).then_inc(S["store"].sem, 16)
        pe_s.close(2)
        dve_s.close(1)
        S["store"].close(16 * 6)

        tiles = ((0, P, P), (1, P, SEQ), (2, DEC, LS))
        with nc.Block() as block:
            @block.tensor
            def _(pe):
                u = 0
                for q, nq, L in tiles:
                    t0 = TOK_TILES[q][0]
                    for hd in range(IHEADS):
                        if u >= 2:
                            pe.wait_ge(act_s.sem, act_s.at(u - 1))
                        lo = DI * (hd % 2)
                        keys = ikeys_s[lo:lo + DI, :] if q == 2 else ix[lo:lo + DI, 4, :]
                        for k0 in range(0, L, 512):
                            k1 = min(L, k0 + 512)
                            mm = nc.tensor.matmul(PS[0:nq, 2 * (u % 2) + k0 // 512, 0:k1 - k0],
                                                  ix[lo:lo + DI, hd // 2, t0:t0 + nq], keys[:, k0:k1],
                                                  start=True, stop=True)
                        mm.then_inc(pe_s.sem, 1)
                        u += 1

            @block.scalar
            def _(act):
                u = 0
                for q, nq, L in tiles:
                    for hd in range(IHEADS):
                        act.wait_ge(pe_s.sem, pe_s.at(u + 1))
                        if u >= 2:
                            act.wait_ge(dve_s.sem, dve_s.at(u - 1))
                        for k0 in range(0, L, 512):
                            k1 = min(L, k0 + 512)
                            ins = nc.scalar.activation(dots[0:nq, u % 2, k0:k1],
                                                       PS[0:nq, 2 * (u % 2) + k0 // 512, 0:k1 - k0], ACT.Relu,
                                                       scale=DI ** -0.5)
                        ins.then_inc(act_s.sem, 1)
                        u += 1

            @block.vector
            def _(dve):
                u = 0
                for q, nq, L in tiles:
                    s = score[q]
                    for hd in range(IHEADS):
                        dve.wait_ge(act_s.sem, act_s.at(u + 1))
                        w = wi[0:nq, q, hd:hd + 1]
                        if hd == 0:
                            nc.vector.tensor_scalar(s[0:nq, 0:L], dots[0:nq, u % 2, 0:L], w, None, ALU.mult) \
                                .then_inc(dve_s.sem, 1)
                        else:
                            dve.wait_ge(dve_s.sem, dve_s.at(u))
                            nc.vector.scalar_tensor_tensor(s[0:nq, 0:L], dots[0:nq, u % 2, 0:L], w, s[0:nq, 0:L],
                                                           ALU.mult, ALU.add).then_inc(dve_s.sem, 1)
                        u += 1
                dve.wait_ge(dve_s.sem, dve_s.at(u))
                dve_own.step(dve, nc.vector.memset(score[0][0:CHUNK, CHUNK:P], NEG))
                dve_own.step(dve, nc.vector.memset(score[1][0:CHUNK, 3 * CHUNK:SEQ], NEG))
                for q, nq, L in tiles:
                    s = score[q]
                    for _ in range((TOPK_S if q == 2 else TOPK_P) // 8):
                        dve_own.step(dve, nc.vector.max(best[0:nq, :], s[0:nq, 0:L]))
                        dve_own.step(dve, nc.vector.match_replace(s[0:nq, 0:L], best[0:nq, :], s[0:nq, 0:L], TAKEN))
                    dve_own.step(dve, nc.vector.tensor_scalar(s[0:nq, 0:L], s[0:nq, 0:L], 0.5 * (NEG + TAKEN), NEG,
                                                              ALU.is_gt, ALU.mult))
        pe_s.close(24)
        act_s.close(24)
        dve_s.close(24)

        units = [(q, hd) for q in range(2) for hd in range(HEADS)] + [(2, 0), (2, 4)]
        with nc.Block() as block:
            @block.tensor
            def _(pe):
                for k0, k1 in ((0, 512), (512, LS)):
                    mm = nc.tensor.matmul(PS[:, 6 + k0 // 512, 0:k1 - k0], rep4[0:DEC, :], score[2][0:DEC, k0:k1],
                                          start=True, stop=True)
                mm.then_inc(S["pe2"].sem, 1)

                def logits(u):
                    q, hd = units[u]
                    if u >= 2:
                        pe.wait_ge(dve_s.sem, dve_s.at(u - 1))
                    lhs = qk[:, hd, q * P:(q + 1) * P] if q < 2 else \
                        q_s[:, hd:hd + 4, :].rearrange("p a b -> p (a b)")
                    keys = qk[:, HEADS, 0:P * (q + 1)] if q < 2 else keys_s[:, :]
                    L = keys.shape[1]
                    for k0 in range(0, L, 512):
                        k1 = min(L, k0 + 512)
                        mm = nc.tensor.matmul(PS[:, 2 * (u % 2) + k0 // 512, 0:k1 - k0], lhs, keys[:, k0:k1],
                                              start=True, stop=True)
                    mm.then_inc(pe_s.sem, 1)

                def values(u):
                    q, hd = units[u]
                    nk = q + 1 if q < 2 else 5
                    pe.wait_ge(dve_s.sem, dve_s.at(u + 1))
                    if u >= 1:
                        pe.wait_ge(act_s.sem, act_s.at(2 * u))
                    for k in range(nk):
                        w = DEC if q == 2 and k == 4 else P
                        mm = nc.tensor.transpose(PS[0:w, 4 + k // 4, (k % 4) * P:(k % 4 + 1) * P],
                                                 prob[:, u % 2, k * P:k * P + w], ident)
                    mm.then_inc(S["pe2"].sem, 1)
                    pe.wait_ge(act_s.sem, act_s.at(2 * u + 1))
                    if u == 0:
                        pe.wait_ge(S["dve2"].sem, S["dve2"].at(1))
                    for k in range(nk):
                        w = DEC if q == 2 and k == 4 else P
                        val = v_tok[:, k, :] if q < 2 else (vc[:, k, :] if k < 4 else v_tok[0:DEC, 2, :])
                        mm = nc.tensor.matmul(PS[:, 6, 0:P], val, prob_t[0:w, u % 2, k, :], start=k == 0,
                                              stop=k == nk - 1)
                    mm.then_inc(S["pe2"].sem, 1)

                logits(0)
                for u in range(len(units)):
                    if u + 1 < len(units):
                        logits(u + 1)
                    values(u)

            @block.scalar
            def _(act):
                def out(u):
                    q, hd = units[u]
                    act.wait_ge(S["pe2"].sem, S["pe2"].at(2 * u + 3))
                    dst = o[:, hd, q * P:(q + 1) * P] if q < 2 else o[:, hd:hd + 4, SEQ:T]
                    src = PS[:, 6, 0:P] if q < 2 else PS[:, 6, 0:P].rearrange("p (a b) -> p a b", a=4)
                    nc.scalar.activation(dst, src, ACT.Copy).then_inc(act_s.sem, 1)

                def exps(u):
                    q, hd = units[u]
                    L = P * (q + 1) if q < 2 else LS
                    act.wait_ge(S["stage_pool"].sem, S["stage_pool"].at(u + 1))
                    nc.scalar.activation(prob[:, u % 2, 0:L], logit[:, u % 2, 0:L], ACT.Exp,
                                         bias=stat[:, u, 2:3], scale=DH ** -0.5,
                                         accum_out=stat[:, u, 3:4]).then_inc(S["act2"].sem, 1)

                exps(0)
                for u, (q, hd) in enumerate(units):
                    if u + 1 < len(units):
                        exps(u + 1)
                    nk = q + 1 if q < 2 else 5
                    act.wait_ge(S["pe2"].sem, S["pe2"].at(2 * u + 2))
                    if nk == 5:
                        nc.scalar.activation(prob_t[0:DEC, u % 2, 4, :], PS[0:DEC, 5, 0:P], ACT.Copy)
                        nk = 4
                    nc.scalar.activation(prob_t[:, u % 2, 0:nk, :],
                                         PS[:, 4, 0:nk * P].rearrange("p (k n) -> p k n", n=P), ACT.Copy) \
                        .then_inc(act_s.sem, 1)
                    out(u)

            @block.vector
            def _(dve):
                dve.wait_ge(S["pe2"].sem, S["pe2"].at(1))
                nc.vector.tensor_copy(hidden[:, 0:512], PS[:, 6, :])
                nc.vector.tensor_copy(hidden[:, 512:LS], PS[:, 7, 0:LS - 512]).then_inc(S["dve2"].sem, 1)
                dve.wait_ge(S["dve2"].sem, S["dve2"].at(1))

                def masked(u):
                    q, hd = units[u]
                    L = P * (q + 1) if q < 2 else LS
                    hide = score[q] if q < 2 else hidden
                    dve.wait_ge(pe_s.sem, pe_s.at(u + 1))
                    if u >= 2:
                        dve.wait_ge(S["act2"].sem, S["act2"].at(u - 1))
                    first = True
                    for k0 in range(0, L, 512):
                        k1 = min(L, k0 + 512)
                        dve_own.step(dve, nc.vector.tensor_tensor_reduce(
                            out=logit[:, u % 2, k0:k1], in0=PS[:, 2 * (u % 2) + k0 // 512, 0:k1 - k0],
                            in1=hide[:, k0:k1], scale=1.0, scalar=-3e38 if first else stat[:, u, 0:1],
                            op0=ALU.add, op1=ALU.max, accum_out=stat[:, u, 0:1] if first else stat[:, u, 1:2]))
                        col, first = (0 if first else 1), False
                    nc.vector.tensor_scalar(stat[:, u, 2:3], stat[:, u, col:col + 1], -DH ** -0.5, None,
                                            ALU.mult).then_inc(S["stage_pool"].sem, 1)

                def normalised(u):
                    q, hd = units[u]
                    L = P * (q + 1) if q < 2 else LS
                    dve.wait_ge(S["act2"].sem, S["act2"].at(u + 1))
                    dve_own.step(dve, nc.vector.reciprocal(stat[:, u, 4:5], stat[:, u, 3:4]))
                    nc.vector.tensor_scalar(prob[:, u % 2, 0:L], prob[:, u % 2, 0:L], stat[:, u, 4:5], None,
                                            ALU.mult).then_inc(dve_s.sem, 1)

                masked(0)
                for u in range(len(units)):
                    if u + 1 < len(units):
                        masked(u + 1)
                    normalised(u)
        pe_s.close(18)
        dve_s.close(18)
        act_s.close(36)
        S["stage_pool"].close(18)
        S["pe2"].close(37)
        S["act2"].close(18)
        S["dve2"].close(1)
        project_residual("attn_out", o)
        with nc.Block() as block:
            @block.sync
            def _(sp):
                sp.wait_ge(S["store"].sem, S["store"].at(0))

    def stage_rwkv():
        a0 = first_chunk["rwkv_w_r"]
        load, pe_s, dve_s, act_s, pool_s = (S[k] for k in ("stage_load", "stage_pe", "stage_dve", "stage_act",
                                                           "stage_pool"))
        ARC = [P, C, T]
        H = P // N
        y_hi, y_lo = at("lerp_hi", unit(2), ARC, F32R), at("lerp_lo", unit(3), ARC, F32R)
        logw = at("log_decay", unit(3), ARC)
        r, k, v = at("r", unit(4), ARC), at("k", unit(5), ARC), at("v", unit(6), ARC)
        rate = at("rate", unit(7), ARC)
        gate = at("gate", unit(8), ARC)
        bonus = at("bonus", unit(9), ARC)
        t1, t2 = at("t1", unit(10), ARC), at("t2", unit(11), ARC)
        ar = at("ar", unit(12), [P, 2, C, T])
        bt = at("bt", unit(4), ARC)
        temp = at("rwkv_temp", unit(2), ARC)
        HS = T + 2
        hs = at("rwkv_h", unit(11), [P, C, HS])
        delta = at("delta", unit(13), ARC)
        lerp = at("lerp", unit(10), ARC)
        sq = at("rwkv_sq", unit(9), ARC)
        lora = Area(unit(8))
        w1 = lora.take("decay_w1", [P, C, N])
        a1 = lora.take("rate_w1", [P, C, N])
        g1 = lora.take("gate_w1", [P, C, P])
        shift_row = lora.take("shift_row", [P, P])
        lora2 = Area(unit(0))
        w2 = lora2.take("decay_w2", [P, D])
        a2 = lora2.take("rate_w2", [P, D])
        g2 = lora2.take("gate_w2", [P, D])
        inner = lora2.take("lora_inner", [P, 3, T])
        shift_out = lora2.take("shift_out", [P, 2, P])
        LAST = (SEQ, HS - 1)
        parts = ((1, 0, SEQ), (SEQ + 2, SEQ, DEC))

        with nc.Block() as block:
            @block.sync
            def _(sp):
                sp.dma_start(shift_row[0:C, :], A["state_shift"][0, 0].rearrange("a (c p) -> (a c) p", p=P)) \
                    .then_inc(load.sem, 16)
                for dst, name in ((w1, "rwkv_w1"), (a1, "rwkv_a1"), (g1, "rwkv_g1")):
                    sp.dma_start(dst[:, :, :], A[name][0].rearrange("(c p) n -> p c n", p=P)).then_inc(load.sem, 16)
                load_ahead(sp, a0, a0 + 12)

            @block.gpsimd
            def _(pool):
                nc.gpsimd.memset(hs[:, :, 0:1], 0.0).then_inc(pool_s.sem, 1)

            @block.tensor
            def _(pe):
                pe.wait_ge(load.sem, load.at(64))
                nc.tensor.transpose(PS[:, 0, 0:C], shift_row[0:C, :], ident[0:C, 0:C]).then_inc(pe_s.sem, 1)
                norm_pe(pe, sq)
                for p in range(3):
                    pe.wait_ge(S["dve2"].sem, S["dve2"].at(p + 1))
                    for g in range(2):
                        if 2 * p + g >= 2:
                            pe.wait_ge(S["act2"].sem, S["act2"].at(2 * p + g - 1))
                        hi, lo = ((x_hi, x_lo), (y_hi, y_lo))[p % 2]
                        project(pe, a0 + 4 * p, g, [CW], hi, lo)

            @block.scalar
            def _(act):
                norm_act(act, sq, hs, split=False)

                def evict(p, g):
                    act.wait_ge(chunk_used, a0 + 4 * p + 2 * g + 2)
                    nc.scalar.activation((r, k, v)[p][:, 4 * g:4 * g + 4, :], PS[:, 4 * g:4 * g + 4, 0:T], ACT.Copy) \
                        .then_inc(S["act2"].sem, 1)

                for p in range(3):
                    act.wait_ge(dve_s.sem, dve_s.at(3 + C * (p + 1)))
                    if p == 2:
                        act.wait_ge(chunk_used, a0 + 4)
                    nc.scalar.activation((x_hi, y_hi)[p % 2][:, :, :], lerp[:, :, :], ACT.Copy).then_inc(act_s.sem, 1)
                    make_hi(act, a0 + 4 * p)
                    make_hi(act, a0 + 4 * p + 1)
                    if p:
                        evict(p - 1, 1)
                    make_hi(act, a0 + 4 * p + 2)
                    make_hi(act, a0 + 4 * p + 3)
                    evict(p, 0)
                evict(2, 1)

            @block.vector
            def _(dve):
                dve.wait_ge(pe_s.sem, pe_s.at(1))
                nc.vector.tensor_copy(hs[:, :, SEQ + 1], PS[:, 0, 0:C]).then_inc(dve_s.sem, 1)
                norm_dve(dve, "ln1_g", 2, lambda c: [(hs[:, c, 1:SEQ + 1], (0, SEQ)),
                                                     (hs[:, c, SEQ + 2:HS], (SEQ, T))], split=False)
                dve.wait_ge(S["h_ready"].sem, S["h_ready"].at(C))
                dve.wait_ge(dve_s.sem, dve_s.at(1))
                dve.wait_ge(pool_s.sem, pool_s.at(1))
                for col, t, n in parts:
                    nc.vector.tensor_tensor(delta[:, :, t:t + n], hs[:, :, col - 1:col - 1 + n],
                                            hs[:, :, col:col + n], ALU.subtract).then_inc(dve_s.sem, 1)
                dve.wait_ge(dve_s.sem, dve_s.at(3))
                for p, mix in enumerate((0, 2, 3)):
                    if p:
                        dve.wait_ge(S["dve2"].sem, S["dve2"].at(p))
                    for c in range(C):
                        for i, (col, t, n) in enumerate(parts):
                            ins = nc.vector.scalar_tensor_tensor(lerp[:, c, t:t + n], delta[:, c, t:t + n],
                                                                 vec("rwkv_mix", mix, c), hs[:, c, col:col + n],
                                                                 ALU.mult, ALU.add)
                        ins.then_inc(dve_s.sem, 1)
                    dve.wait_ge(act_s.sem, act_s.at(p + 1))
                    nc.vector.tensor_tensor((x_lo, y_lo)[p % 2][:, :, :], lerp[:, :, :],
                                            (x_hi, y_hi)[p % 2][:, :, :].bitcast(F32), ALU.subtract) \
                        .then_inc(S["dve2"].sem, 1)
                    for n in range(a0 + 4 * p, a0 + 4 * p + 4):
                        make_lo(dve, n)
        norm_close(split=False)
        load.close(64)
        pool_s.close(1)
        pe_s.close(1)
        dve_s.close(3 + 3 * C)
        S["dve2"].close(3)
        act_s.close(3)
        S["act2"].close(6)

        lerps = (at("lerp_w", unit(10), ARC), at("lerp_a", unit(2), ARC), at("lerp_g", unit(9), ARC))
        scan_keep = at("scan_keep", hi_at, [P, T])
        tri = at("triangles", hi_at + 31232, [P, 4, TT])
        with nc.Block() as block:
            @block.sync
            def _(sp):
                for dst, name, n in ((w2, "rwkv_w2", N), (a2, "rwkv_a2", N), (g2, "rwkv_g2", P)):
                    sp.dma_start(dst[0:n, :], A[name][0]).then_inc(load.sem, 16)
                sp.dma_start(scan_keep[:, :], const_dram("scan_keep")).then_inc(S["load2"].sem, 16)
                o0 = const_order["row_after_col"][0]
                sp.dma_start(tri[:, :, :].rearrange("p a b -> p (a b)"), consts[:, o0:o0 + 4 * TT]) \
                    .then_inc(S["load2"].sem, 16)
                sp.wait_ge(act_s.sem, act_s.at(4))
                for g in range(2):
                    sp.dma_start(O[10 + g][0, 0].rearrange("a (c p) -> (a c) p", p=P), shift_out[0:C, g, :]) \
                        .then_inc(S["store"].sem, 16)
                sp.wait_ge(S["store"].sem, S["store"].at(32))

            @block.vector
            def _(dve):
                for j, mix in enumerate((1, 4, 5)):
                    for c in range(C):
                        for i, (col, t, n) in enumerate(parts):
                            ins = nc.vector.scalar_tensor_tensor(lerps[j][:, c, t:t + n], delta[:, c, t:t + n],
                                                                 vec("rwkv_mix", mix, c), hs[:, c, col:col + n],
                                                                 ALU.mult, ALU.add)
                        ins.then_inc(dve_s.sem, 1)

            @block.tensor
            def _(pe):
                for g in range(2):
                    mm = nc.tensor.transpose(PS[0:C, 7, g * P:(g + 1) * P], hs[:, :, LAST[g]], ident)
                mm.then_inc(S["pe2"].sem, 1)
                for j, w in enumerate((w1, a1, g1)):
                    n = w.shape[2]
                    for c in range(C):
                        pe.wait_ge(dve_s.sem, dve_s.at(C * j + c + 1))
                        mm = nc.tensor.matmul(PS[0:n, j, 0:T], w[:, c, :], lerps[j][:, c, :], start=c == 0,
                                              stop=c == C - 1)
                    mm.then_inc(pe_s.sem, 1)
                pe.wait_ge(load.sem, load.at(48))
                for s in range(6):
                    j, b = s // 2, 4 * ((s + 1) % 2)
                    w, n = ((w2, N), (a2, N), (g2, P))[j]
                    pe.wait_ge(act_s.sem, act_s.at(4 if s < 2 else 4 + s - 1))
                    for m in range(4):
                        c = 4 * (s % 2) + m
                        mm = nc.tensor.matmul(PS[:, b + m, 0:T], w[0:n, c * P:(c + 1) * P], inner[0:n, j, :],
                                              start=True, stop=True)
                    mm.then_inc(pe_s.sem, 1)

            @block.scalar
            def _(act):
                act.wait_ge(S["pe2"].sem, S["pe2"].at(1))
                nc.scalar.activation(shift_out[0:C, :, :], PS[0:C, 7, 0:2 * P].rearrange("p (a b) -> p a b", a=2),
                                     ACT.Copy).then_inc(act_s.sem, 1)
                for j, (fn, n) in enumerate(((ACT.Tanh, N), (ACT.Copy, N), (ACT.Sigmoid, P))):
                    act.wait_ge(pe_s.sem, pe_s.at(j + 1))
                    nc.scalar.activation(inner[0:n, j, :], PS[0:n, j, 0:T], fn).then_inc(act_s.sem, 1)
                for s in range(6):
                    act.wait_ge(pe_s.sem, pe_s.at(4 + s))
                    j, b, c0 = s // 2, 4 * ((s + 1) % 2), 4 * (s % 2)
                    if j == 2:
                        ins = nc.scalar.activation(gate[:, c0:c0 + 4, :], PS[:, b:b + 4, 0:T], ACT.Copy)
                    else:
                        for m in range(4):
                            ins = nc.scalar.activation((logw, rate)[j][:, c0 + m, :], PS[:, b + m, 0:T], ACT.Sigmoid,
                                                       bias=vec(("rwkv_w0", "rwkv_a0")[j], 0, c0 + m))
                    ins.then_inc(act_s.sem, 1)
        load.close(48)
        S["load2"].close(32)
        S["store"].close(32)
        dve_s.close(3 * C)
        pe_s.close(9)
        S["pe2"].close(1)
        act_s.close(10)

        seg = "p c (j s) -> p (c j) s"
        LAST_DECAY = rate[:, :, :].rearrange(seg, s=CH)[:, :, CH - 1:CH].to_broadcast([P, C * NCH, CH])
        with nc.Block() as block:
            @block.scalar
            def _(act):
                for c in range(C):
                    nc.scalar.activation(t2[:, c, :], k[:, c, :], ACT.Square, scale=vec("rwkv_k_k", 0, c)) \
                        .then_inc(act_s.sem, 1)
                for c in range(C):
                    ins = nc.scalar.activation(t1[:, c, :], k[:, c, :], ACT.Copy, scale=vec("rwkv_k_k", 0, c))
                ins.then_inc(act_s.sem, 1)
                act.wait_ge(dve_s.sem, dve_s.at(2))
                nc.scalar.activation(t2[:, :, :], t2[:, :, :], ACT.Sqrt).then_inc(act_s.sem, 1)
                act.wait_ge(dve_s.sem, dve_s.at(1))
                nc.scalar.activation(logw[:, :, :], logw[:, :, :], ACT.Exp).then_inc(act_s.sem, 1)
                act.wait_ge(dve_s.sem, dve_s.at(4))
                nc.scalar.activation(rate[:, :, :], ar[:, 1, :, :], ACT.Exp).then_inc(act_s.sem, 1)
                nc.scalar.activation(t2[:, :, :], ar[:, 1, :, :], ACT.Exp, scale=-1.0).then_inc(act_s.sem, 1)

            @block.tensor
            def _(pe):
                for c in range(C):
                    pe.wait_ge(act_s.sem, act_s.at(c + 1))
                    mm = nc.tensor.matmul(PS[:, c, 0:T], head_ones, t2[:, c, :], start=True, stop=True)
                mm.then_inc(pe_s.sem, 1)
                pe.wait_ge(dve_s.sem, dve_s.at(3))
                for c in range(C):
                    mm = nc.tensor.matmul(PS[:, c, 0:T], head_ones, temp[:, c, :], start=True, stop=True)
                mm.then_inc(pe_s.sem, 1)

            @block.vector
            def _(dve):
                def step(ins):
                    dve_own.step(dve, ins)
                V = nc.vector
                dve.wait_ge(S["load2"].sem, S["load2"].at(0))
                step(V.tensor_scalar(logw[:, :, :], logw[:, :, :], -float(np.exp(-0.5)), None, ALU.mult))
                for c in range(C):
                    step(V.tensor_tensor_scan(ar[:, 1, c, :], scan_keep[:, :], logw[:, c, :], 0.0, ALU.mult, ALU.add))
                V.tensor_tensor(logw[:, :, :], ar[:, 1, :, :], logw[:, :, :], ALU.subtract).then_inc(dve_s.sem, 1)
                dve.wait_ge(pe_s.sem, pe_s.at(1))
                step(V.tensor_scalar(t2[:, :, :], PS[:, :, 0:T], 1e-24, None, ALU.max))
                V.reciprocal(t2[:, :, :], t2[:, :, :]).then_inc(dve_s.sem, 1)
                for c in range(C):
                    V.tensor_scalar(temp[:, c, :], rate[:, c, :], 1.0, vec("rwkv_k_a", 0, c), ALU.subtract, ALU.mult) \
                        .then_inc(dve_own.sem, 1)
                dve_own.n += C
                dve.wait_ge(dve_own.sem, dve_own.n)
                dve.wait_ge(act_s.sem, act_s.at(C + 1))
                step(V.scalar_tensor_tensor(k[:, :, :], temp[:, :, :], 1.0, k[:, :, :], ALU.add, ALU.mult))
                for c in range(C):
                    ins = V.scalar_tensor_tensor(temp[:, c, :], r[:, c, :], vec("rwkv_r_k", 0, c), k[:, c, :],
                                                 ALU.mult, ALU.mult)
                ins.then_inc(dve_s.sem, 1)
                dve.wait_ge(act_s.sem, act_s.at(C + 2))
                step(V.tensor_tensor(t1[:, :, :], t1[:, :, :], t2[:, :, :], ALU.mult))
                dve.wait_ge(act_s.sem, act_s.at(C + 3))
                step(V.scalar_tensor_tensor(ar[:, 0, :, :], t1[:, :, :], -1.0, logw[:, :, :], ALU.mult, ALU.mult))
                V.tensor_tensor(t1[:, :, :], t1[:, :, :], rate[:, :, :], ALU.mult).then_inc(dve_s.sem, 1)
                dve.wait_ge(pe_s.sem, pe_s.at(2))
                step(V.tensor_tensor(bonus[:, :, :], PS[:, :, 0:T], v[:, :, :], ALU.mult))
                dve.wait_ge(act_s.sem, act_s.at(C + 5))
                dve.wait_ge(dve_s.sem, dve_s.at(4))
                step(V.tensor_tensor(ar[:, 1, :, :], r[:, :, :], rate[:, :, :], ALU.mult))
                step(V.tensor_tensor(bt[:, :, :], t1[:, :, :], t2[:, :, :], ALU.mult))
                step(V.tensor_tensor(k[:, :, :], k[:, :, :], t2[:, :, :], ALU.mult))
                step(V.tensor_tensor(t1[:, :, :].rearrange(seg, s=CH), bt[:, :, :].rearrange(seg, s=CH), LAST_DECAY,
                                     ALU.mult))
                step(V.tensor_tensor(t2[:, :, :].rearrange(seg, s=CH), k[:, :, :].rearrange(seg, s=CH), LAST_DECAY,
                                     ALU.mult))
        act_s.close(C + 5)
        pe_s.close(2)
        dve_s.close(4)

        TOK = [P, NT, D]
        a_tok = at("a_tok", unit(0), TOK)
        b_tok = at("b_tok", unit(0) + 12288, TOK)
        k_tok = at("k_tokens", unit(0) + 24576, TOK)
        v_tok = at("v_tokens", unit(10), TOK)
        sources = ((t1[:, :, :], b_tok), (t2[:, :, :], k_tok), (ar[:, 0, :, :], a_tok), (v[:, :, :], v_tok))
        jobs = [(src, dst, t) for src, dst in sources for t in range(NT)]
        with nc.Block() as block:
            @block.tensor
            def _(pe):
                for i, (src, dst, t) in enumerate(jobs):
                    if i >= 4:
                        s = (act_s, dve_s)[i % 2]
                        pe.wait_ge(s.sem, s.at((i - 4) // 2 + 1))
                    for c in range(C):
                        mm = nc.tensor.transpose(PS[0:TT, 2 * (i % 4) + c // 4, (c % 4) * P:(c % 4 + 1) * P],
                                                 src[:, c, t * TT:(t + 1) * TT], ident)
                    mm.then_inc(pe_s.sem, 1)

            def copy_out(eng, odd, sig):
                for i, (src, dst, t) in enumerate(jobs):
                    if i % 2 == odd:
                        eng.wait_ge(pe_s.sem, pe_s.at(i + 1))
                        out = dst[0:TT, t, :].rearrange("p (b n) -> p b n", b=2)
                        ps = PS[0:TT, 2 * (i % 4):2 * (i % 4) + 2, :]
                        ins = nc.vector.tensor_copy(out, ps) if odd else nc.scalar.activation(out, ps, ACT.Copy)
                        ins.then_inc(sig.sem, 1)

            @block.scalar
            def _(act):
                copy_out(act, 0, act_s)

            @block.vector
            def _(dve):
                copy_out(dve, 1, dve_s)
        pe_s.close(12)
        act_s.close(6)
        dve_s.close(6)

        scratch = Area(hi_at)
        gram = scratch.take("gram", [P, H, 3, NT * TT])
        power = [scratch.take(f"power{i}", [P, H, 2, NT * TT]) for i in range(2)]
        inv = [scratch.take(f"inverse{i}", [P, 6, TT]) for i in range(2)]
        lv = scratch.take("lv", [P, 6, N])
        wt = at("wt", unit(6), ARC)
        state_rows = at("state_rows", unit(10) + 12288, [P, D // N, N])
        LEVELS = 5
        with nc.Block() as block:
            @block.sync
            def _(sp):
                sp.dma_start(state_rows[0:N, :, :], A["state_wkv"][0, 0].rearrange("h v k -> v h k")) \
                    .then_inc(load.sem, 16)

            def systems(half):
                return [(3 * half + t, t) for t in range(NT)]

            def head(x, c, half, t):
                return x[N * half:N * half + N, c, t * TT:(t + 1) * TT]

            def pair(level, half, t):
                m = gram if level == 0 else power[level % 2]
                return (m[0:TT, half, kind, t * TT:(t + 1) * TT] for kind in range(2))

            def bank(half, kind, t):
                return PS[0:TT, 3 * half + kind, t * TT:(t + 1) * TT]

            PE_N, ACT_N, DVE_N = 2 * (LEVELS + 1), 2 * (LEVELS - 1), 2 * LEVELS

            @block.tensor
            def _(pe):
                for c in range(C):
                    for half in range(H):
                        if c:
                            pe.wait_ge(dve_s.sem, dve_s.at(DVE_N * c - 1 + half))
                        for s, t in systems(half):
                            a_, b_, k_ = head(ar[:, 0, :, :], c, half, t), head(bt, c, half, t), head(k, c, half, t)
                            nc.tensor.matmul(bank(half, 0, t), a_, b_, start=True, stop=True)
                            nc.tensor.matmul(bank(half, 1, t), b_, a_, start=True, stop=True)
                            mm = nc.tensor.matmul(bank(half, 2, t), k_, a_, start=True, stop=True)
                        mm.then_inc(pe_s.sem, 1)
                    for level in range(1, LEVELS + 1):
                        for half in range(H):
                            pe.wait_ge(dve_s.sem, dve_s.at(DVE_N * c + 2 * max(0, level - 2) + half + 1))
                            if level >= 2:
                                pe.wait_ge(act_s.sem, act_s.at(ACT_N * c + 2 * (level - 2) + half + 1))
                            for s, t in systems(half):
                                m, mt = pair(level - 1, half, t)
                                if level < LEVELS:
                                    mm = nc.tensor.matmul(bank(half, 0, t), mt, m, start=True, stop=True)
                                if level < LEVELS - 1:
                                    mm = nc.tensor.matmul(bank(half, 1, t), m, mt, start=True, stop=True)
                                if level >= 2:
                                    mm = nc.tensor.matmul(bank(half, 2, t), m,
                                                          inv[(level - 1) % 2][0:TT, s, :], start=True, stop=True)
                            mm.then_inc(pe_s.sem, 1)
                        if level == 1:
                            if c:
                                pe.wait_ge(S["dve2"].sem, S["dve2"].at(c))
                            for half in range(H):
                                for s, t in systems(half):
                                    mm = nc.tensor.matmul(PS[0:TT, 7, s * N:(s + 1) * N],
                                                          gram[0:TT, half, 2, t * TT:(t + 1) * TT],
                                                          v_tok[0:TT, t, c * P + half * N:c * P + (half + 1) * N],
                                                          start=True, stop=True)
                            mm.then_inc(S["pe2"].sem, 1)
                    z = inv[LEVELS % 2]
                    pe.wait_ge(dve_s.sem, dve_s.at(DVE_N * (c + 1)))
                    if c:
                        pe.wait_ge(S["act2"].sem, S["act2"].at(2 * c))
                    for half in range(H):
                        for s, t in systems(half):
                            nc.tensor.matmul(PS[N * half:N * half + N, 6, t * TT:(t + 1) * TT],
                                             a_tok[0:TT, t, c * P + half * N:c * P + (half + 1) * N], z[0:TT, s, :],
                                             start=True, stop=True)
                    pe.wait_ge(S["act2"].sem, S["act2"].at(2 * c + 1))
                    for half in range(H):
                        for s, t in systems(half):
                            mm = nc.tensor.matmul(PS[0:TT, 7, s * N:(s + 1) * N], z[0:TT, s, :], lv[0:TT, s, :],
                                                  start=True, stop=True)
                    mm.then_inc(S["pe2"].sem, 1)

            @block.scalar
            def _(act):
                for c in range(C):
                    for level in range(1, LEVELS):
                        for half in range(H):
                            act.wait_ge(pe_s.sem, pe_s.at(PE_N * c + 2 * level + half + 1))
                            w = 2 if level < LEVELS - 1 else 1
                            nc.scalar.activation(power[level % 2][0:TT, half, 0:w, :],
                                                 PS[0:TT, 3 * half:3 * half + w, 0:NT * TT], ACT.Copy) \
                                .then_inc(act_s.sem, 1)
                        if level == 1:
                            act.wait_ge(S["pe2"].sem, S["pe2"].at(2 * c + 1))
                            nc.scalar.activation(lv[0:TT, :, :],
                                                 PS[0:TT, 7, 0:6 * N].rearrange("p (s n) -> p s n", n=N), ACT.Copy) \
                                .then_inc(S["act2"].sem, 1)
                    act.wait_ge(S["pe2"].sem, S["pe2"].at(2 * c + 2))
                    nc.scalar.activation(wt[:, c, :], PS[:, 6, 0:T], ACT.Copy).then_inc(S["act2"].sem, 1)

            @block.vector
            def _(dve):
                dve.wait_ge(S["load2"].sem, S["load2"].at(0))
                eye = ident[0:TT, 0:TT].unsqueeze(1)
                for c in range(C):
                    for half in range(H):
                        s3 = slice(3 * half, 3 * half + 3)
                        dve.wait_ge(pe_s.sem, pe_s.at(PE_N * c + half + 1))
                        split_t = "p k (t n) -> p k t n"
                        dve_own.step(dve, nc.vector.tensor_tensor(
                            gram[0:TT, half, :, :].rearrange(split_t, n=TT),
                            PS[0:TT, 3 * half:3 * half + 3, 0:NT * TT].rearrange(split_t, n=TT),
                            tri[0:TT, 0:3, :].unsqueeze(2).to_broadcast([TT, 3, NT, TT]), ALU.mult))
                        nc.vector.tensor_tensor(inv[1][0:TT, s3, :],
                                                gram[0:TT, half, 1, :].rearrange("p (t n) -> p t n", n=TT),
                                                eye.to_broadcast([TT, NT, TT]), ALU.add).then_inc(dve_s.sem, 1)
                    for level in range(2, LEVELS + 1):
                        for half in range(H):
                            s3 = slice(3 * half, 3 * half + 3)
                            dve.wait_ge(pe_s.sem, pe_s.at(PE_N * c + 2 * level + half + 1))
                            dve.wait_ge(dve_s.sem, dve_s.at(DVE_N * c + 2 * (level - 2) + half + 1))
                            nc.vector.tensor_tensor(inv[level % 2][0:TT, s3, :], inv[(level - 1) % 2][0:TT, s3, :],
                                                    PS[0:TT, 3 * half + 2, 0:NT * TT]
                                                    .rearrange("p (t n) -> p t n", n=TT), ALU.add).then_inc(dve_s.sem, 1)
                    dve.wait_ge(S["pe2"].sem, S["pe2"].at(2 * c + 2))
                    nc.vector.tensor_copy(
                        a_tok[0:TT, :, c * P:(c + 1) * P].rearrange("p t (h n) -> p h t n", n=N),
                        PS[0:TT, 7, 0:6 * N].rearrange("p (h t n) -> p h t n", h=H, n=N)).then_inc(S["dve2"].sem, 1)
        load.close(16)
        pe_s.close(C * 2 * (LEVELS + 1))
        act_s.close(C * 2 * (LEVELS - 1))
        dve_s.close(C * 2 * LEVELS)
        S["pe2"].close(2 * C)
        S["act2"].close(2 * C)
        S["dve2"].close(C)

        u_tok = a_tok
        chain = Area(hi_at)
        states = chain.take("states", [P, C, NCH + 2, N])
        state_out = chain.take("state_out", [P, 2, D])
        decayed = at("decayed", unit(10) + 12288 + 4096, [P, C, N])
        SLOTS = [(n, n + 1) for n in range(NCH - 2)] + [(NCH - 2, NCH), (NCH - 1, NCH + 1)]
        with nc.Block() as block:
            def cols(c, half):
                return slice(c * P + half * N, c * P + (half + 1) * N)

            @block.tensor
            def _(pe):
                pe.wait_ge(load.sem, load.at(0))
                for c in range(C):
                    mm = nc.tensor.transpose(PS[:, 6, c * N:(c + 1) * N],
                                             state_rows[0:N, 2 * c:2 * c + 2, :].rearrange("v h k -> v (h k)"),
                                             ident[0:N, 0:N])
                mm.then_inc(S["pe2"].sem, 1)
                for n, (cur, nxt) in enumerate(SLOTS):
                    t, p0 = n // 3, CH * (n % 3)
                    rows = slice(p0, p0 + CH)
                    for q in range(2):
                        pe.wait_ge(dve_s.sem, dve_s.at(1 + (4 * (n - 1) + 3 + q if n else 0)))
                        for c in range(4 * q, 4 * q + 4):
                            for half in range(H):
                                f = slice(N * half, N * half + N)
                                mm = nc.tensor.matmul(PS[rows, 2 * q + half, (c % 4) * N:(c % 4 + 1) * N],
                                                      wt[f, c, n * CH:(n + 1) * CH], states[f, c, cur, :],
                                                      start=True, stop=True)
                        mm.then_inc(pe_s.sem, 1)
                        for c in range(4 * q, 4 * q + 4):
                            for half in range(H):
                                nc.tensor.matmul(PS[N * half:N * half + N, 4 + q, (c % 4) * N:(c % 4 + 1) * N],
                                                 k_tok[rows, t, cols(c, half)], v_tok[rows, t, cols(c, half)],
                                                 start=c % 4 == 0, stop=False, skip_group_check=True)
                    for q in range(2):
                        pe.wait_ge(dve_s.sem, dve_s.at(1 + 4 * n + q + 1))
                        for c in range(4 * q, 4 * q + 4):
                            for half in range(H):
                                mm = nc.tensor.matmul(PS[N * half:N * half + N, 4 + q, (c % 4) * N:(c % 4 + 1) * N],
                                                      b_tok[rows, t, cols(c, half)], u_tok[rows, t, cols(c, half)],
                                                      start=False, stop=c % 4 == 3, skip_group_check=True)
                        mm.then_inc(pe_s.sem, 1)
                pe.wait_ge(dve_s.sem, dve_s.at(1 + 4 * NCH))
                for g in range(2):
                    for c in range(C):
                        mm = nc.tensor.transpose(PS[0:N, 2 * g + c // 4, (c % 4) * P:(c % 4 + 1) * P],
                                                 states[:, c, NCH + g, :], ident)
                    mm.then_inc(S["pe2"].sem, 1)

            @block.gpsimd
            def _(pool):
                nc.gpsimd.memset(states[:, :, 0, :], 0.0).then_inc(pool_s.sem, 1)
                for n, (cur, nxt) in enumerate(SLOTS):
                    for q in range(2):
                        pool.wait_ge(dve_s.sem, dve_s.at(1 + (4 * (n - 1) + 3 + q if n else 0)))
                        if n == 0:
                            pool.wait_ge(pool_s.sem, pool_s.at(1))
                        c4 = slice(4 * q, 4 * q + 4)
                        last = n * CH + CH - 1
                        nc.gpsimd.tensor_tensor(decayed[:, c4, :], states[:, c4, cur, :],
                                                rate[:, c4, last:last + 1].to_broadcast([P, 4, N]), ALU.mult) \
                            .then_inc(pool_s.sem, 1)

            @block.vector
            def _(dve):
                dve.wait_ge(S["pe2"].sem, S["pe2"].at(1))
                dve.wait_ge(pool_s.sem, pool_s.at(1))
                nc.vector.tensor_copy(states[:, :, NCH - 1, :], PS[:, 6, :].rearrange("p (c n) -> p c n", n=N)) \
                    .then_inc(dve_s.sem, 1)
                for n, (cur, nxt) in enumerate(SLOTS):
                    t, p0 = n // 3, CH * (n % 3)
                    rows = slice(p0, p0 + CH)
                    for q in range(2):
                        dve.wait_ge(pe_s.sem, pe_s.at(4 * n + q + 1))
                        u = u_tok[rows, t, q * 4 * P:(q + 1) * 4 * P].rearrange("p (c h n) -> p h c n", h=H, n=N)
                        nc.vector.tensor_tensor(u, u, PS[rows, 2 * q:2 * q + 2, 0:4 * N]
                                                .rearrange("p h (c n) -> p h c n", n=N), ALU.add) \
                            .then_inc(dve_s.sem, 1)
                    for q in range(2):
                        dve.wait_ge(pe_s.sem, pe_s.at(4 * n + 3 + q))
                        dve.wait_ge(pool_s.sem, pool_s.at(2 + 2 * n + q))
                        nc.vector.tensor_tensor(states[:, 4 * q:4 * q + 4, nxt, :], decayed[:, 4 * q:4 * q + 4, :],
                                                PS[:, 4 + q, 0:4 * N].rearrange("p (c n) -> p c n", n=N), ALU.add) \
                            .then_inc(dve_s.sem, 1)

            @block.scalar
            def _(act):
                for g in range(2):
                    act.wait_ge(S["pe2"].sem, S["pe2"].at(2 + g))
                    nc.scalar.activation(state_out[0:N, g, :].rearrange("p (b n) -> p b n", b=2),
                                         PS[0:N, 2 * g:2 * g + 2, :], ACT.Copy).then_inc(act_s.sem, 1)

            @block.sync
            def _(sp):
                for g in range(2):
                    sp.wait_ge(act_s.sem, act_s.at(g + 1))
                    sp.dma_start(O[12 + g][0, 0].rearrange("h v k -> v h k"),
                                 state_out[0:N, g, :].rearrange("v (h k) -> v h k", k=N)).then_inc(S["store"].sem, 16)
        pe_s.close(4 * NCH)
        dve_s.close(1 + 4 * NCH)
        pool_s.close(1 + 2 * NCH)
        act_s.close(2)
        S["pe2"].close(3)
        S["store"].close(32)

        y = at("y", unit(2), ARC)
        cross = at("cross", unit(3), [P, 2, 2 * H, NT * TT])
        with nc.Block() as block:
            def head(x, c, half, t):
                return x[N * half:N * half + N, c, t * TT:(t + 1) * TT]

            @block.tensor
            def _(pe):
                def grams(c):
                    if c:
                        pe.wait_ge(dve_s.sem, dve_s.at(c))
                    for half in range(H):
                        for t in range(NT):
                            rr = head(ar[:, 1, :, :], c, half, t)
                            for kind, x in enumerate((bt, k)):
                                mm = nc.tensor.matmul(PS[0:TT, 2 * half + kind, t * TT:(t + 1) * TT],
                                                      head(x, c, half, t), rr, start=True, stop=True)
                    mm.then_inc(pe_s.sem, 1)

                grams(0)
                for c in range(C):
                    if c + 1 < C:
                        grams(c + 1)
                    pe.wait_ge(dve_s.sem, dve_s.at(c + 1))
                    if c >= 4:
                        pe.wait_ge(act_s.sem, act_s.at(c - 3))
                    for half in range(H):
                        f = slice(N * half, N * half + N)
                        hc = slice(c * P + half * N, c * P + (half + 1) * N)
                        for t in range(NT):
                            nc.tensor.matmul(PS[f, 4 + c % 4, t * TT:(t + 1) * TT], u_tok[0:TT, t, hc],
                                             cross[0:TT, c % 2, 2 * half, t * TT:(t + 1) * TT], start=True, stop=False)
                            nc.tensor.matmul(PS[f, 4 + c % 4, t * TT:(t + 1) * TT], v_tok[0:TT, t, hc],
                                             cross[0:TT, c % 2, 2 * half + 1, t * TT:(t + 1) * TT], start=False, stop=False)
                            for n in range(3 * t, 3 * t + 3):
                                mm = nc.tensor.matmul(PS[f, 4 + c % 4, n * CH:(n + 1) * CH], states[f, c, n, :],
                                                      ar[f, 1, c, n * CH:(n + 1) * CH], start=False,
                                                      stop=n == 3 * t + 2)
                    mm.then_inc(S["pe2"].sem, 1)

            @block.vector
            def _(dve):
                for c in range(C):
                    dve.wait_ge(pe_s.sem, pe_s.at(c + 1))
                    if c >= 2:
                        dve.wait_ge(S["pe2"].sem, S["pe2"].at(c - 1))
                    nc.vector.tensor_tensor(
                        cross[0:TT, c % 2, :, :].rearrange("p b (t n) -> p b t n", n=TT),
                        PS[0:TT, 0:2 * H, 0:NT * TT].rearrange("p b (t n) -> p b t n", n=TT),
                        tri[0:TT, 3:4, :].unsqueeze(1).to_broadcast([TT, 2 * H, NT, TT]), ALU.mult).then_inc(dve_s.sem, 1)

            @block.scalar
            def _(act):
                for c in range(C):
                    act.wait_ge(S["pe2"].sem, S["pe2"].at(c + 1))
                    nc.scalar.activation(y[:, c, :], PS[:, 4 + c % 4, 0:T], ACT.Copy).then_inc(act_s.sem, 1)
        pe_s.close(C)
        S["pe2"].close(C)
        dve_s.close(C)
        act_s.close(C)

        ysq, yvar = at("y_squared", unit(3), ARC), at("y_var", unit(4), ARC)
        with nc.Block() as block:
            @block.tensor
            def _(pe):
                for c in range(C):
                    mm = nc.tensor.matmul(PS[:, c, 0:T], head_ones, y[:, c, :], start=True, stop=True)
                    mm.then_inc(pe_s.sem, 1)
                for c in range(C):
                    pe.wait_ge(act_s.sem, act_s.at(c + 1))
                    mm = nc.tensor.matmul(PS[:, c, 0:T], head_ones, ysq[:, c, :], start=True, stop=True)
                mm.then_inc(pe_s.sem, 1)

            @block.scalar
            def _(act):
                for c in range(C):
                    act.wait_ge(dve_s.sem, dve_s.at(c + 1))
                    nc.scalar.activation(ysq[:, c, :], y[:, c, :], ACT.Square).then_inc(act_s.sem, 1)
                act.wait_ge(dve_s.sem, dve_s.at(C + 1))
                nc.scalar.activation(yvar[:, :, :], yvar[:, :, :], ACT.Sqrt).then_inc(act_s.sem, 1)

            @block.vector
            def _(dve):
                V = nc.vector
                for c in range(C):
                    dve.wait_ge(pe_s.sem, pe_s.at(c + 1))
                    V.scalar_tensor_tensor(y[:, c, :], PS[:, c, 0:T], -1.0 / N, y[:, c, :], ALU.mult, ALU.add) \
                        .then_inc(dve_s.sem, 1)
                dve.wait_ge(pe_s.sem, pe_s.at(C + 1))
                dve_own.step(dve, V.tensor_scalar(yvar[:, :, :], PS[:, :, 0:T], 1.0 / N, LNX_EPS, ALU.mult, ALU.add))
                V.reciprocal(yvar[:, :, :], yvar[:, :, :]).then_inc(dve_s.sem, 1)
                dve.wait_ge(act_s.sem, act_s.at(C + 1))
                dve_own.step(dve, V.tensor_tensor(y[:, :, :], y[:, :, :], yvar[:, :, :], ALU.mult))
                for c in range(C):
                    dve_own.step(dve, V.tensor_scalar(y[:, c, :], y[:, c, :], vec("rwkv_lnx_g", 0, c),
                                                      vec("rwkv_lnx_b", 0, c), ALU.mult, ALU.add))
                dve_own.step(dve, V.tensor_tensor(y[:, :, :], y[:, :, :], bonus[:, :, :], ALU.add))
                dve_own.step(dve, V.tensor_tensor(y[:, :, :], y[:, :, :], gate[:, :, :], ALU.mult))

            @block.sync
            def _(sp):
                sp.wait_ge(S["store"].sem, S["store"].at(0))
        pe_s.close(C + 1)
        act_s.close(C + 1)
        dve_s.close(C + 1)
        project_residual("rwkv_w_o", y)

    STAGE = {"input": stage_input, "mlp": stage_mlp, "output": stage_output, "pool": stage_pool, "attn": stage_attn, "rwkv": stage_rwkv}
    for stage in STAGES:
        key = stage.rstrip("0123")
        STAGE[key](*([int(stage[len(key):])] if key in ("mlp", "pool") else []))


_INS = ["x_prompt", "x_sample", "state_pool", "cache_k", "cache_v", "cache_kidx", "state_shift", "state_wkv",
        "ln1_g", "ln2_g", "w_up", "w_down", "ln_f_g", "pool_w", "pool_scale", "attn_w_in", "attn_w_out",
        "rwkv_mix", "rwkv_w0", "rwkv_w1", "rwkv_w2", "rwkv_a0", "rwkv_a1", "rwkv_a2", "rwkv_g1", "rwkv_g2",
        "rwkv_k_k", "rwkv_k_a", "rwkv_r_k", "rwkv_w_r", "rwkv_w_k", "rwkv_w_v", "rwkv_w_o", "rwkv_lnx_g",
        "rwkv_lnx_b"]
_OUTS = [(1, SEQ, D), (1, DEC, D), (2, 1, HIST, D), (2, 1, HIST, D), (1, 1, SEQ, DH), (1, 1, DEC, DH),
         (1, 1, SEQ, DH), (1, 1, DEC, DH), (1, 1, SEQ, DI), (1, 1, DEC, DI), (1, 1, 1, D), (1, 1, 1, D),
         (1, 1, D // N, N, N), (1, 1, D // N, N, N)]


def kernel(**inputs):
    import concourse.bacc as bacc
    from concourse.bass_utils import run_bass_kernel_spmd

    nc = bacc.Bacc("TRN2", target_bir_lowering=False, num_devices=1)
    constants, order = shape_constants()
    arrays, views = {}, {}
    for name in _INS:
        arrays[f"in_{name}"] = np.ascontiguousarray(inputs[name])
    arrays["in_shape_constants"] = constants
    for key, a in arrays.items():
        views[key[3:]] = nc.dram_tensor(key, a.shape, mybir.dt.from_np(a.dtype), kind="ExternalInput").ap()
    outs = [nc.dram_tensor(f"out_{i}", shape, F32, kind="ExternalOutput").ap() for i, shape in enumerate(_OUTS)]
    build(nc, views, outs, order)
    r = run_bass_kernel_spmd(nc, [arrays], core_ids=[0])
    return tuple(r.results[0][f"out_{i}"] for i in range(len(_OUTS)))
```

```python
import concourse.bass as bass
from concourse import mybir
import numpy as np

F32, F32R = mybir.dt.float32, mybir.dt.float32r
ALU, ACT, AX = mybir.AluOpType, mybir.ActivationFunctionType, mybir.AxisListType

P = 128
D = 1024
C = D // P
SEQ, DEC = 256, 32
T = SEQ + DEC
PAST = 512
DEPTH = 4
FF = 4 * D
KT = 4
CW = 512
RAWS, SPLITS = 4, 2
EPS = 1e-6
WINDOWS = (2, 4, 8, 16)
HIST = 15
HEADS, DH = 8, 128
IHEADS, DI = 8, 64
CHUNK = 64
TOPK_P = SEQ // 4
TOPK_S = (PAST + DEC) // 4
LS = PAST + DEC
NEG = -1e30
TAKEN = -3e30
ATTN_IN = 1864
OFF_K, OFF_WI = 1024, 1856
THETA = 500000.0
N = 64
CH = 32
NCH = T // CH
TT = 96
NT = T // TT
LNX_EPS = 64e-5
TOK_TILES = ((0, 128), (128, 128), (256, 32))

VEC_SOURCES = (("ln1_g", 4), ("ln2_g", 4), ("ln_f_g", 1), ("pool_scale", 2), ("rwkv_mix", 6), ("rwkv_w0", 1),
               ("rwkv_a0", 1), ("rwkv_k_k", 1), ("rwkv_k_a", 1), ("rwkv_r_k", 1), ("rwkv_lnx_g", 1),
               ("rwkv_lnx_b", 1))
VEC = {}
_n = 0
for _name, _rows in VEC_SOURCES:
    VEC[_name] = _n
    _n += _rows
NVEC = _n


STAGES = ("input", "pool0", "mlp0", "attn", "mlp1", "rwkv", "mlp2", "pool1", "mlp3", "output")


def shape_constants():
    pos = np.concatenate([np.arange(SEQ), PAST + np.arange(DEC)]).astype(np.float32)
    parts = {}
    parts["ident"] = np.eye(P)
    parts["ones"] = np.ones((P, P))
    head_of = np.arange(P) // N
    parts["head_ones"] = (head_of[:, None] == head_of[None, :]) * 1.0

    def rope(dim, block):
        half = dim // 4 // 2
        inv = np.float32(THETA) ** (-np.arange(half, dtype=np.float32) / np.float32(half))
        ang = (pos[:, None] * inv[None, :].astype(np.float32)).astype(np.float32)
        cos, sin = np.ones((P, T)), np.zeros((P, T))
        swap = np.zeros((P, P))
        for b in range(0, P, block):
            cos[b:b + half] = cos[b + half:b + 2 * half] = np.cos(ang).T
            sin[b:b + half] = sin[b + half:b + 2 * half] = np.sin(ang).T
            for i in range(half):
                swap[b + i, b + half + i] = -1.0
                swap[b + half + i, b + i] = 1.0
        return cos, sin, swap.T

    parts["cos_q"], parts["sin_q"], parts["swap_q"] = rope(DH, DH)
    parts["cos_i"], parts["sin_i"], parts["swap_i"] = rope(DI, DI)
    count = np.arange(HIST) + 1.0
    parts["inv_count"] = np.broadcast_to(1.0 / count, (P, HIST))
    parts["scan_keep"] = np.broadcast_to((np.arange(T) % CH != 0) * 1.0, (P, T))
    i, j = np.arange(P)[:, None], np.arange(TT)[None, :]
    same = (i // CH == j // CH)
    parts["row_after_col"] = (same & (j < i)) * 1.0
    parts["col_after_row"] = (same & (i < j)) * 1.0
    parts["col_after_row_2"] = parts["col_after_row"]
    parts["col_from_row"] = (same & (i <= j)) * 1.0
    to_head = np.arange(D // N)[None, :, None] == 2 * np.arange(C)[:, None, None] + head_of[None, None, :]
    parts["to_head"] = to_head.transpose(2, 0, 1).reshape(P, D // N * C) * 1.0
    parts["from_head"] = np.zeros((P, D))
    parts["from_head"][0:D // N] = to_head.transpose(1, 0, 2).reshape(D // N, D)
    rep = np.zeros((P, P))
    for g in range(4):
        rep[:DEC, g * DEC:(g + 1) * DEC] = np.eye(DEC)
    parts["repeat4"] = rep
    order, at = {}, 0
    for k, v in parts.items():
        order[k] = (at, v.shape[1])
        at += v.shape[1]
    return np.concatenate([v for v in parts.values()], axis=1).astype(np.float32), order


class Signal:

    def __init__(self, nc, name):
        self.sem, self.base = nc.alloc_semaphore(name), 0

    def at(self, k):
        return self.base + k

    def close(self, total):
        self.base += total


class Own:

    def __init__(self, nc, name):
        self.sem, self.n = nc.alloc_semaphore(name), 0

    def step(self, eng, ins):
        self.n += 1
        ins.then_inc(self.sem, 1)
        eng.wait_ge(self.sem, self.n)


def build(nc, A, O, const_order):
    UNIT = C * T * 4
    base0 = (nc.sbuf_base + 63) // 64 * 64
    small = base0 + UNIT
    raw_at = small + 5120
    hi_at = raw_at + RAWS * KT * CW * 4
    lo_at = hi_at + SPLITS * KT * CW * 4
    work = lo_at + SPLITS * KT * CW * 4

    def at(name, offset, shape, dt=F32):
        return nc.alloc_sbuf_tensor_at(name, shape, dt, offset=offset)

    def unit(k):
        return work + k * UNIT

    class Area:
        def __init__(self, start):
            self.next = start

        def take(self, name, shape, dt=F32):
            size = int(np.prod(shape[1:])) * 4
            t = at(name, self.next, shape, dt)
            self.next += (size + 31) // 32 * 32
            return t

    X = at("X", base0, [P, C, T])
    sm = Area(small)
    vecs = sm.take("vecs", [P, NVEC * C])
    fixed = sm.take("fixed", [P, 3 * P])
    var = sm.take("var", [P, T])
    rstd = sm.take("rstd", [P, T])
    ident, ones, head_ones = (fixed[:, k * P:(k + 1) * P] for k in range(3))
    raw = at("raw", raw_at, [P, RAWS, KT, CW])
    w_hi = at("w_hi", hi_at, [P, SPLITS, KT, CW], F32R)
    w_lo = at("w_lo", lo_at, [P, SPLITS, KT, CW], F32R)
    x_hi = at("x_hi", unit(0), [P, C, T], F32R)
    x_lo = at("x_lo", unit(1), [P, C, T], F32R)
    m_hi = at("mlp_x_hi", unit(11), [P, C, T], F32R)
    m_lo = at("mlp_x_lo", unit(12), [P, C, T], F32R)
    squares = at("squares", unit(13), [P, C, T])
    PS = nc.alloc_psum_tensor("PS", [P, 8, 512], F32)

    def vec(name, row, c):
        k = (VEC[name] + row) * C + c
        return vecs[:, k:k + 1]

    consts = A["shape_constants"]

    def const_dram(name, rows=P):
        o, w = const_order[name]
        return consts[0:rows, o:o + w]

    raw_loaded = [nc.alloc_semaphore(f"raw_loaded{s}") for s in range(RAWS)]
    hi_made = nc.alloc_semaphore("hi_made")
    lo_made = nc.alloc_semaphore("lo_made")
    chunk_used = nc.alloc_semaphore("chunk_used")
    S = {n: Signal(nc, n) for n in (
        "squares", "sum_ready", "var_ready", "rstd_ready", "h_ready", "xhi_ready", "xlo_ready",
        "group_out", "relu_ready", "ff_hi", "stage_load", "stage_pe", "stage_act", "stage_dve",
        "stage_pool", "store", "pe2", "act2", "dve2", "load2",
        "max_ready", "exp_ready", "prob_ready", "turned", "turned_out", "value_ready", "value_out", "taken",
        "repeated", "residual", "added", "pre_hi", "pre_lo", "lerp_ready", "in_hi",
        "in_lo", "y_copied", "mean_ready", "centred", "centred_sq", "spread_ready", "spread_inv", "root_ready",
        "mixed_ready", "inner_done", "inner_out", "lora_done", "lora_out", "proj_out")}
    dve_own, act_own, pool_own = Own(nc, "dve_own"), Own(nc, "act_own"), Own(nc, "pool_own")

    def rows4(w, r0, c0, width=CW):
        return w[r0:r0 + KT * P, c0:c0 + width].rearrange("(k p) n -> p k n", p=P)

    chunks = []
    first_chunk = {}

    def plan_matrix(key, w, cols):
        first_chunk.setdefault(key, len(chunks))
        for c0 in range(0, cols, CW):
            width = min(CW, cols - c0)
            for r0 in range(0, D, KT * P):
                chunks.append((rows4(w, r0, c0, width), width))

    def plan_mlp(i):
        first_chunk[f"mlp{i}"] = len(chunks)
        for g in range(FF // CW):
            for half in range(2):
                chunks.append((rows4(A["w_up"][i], half * KT * P, g * CW), CW))
        for g in range(D // CW):
            for q in range(FF // (KT * P)):
                chunks.append((rows4(A["w_down"][i], q * KT * P, g * CW), CW))

    for stage in STAGES:
        if stage.startswith("mlp"):
            plan_mlp(int(stage[3:]))
        if stage == "attn":
            plan_matrix("attn_in", A["attn_w_in"][0], OFF_WI)
            plan_matrix("attn_out", A["attn_w_out"][0], D)
        if stage == "rwkv":
            for key in ("rwkv_w_r", "rwkv_w_k", "rwkv_w_v", "rwkv_w_o"):
                plan_matrix(key, A[key][0], D)
    first_chunk["end"] = len(chunks)

    def load_chunk(sp, n):
        src, width = chunks[n]
        if n >= RAWS:
            sp.wait_ge(lo_made, n - RAWS + 1)
        sp.dma_start(raw[:, n % RAWS, :, 0:width], src).then_inc(raw_loaded[n % RAWS], 16)

    def first_loads(sp):
        for n in range(min(RAWS, len(chunks))):
            load_chunk(sp, n)

    def load_ahead(sp, start, end):
        for n in range(start + RAWS, min(end + RAWS, len(chunks))):
            load_chunk(sp, n)

    split_early = {"hi": set(), "lo": set()}

    def make_hi(act, n, repeat=0, early=False):
        if n in split_early["hi"] or n >= len(chunks):
            return
        if early:
            split_early["hi"].add(n)
        width = chunks[n][1]
        act.wait_ge(raw_loaded[n % RAWS], 16 * (n // RAWS + 1))
        if n >= SPLITS:
            act.wait_ge(chunk_used, n - SPLITS + 1)
        if repeat:
            nc.scalar.activation(w_hi[:, n % SPLITS, :, width:width + repeat],
                                 raw[:, n % RAWS, :, width - repeat:width], ACT.Copy)
        nc.scalar.activation(w_hi[:, n % SPLITS, :, 0:width], raw[:, n % RAWS, :, 0:width], ACT.Copy) \
            .then_inc(hi_made, 1)

    def make_lo(dve, n, repeat=0, early=False):
        if n in split_early["lo"] or n >= len(chunks):
            return
        if early:
            split_early["lo"].add(n)
        width = chunks[n][1]
        dve.wait_ge(hi_made, n + 1)
        if repeat:
            nc.vector.tensor_tensor(w_lo[:, n % SPLITS, :, width:width + repeat],
                                    raw[:, n % RAWS, :, width - repeat:width],
                                    w_hi[:, n % SPLITS, :, width:width + repeat].bitcast(F32), ALU.subtract)
        nc.vector.tensor_tensor(w_lo[:, n % SPLITS, :, 0:width], raw[:, n % RAWS, :, 0:width],
                                w_hi[:, n % SPLITS, :, 0:width].bitcast(F32), ALU.subtract).then_inc(lo_made, 1)

    def use_chunk(slot, rhs_hi, rhs_lo, bank, first, last, width=CW, midway=None):
        for m in range((width + P - 1) // P):
            w = min(P, width - m * P)
            if midway and m == 2:
                midway()
            out = PS[0:w, bank + m, 0:T] if isinstance(bank, int) else PS[0:w, bass.ds(bank + m, 1), 0:T]
            for k in range(KT):
                hi = w_hi[:, slot, k, m * P:m * P + w]
                lo = w_lo[:, slot, k, m * P:m * P + w]
                nc.tensor.matmul(out, hi, rhs_hi(k), start=first and k == 0, stop=False)
                nc.tensor.matmul(out, lo, rhs_hi(k), start=False, stop=False)
                mm = nc.tensor.matmul(out, hi, rhs_lo(k), start=False, stop=last and k == KT - 1)
        return mm

    def project(pe, a, g0, widths, hi=None, lo=None, split=None):
        hi, lo = hi or x_hi, lo or x_lo
        for g, width in enumerate(widths, g0):
            for half in range(2):
                n = a + 2 * g + half
                pe.wait_ge(lo_made, n + 1)
                if split and g == g0:
                    pe.wait_ge(split.sem, split.at(half + 1))
                use_chunk(n % 2, lambda k: hi[:, half * KT + k, :], lambda k: lo[:, half * KT + k, :],
                          4 * (g % 2), half == 0, half == 1, width).then_inc(chunk_used, 1)

    def norm_act(act, sq, meanwhile=None):
        for c in range(C):
            nc.scalar.activation(sq[:, c, :], X[:, c, :], ACT.Square).then_inc(S["squares"].sem, 1)
        if meanwhile:
            meanwhile()
        act.wait_ge(S["var_ready"].sem, S["var_ready"].at(1))
        nc.scalar.activation(rstd[:, :], var[:, :], ACT.Sqrt).then_inc(S["rstd_ready"].sem, 1)

    def norm_pe(pe, sq, bank=7):
        for c in range(C):
            pe.wait_ge(S["squares"].sem, S["squares"].at(c + 1))
            mm = nc.tensor.matmul(PS[:, bank, 0:T], ones, sq[:, c, :], start=c == 0, stop=c == C - 1)
        mm.then_inc(S["sum_ready"].sem, 1)

    def norm_dve(dve, gain, row, outs, bank=7):
        dve.wait_ge(S["sum_ready"].sem, S["sum_ready"].at(1))
        dve_own.step(dve, nc.vector.tensor_scalar(var[:, :], PS[:, bank, 0:T], 1.0 / D, EPS, ALU.mult, ALU.add))
        nc.vector.reciprocal(var[:, :], var[:, :]).then_inc(S["var_ready"].sem, 1)
        dve.wait_ge(S["rstd_ready"].sem, S["rstd_ready"].at(1))
        for c in range(C):
            for dst, (t0, t1) in outs(c):
                ins = nc.vector.scalar_tensor_tensor(dst, X[:, c, t0:t1], vec(gain, row, c), rstd[:, t0:t1],
                                                     ALU.mult, ALU.mult)
                last = ins
                if (t0, t1) != outs(c)[-1][1]:
                    ins.then_inc(dve_own.sem, 1)
                    dve_own.n += 1
            last.then_inc(S["h_ready"].sem, 1)

    def norm_close():
        for name, n in (("squares", C), ("sum_ready", 1), ("var_ready", 1), ("rstd_ready", 1), ("h_ready", C)):
            S[name].close(n)

    SPLIT = {f"mlp{i}": ("ln2_g", i, m_hi, m_lo) for i in range(DEPTH)}
    SPLIT["attn"] = ("ln1_g", 1, x_hi, x_lo)
    after = dict(zip(STAGES, STAGES[1:]))
    half_split = {b: (a.startswith("mlp") or a in ("attn", "rwkv")) and b in SPLIT for a, b in after.items()}
    HALF = C // 2

    def split_hi(act, stage, tiles, sig):
        gain, row, hi, lo = SPLIT[stage]
        for c in tiles:
            nc.scalar.activation(hi[:, c, :], X[:, c, :], ACT.Copy, scale=vec(gain, row, c)).then_inc(sig.sem, 1)

    def split_lo(dve, stage, tiles, hi_sig, lo_sig):
        gain, row, hi, lo = SPLIT[stage]
        for i, c in enumerate(tiles):
            dve.wait_ge(hi_sig.sem, hi_sig.at(i + 1))
            nc.vector.scalar_tensor_tensor(lo[:, c, :], X[:, c, :], vec(gain, row, c), hi[:, c, :].bitcast(F32),
                                           ALU.mult, ALU.subtract).then_inc(lo_sig.sem, 1)

    def square_tiles(act, tiles, sig=None):
        for c in tiles:
            ins = nc.scalar.activation(squares[:, c, :], X[:, c, :], ACT.Square)
            if sig:
                ins.then_inc(sig.sem, 1)

    def start_act(act, stage, a):
        split_hi(act, stage, range(HALF if half_split[stage] else 0, C), S["xhi_ready"])
        make_hi(act, a)
        make_hi(act, a + 1)
        square_tiles(act, range(HALF if half_split[stage] else 0, C), S["squares"])
        make_hi(act, a + 2, early=True)
        act.wait_ge(S["var_ready"].sem, S["var_ready"].at(1))
        nc.scalar.activation(rstd[:, :], var[:, :], ACT.Sqrt).then_inc(S["rstd_ready"].sem, 1)

    def start_pool(pool, stage):
        def add(dst, src):
            pool_own.step(pool, nc.gpsimd.tensor_tensor(squares[:, dst, :], squares[:, dst, :], squares[:, src, :],
                                                        ALU.add))

        for half in range(2):
            if not half_split[stage]:
                pool.wait_ge(S["squares"].sem, S["squares"].at(HALF * (half + 1)))
            elif half:
                pool.wait_ge(S["squares"].sem, S["squares"].at(HALF))
            f = HALF * half
            add(slice(f, f + 2), slice(f + 2, f + 4))
            add(slice(f, f + 1), slice(f + 1, f + 2))
        nc.gpsimd.tensor_tensor(squares[:, 0, :], squares[:, 0, :], squares[:, HALF, :], ALU.add) \
            .then_inc(S["added"].sem, 1)

    def start_dve(dve, stage, a):
        split_lo(dve, stage, range(HALF if half_split[stage] else 0, C), S["xhi_ready"], S["xlo_ready"])
        make_lo(dve, a)
        make_lo(dve, a + 1)
        make_lo(dve, a + 2, early=True)
        dve.wait_ge(S["sum_ready"].sem, S["sum_ready"].at(1))
        dve_own.step(dve, nc.vector.tensor_scalar(var[:, :], PS[:, 7, 0:T], 1.0 / D, EPS, ALU.mult, ALU.add))
        nc.vector.reciprocal(var[:, :], var[:, :]).then_inc(S["var_ready"].sem, 1)
        dve.wait_ge(S["rstd_ready"].sem, S["rstd_ready"].at(1))

    def start_pe(pe, stage, a):
        gain, row, hi, lo = SPLIT[stage]

        def sum_of_squares():
            pe.wait_ge(S["added"].sem, S["added"].at(1))
            nc.tensor.matmul(PS[:, 7, 0:T], ones, squares[:, 0, :], start=True, stop=True) \
                .then_inc(S["sum_ready"].sem, 1)

        for half in range(2):
            first_left = HALF if half_split[stage] else 0
            pe.wait_ge(lo_made, a + half + 1)
            if half * KT + KT > first_left:
                pe.wait_ge(S["xlo_ready"].sem, S["xlo_ready"].at(half * KT + KT - first_left))
            use_chunk((a + half) % 2, lambda k: hi[:, half * KT + k, :], lambda k: lo[:, half * KT + k, :],
                      0, half == 0, half == 1, midway=sum_of_squares if half else None).then_inc(chunk_used, 1)
        pe.wait_ge(S["var_ready"].sem, S["var_ready"].at(1))

    def start_close(stage):
        left = C - (HALF if half_split[stage] else 0)
        for name, n in (("squares", left), ("added", 1), ("sum_ready", 1), ("var_ready", 1), ("rstd_ready", 1),
                        ("xhi_ready", left), ("xlo_ready", left)):
            S[name].close(n)

    def finish_act(act, stage, end):
        if half_split.get(after[stage]):
            act.wait_ge(S["residual"].sem, S["residual"].at(1))
            split_hi(act, after[stage], range(HALF), S["pre_hi"])
            square_tiles(act, range(HALF))
        make_hi(act, end, early=True)

    def finish_dve(dve, stage, end, half_used):
        def add(g, used):
            dve.wait_ge(chunk_used, used)
            nc.vector.tensor_tensor(X[:, 4 * g:4 * g + 4, :], X[:, 4 * g:4 * g + 4, :], PS[:, 4 * g:4 * g + 4, 0:T],
                                    ALU.add).then_inc(S["residual"].sem, 1)

        add(0, half_used)
        if half_split.get(after[stage]):
            split_lo(dve, after[stage], range(HALF), S["pre_hi"], S["pre_lo"])
        make_lo(dve, end, early=True)
        add(1, end)

    def finish_close(stage):
        S["residual"].close(2)
        if half_split.get(after[stage]):
            S["pre_hi"].close(HALF)
            S["pre_lo"].close(HALF)

    def stage_input():
        x_tok = at("x_tok", unit(2), [P, 3, D])
        rows = at("vec_rows", unit(4), [P, 2, P])
        load, pe_s, dve_s = S["stage_load"], S["stage_pe"], S["stage_dve"]
        with nc.Block() as block:
            @block.sync
            def _(sp):
                sp.dma_start(fixed[:, :], consts[:, 0:3 * P]).then_inc(load.sem, 16)
                sp.dma_start(x_tok[:, 0:2, :], A["x_prompt"][0].rearrange("(t p) d -> p t d", p=P)) \
                    .then_inc(load.sem, 16)
                sp.dma_start(x_tok[0:DEC, 2, :], A["x_sample"][0]).then_inc(load.sem, 16)
                if not after["input"].startswith("pool"):
                    first_loads(sp)

            @block.scalar
            def _(act):
                for name, count in VEC_SOURCES:
                    src = A[name]
                    src = src.rearrange("a h n -> a (h n)") if name == "rwkv_r_k" else src
                    src = src.rearrange("(a d) -> a d", a=1) if name == "ln_f_g" else src
                    src = src[0] if name == "rwkv_mix" else src
                    src = src.rearrange("a (c p) -> (a c) p", p=P)
                    r0, n = VEC[name] * C, count * C
                    while n:
                        here = min(n, P - r0 % P)
                        act.dma_start(rows[r0 % P:r0 % P + here, r0 // P, :], src[0:here, :]) \
                            .then_inc(S["load2"].sem, 16)
                        src = src[here:, :] if n > here else src
                        r0, n = r0 + here, n - here

            @block.tensor
            def _(pe):
                pe.wait_ge(load.sem, load.at(48))
                for c in range(C):
                    for t, (t0, n) in enumerate(TOK_TILES):
                        mm = nc.tensor.transpose(PS[:, c, t0:t0 + n], x_tok[0:n, t, c * P:(c + 1) * P],
                                                 ident[0:n, 0:n])
                    mm.then_inc(pe_s.sem, 1)
                pe.wait_ge(S["load2"].sem, S["load2"].at(16 * (len(VEC_SOURCES) + 1)))
                pe.wait_ge(dve_s.sem, dve_s.at(1))
                nc.tensor.transpose(PS[:, 0, 0:P], rows[:, 0, :], ident)
                rest = NVEC * C - P
                nc.tensor.transpose(PS[:, 0, P:P + rest], rows[0:rest, 1, :], ident[0:rest, 0:rest]) \
                    .then_inc(pe_s.sem, 1)

            @block.vector
            def _(dve):
                for c in range(C):
                    dve.wait_ge(pe_s.sem, pe_s.at(c + 1))
                    nc.vector.tensor_copy(X[:, c, :], PS[:, c, 0:T]).then_inc(dve_s.sem, 1)
                dve.wait_ge(pe_s.sem, pe_s.at(C + 1))
                nc.vector.tensor_copy(vecs[:, :], PS[:, 0, 0:NVEC * C]).then_inc(dve_s.sem, 1)
        load.close(48)
        S["load2"].close(16 * (len(VEC_SOURCES) + 1))
        pe_s.close(C + 1)
        dve_s.close(C + 1)

    def stage_mlp(i):
        a = first_chunk[f"mlp{i}"]
        GROUPS = FF // CW
        f_hi = at(f"ff_hi{i}", unit(2), [P, FF // P, T], F32R)
        f_lo = at(f"ff_lo{i}", unit(6), [P, FF // P, T], F32R)
        relu = at(f"relu{i}", unit(10), [P, 4, T])
        squared = at(f"squared{i}", unit(10) + UNIT // 2, [P, 4, T])
        out, relu_s, ffhi_s, fflo_s = (S[k] for k in ("group_out", "relu_ready", "ff_hi", "dve2"))
        up_dram = A["w_up"][i]
        stage = f"mlp{i}"
        rms4 = rstd[:, :].rearrange("p (a t) -> p a t", a=1).to_broadcast([P, 4, T])

        with nc.Block() as block:
            @block.sync
            def _(sp):
                with sp.Fori(0, GROUPS // 2 - 1) as it:
                    for j in range(4):
                        half, dg = j % 2, 2 + j // 2
                        src = up_dram[half * KT * P:(half + 1) * KT * P, bass.ds((2 * it + dg) * CW, CW)] \
                            .rearrange("(k p) n -> p k n", p=P)
                        sp.wait_ge(lo_made, a + 1 + j + 4 * it)
                        sp.dma_start(raw[:, j, :, :], src).then_inc(raw_loaded[j], 16)
                load_ahead(sp, a + 2 * GROUPS - RAWS, a + 4 * GROUPS)

            @block.scalar
            def _(act):
                start_act(act, stage, a)

                def hi(it, j):
                    act.wait_ge(raw_loaded[j], 16 * (a // RAWS + 1) + 16 * it)
                    if not isinstance(it, int) or a + j + 4 * it >= SPLITS:
                        act.wait_ge(chunk_used, a + j - SPLITS + 1 + 4 * it)
                    nc.scalar.activation(w_hi[:, j % 2, :, :], raw[:, j, :, :], ACT.Copy).then_inc(hi_made, 1)

                def evict(g):
                    act.wait_ge(relu_s.sem, relu_s.at(1) + g)
                    nc.scalar.activation(f_hi[:, bass.ds(4 * g, 4), :], relu[:, :, :], ACT.Square) \
                        .then_inc(ffhi_s.sem, 1)

                hi(0, 3)
                evict(0)
                with act.Fori(1, GROUPS // 2) as it:
                    hi(it, 0)
                    hi(it, 1)
                    evict(2 * it - 1)
                    hi(it, 2)
                    hi(it, 3)
                    evict(2 * it)
                down = a + 2 * GROUPS
                make_hi(act, down)
                make_hi(act, down + 1)
                evict(GROUPS - 1)
                for n in range(down + 2, down + 2 * GROUPS):
                    make_hi(act, n)
                finish_act(act, stage, down + 2 * GROUPS)

            @block.gpsimd
            def _(pool):
                start_pool(pool, stage)

            @block.vector
            def _(dve):
                start_dve(dve, stage, a)

                def lo(it, j):
                    dve.wait_ge(hi_made, a + j + 1 + 4 * it)
                    nc.vector.tensor_tensor(w_lo[:, j % 2, :, :], raw[:, j, :, :], w_hi[:, j % 2, :, :].bitcast(F32),
                                            ALU.subtract).then_inc(lo_made, 1)

                def evict(g, half):
                    dve.wait_ge(chunk_used, a + 2 + 2 * g)
                    if not isinstance(g, int) or g >= 1:
                        dve.wait_ge(ffhi_s.sem, ffhi_s.at(0) + g)
                    nc.vector.scalar_tensor_tensor(relu[:, :, :], PS[:, 4 * half:4 * half + 4, 0:T], 0.0, rms4,
                                                   ALU.max, ALU.mult).then_inc(relu_s.sem, 1)
                    dve.wait_ge(relu_s.sem, relu_s.at(1) + g)
                    nc.vector.tensor_tensor(squared[:, :, :], relu[:, :, :], relu[:, :, :], ALU.mult) \
                        .then_inc(out.sem, 1)
                    dve.wait_ge(out.sem, out.at(1) + g)
                    dve.wait_ge(ffhi_s.sem, ffhi_s.at(1) + g)
                    nc.vector.tensor_tensor(f_lo[:, bass.ds(4 * g, 4), :], squared[:, :, :],
                                            f_hi[:, bass.ds(4 * g, 4), :].bitcast(F32), ALU.subtract) \
                        .then_inc(fflo_s.sem, 1)

                evict(0, 0)
                lo(0, 3)
                with dve.Fori(1, GROUPS // 2) as it:
                    lo(it, 0)
                    lo(it, 1)
                    evict(2 * it - 1, 1)
                    lo(it, 2)
                    lo(it, 3)
                    evict(2 * it, 0)
                down = a + 2 * GROUPS
                make_lo(dve, down)
                make_lo(dve, down + 1)
                evict(GROUPS - 1, 1)
                for n in range(down + 2, down + 2 * GROUPS):
                    make_lo(dve, n)
                finish_dve(dve, stage, down + 2 * GROUPS, down + GROUPS)

            @block.tensor
            def _(pe):
                start_pe(pe, stage, a)

                def up_group(it, half, peeled):
                    for kh in range(2):
                        j = 2 * half + kh
                        pe.wait_ge(lo_made, a + j + 1 + 4 * it)
                        if kh == 0 and not peeled:
                            pe.wait_ge(relu_s.sem, relu_s.at(half - 1) + 2 * it)
                        mm = use_chunk(j % 2, lambda k: m_hi[:, kh * KT + k, :], lambda k: m_lo[:, kh * KT + k, :],
                                       4 * half, kh == 0, kh == 1)
                        mm.then_inc(chunk_used, 1)

                up_group(0, 1, True)
                with pe.Fori(1, GROUPS // 2) as it:
                    up_group(it, 0, False)
                    up_group(it, 1, False)
                down = a + 2 * GROUPS
                for g in range(2):
                    pe.wait_ge(relu_s.sem, relu_s.at(GROUPS - 1 + g))
                    for q in range(GROUPS):
                        n = down + g * GROUPS + q
                        pe.wait_ge(lo_made, n + 1)
                        if g == 0:
                            pe.wait_ge(fflo_s.sem, fflo_s.at(q + 1))
                        mm = use_chunk(n % 2, lambda k: f_hi[:, 4 * q + k, :], lambda k: f_lo[:, 4 * q + k, :],
                                       4 * g, q == 0, q == GROUPS - 1)
                        mm.then_inc(chunk_used, 1)
        start_close(stage)
        finish_close(stage)
        out.close(GROUPS)
        relu_s.close(GROUPS)
        ffhi_s.close(GROUPS)
        fflo_s.close(GROUPS)

    def project_residual(stage, key, src=None, halves=None):
        a = first_chunk[key]
        act_s, dve_s = S["act2"], S["dve2"]
        with nc.Block() as block:
            @block.sync
            def _(sp):
                load_ahead(sp, a, a + 4)

            @block.scalar
            def _(act):
                for k in () if halves else (0, KT):
                    nc.scalar.activation(x_hi[:, k:k + KT, :], src[:, k:k + KT, :], ACT.Copy).then_inc(act_s.sem, 1)
                for n in range(a, a + 4):
                    make_hi(act, n)
                finish_act(act, stage, a + 4)

            @block.vector
            def _(dve):
                for half, k in enumerate(() if halves else (0, KT)):
                    dve.wait_ge(act_s.sem, act_s.at(half + 1))
                    nc.vector.tensor_tensor(x_lo[:, k:k + KT, :], src[:, k:k + KT, :],
                                            x_hi[:, k:k + KT, :].bitcast(F32), ALU.subtract).then_inc(dve_s.sem, 1)
                for n in range(a, a + 4):
                    make_lo(dve, n)
                finish_dve(dve, stage, a + 4, a + 2)

            @block.tensor
            def _(pe):
                if halves:
                    project(pe, a, 0, [CW, CW], *halves)
                else:
                    project(pe, a, 0, [CW, CW], split=dve_s)
        if not halves:
            act_s.close(2)
            dve_s.close(2)
        finish_close(stage)

    def stage_output():
        h = at("out_h", unit(2), [P, C, T])
        sq = at("out_sq", unit(4), [P, C, T])
        tok = at("out_tok", unit(6), [P, 3, D])
        rms = at("out_inv_rms", unit(8), [P, 3, 8])
        dsts = (O[0][0, 0:P, :], O[0][0, P:SEQ, :], O[1][0])
        squares_s, sum_s, inv_s, root_s, h_s, turned, tok_act, tok_dve, store = (S[n] for n in (
            "squares", "sum_ready", "var_ready", "rstd_ready", "h_ready", "turned", "act2", "dve2", "store"))
        parts = ((0, 2, P), (2, 3, DEC))

        def rows_of(t, n):
            return (tok[0:n, t, :].rearrange("p (b n) -> p b n", b=2), PS[0:n, 2 * t:2 * t + 2, :])

        with nc.Block() as block:
            @block.scalar
            def _(act):
                for c in range(C):
                    nc.scalar.activation(sq[:, c, :], X[:, c, :], ACT.Square).then_inc(squares_s.sem, 1)
                act.wait_ge(inv_s.sem, inv_s.at(2))
                for t0, t1, n in parts:
                    nc.scalar.activation(rms[0:n, t0:t1, :], rms[0:n, t0:t1, :], ACT.Sqrt).then_inc(root_s.sem, 1)
                act.wait_ge(root_s.sem, root_s.at(2))
                for t, (t0, n) in enumerate(TOK_TILES):
                    if t != 1:
                        act.wait_ge(turned.sem, turned.at(t + 1))
                        dst, src = rows_of(t, n)
                        nc.scalar.activation(dst, src, ACT.Copy, scale=rms[0:n, t, 0:1]).then_inc(tok_act.sem, 1)

            @block.tensor
            def _(pe):
                for t, (t0, n) in enumerate(TOK_TILES):
                    for c in range(C):
                        pe.wait_ge(squares_s.sem, squares_s.at(c + 1))
                        mm = nc.tensor.matmul(PS[0:n, 6, t * 8:t * 8 + 8], sq[:, c, t0:t0 + n], ones[:, 0:8],
                                              start=c == 0, stop=c == C - 1)
                mm.then_inc(sum_s.sem, 1)
                pe.wait_ge(h_s.sem, h_s.at(C))
                for t, (t0, n) in enumerate(TOK_TILES):
                    for c in range(C):
                        mm = nc.tensor.transpose(PS[0:n, 2 * t + c // 4, (c % 4) * P:(c % 4 + 1) * P],
                                                 h[:, c, t0:t0 + n], ident)
                    mm.then_inc(turned.sem, 1)

            @block.vector
            def _(dve):
                for c in range(C):
                    nc.vector.tensor_scalar(h[:, c, :], X[:, c, :], vec("ln_f_g", 0, c), None, ALU.mult) \
                        .then_inc(h_s.sem, 1)
                dve.wait_ge(sum_s.sem, sum_s.at(1))
                for t0, t1, n in parts:
                    dve_own.step(dve, nc.vector.tensor_scalar(
                        rms[0:n, t0:t1, :], PS[0:n, 6, 8 * t0:8 * t1].rearrange("p (t k) -> p t k", k=8),
                        1.0 / D, EPS, ALU.mult, ALU.add))
                    nc.vector.reciprocal(rms[0:n, t0:t1, :], rms[0:n, t0:t1, :]).then_inc(inv_s.sem, 1)
                dve.wait_ge(root_s.sem, root_s.at(1))
                dve.wait_ge(turned.sem, turned.at(2))
                dst, src = rows_of(1, P)
                nc.vector.tensor_scalar(dst, src, rms[:, 1, 0:1], None, ALU.mult).then_inc(tok_dve.sem, 1)

            @block.sync
            def _(sp):
                for t, sig, count in ((0, tok_act, 1), (1, tok_dve, 1), (2, tok_act, 2)):
                    n = TOK_TILES[t][1]
                    sp.wait_ge(sig.sem, sig.at(count))
                    sp.dma_start(dsts[t], tok[0:n, t, :]).then_inc(store.sem, 16)
                sp.wait_ge(store.sem, store.at(48))

    def stage_pool(j):
        layer = 3 * j
        G = HIST + SEQ + HIST + DEC
        P0, S0 = HIST, HIST + SEQ + HIST
        area = Area(unit(2))
        h = area.take(f"pool_h{j}", [P, C, G])
        even = area.take(f"pool_even{j}", [P, C, G])
        odd = area.take(f"pool_odd{j}", [P, C, G])
        pooled = area.take(f"pooled{j}", [P, C, T])
        inv_count = area.take(f"inv_count{j}", [P, 1, HIST])
        pw = area.take(f"pool_w_raw{j}", [P, C, 256])
        pw_hi = area.take(f"pool_w_hi{j}", [P, C, 256], F32R)
        pw_lo = area.take(f"pool_w_lo{j}", [P, C, 256], F32R)
        sq = area.take(f"pool_sq{j}", [P, C, T])
        hist = area.take(f"pool_hist{j}", [P, D])
        rows = area.take(f"pool_rows{j}", [P, 2, D])
        load, pe_s, dve_s, act_s, pool_s = (S[k] for k in ("stage_load", "stage_pe", "stage_dve", "stage_act",
                                                           "stage_pool"))
        in_hi, in_lo = S["in_hi"], S["in_lo"]

        with nc.Block() as block:
            @block.sync
            def _(sp):
                sp.dma_start(hist[0:HIST, :], A["state_pool"][j, 0]).then_inc(load.sem, 16)
                sp.dma_start(inv_count[:, :, :].rearrange("p a b -> p (a b)"), const_dram("inv_count")) \
                    .then_inc(load.sem, 16)
                sp.dma_start(pw[:, :, :], A["pool_w"][j].rearrange("g (k p) n -> p (g k) n", p=P)) \
                    .then_inc(load.sem, 16)
                if STAGES[1] == f"pool{j}":
                    first_loads(sp)

            @block.gpsimd
            def _(pool):
                nc.gpsimd.memset(h[:, :, 0:HIST], 0.0).then_inc(pool_s.sem, 1)

            @block.tensor
            def _(pe):
                pe.wait_ge(load.sem, load.at(48))
                for c in range(C):
                    mm = nc.tensor.transpose(PS[:, 0, c * 16:c * 16 + HIST], hist[0:HIST, c * P:(c + 1) * P],
                                             ident[0:HIST, 0:HIST])
                mm.then_inc(pe_s.sem, 1)
                norm_pe(pe, sq)

            @block.scalar
            def _(act):
                def weights():
                    act.wait_ge(load.sem, load.at(48))
                    nc.scalar.activation(pw_hi[:, :, :], pw[:, :, :], ACT.Copy).then_inc(act_s.sem, 1)
                    make_hi(act, first_chunk[f"mlp{layer}"], early=True)

                norm_act(act, sq, meanwhile=weights)

            @block.vector
            def _(dve):
                dve.wait_ge(pe_s.sem, pe_s.at(1))
                nc.vector.tensor_copy(h[:, :, HIST + SEQ:S0],
                                      PS[:, 0, 0:16 * C].rearrange("p (c t) -> p c t", c=C)[:, :, 0:HIST]) \
                    .then_inc(dve_s.sem, 1)
                dve.wait_ge(act_s.sem, act_s.at(1))
                nc.vector.tensor_tensor(pw_lo[:, :, :], pw[:, :, :], pw_hi[:, :, :].bitcast(F32), ALU.subtract) \
                    .then_inc(dve_s.sem, 1)
                make_lo(dve, first_chunk[f"mlp{layer}"], early=True)
                norm_dve(dve, "ln1_g", layer, lambda c: [(h[:, c, P0:P0 + SEQ], (0, SEQ)),
                                                         (h[:, c, S0:G], (SEQ, T))])
        load.close(48)
        pe_s.close(1)
        act_s.close(1)
        dve_s.close(2)
        pool_s.close(1)
        norm_close()

        with nc.Block() as block:
            @block.vector
            def _(dve):
                def lo_of_input(g):
                    f = slice(2 * g, 2 * g + 2)
                    dve.wait_ge(in_hi.sem, in_hi.at(g + 1))
                    nc.vector.tensor_tensor(x_lo[:, f, :], pooled[:, f, :], x_hi[:, f, :].bitcast(F32),
                                            ALU.subtract).then_inc(in_lo.sem, 1)

                cur, step = h, 1
                for g, w in enumerate(WINDOWS):
                    dst, f = (even, odd)[g % 2], slice(2 * g, 2 * g + 2)
                    lo, skip = 2 * g, 2 * step - 1
                    dve_own.step(dve, nc.vector.tensor_tensor(
                        dst[:, lo:C, skip:G], cur[:, lo:C, skip:G], cur[:, lo:C, skip - step:G - step], ALU.add))
                    cur, step = dst, 2 * step
                    few = w - 1
                    dve_own.step(dve, nc.vector.tensor_tensor(
                        pooled[:, f, 0:few], dst[:, f, P0:P0 + few], inv_count[:, :, 0:few].to_broadcast([P, 2, few]),
                        ALU.mult))
                    nc.vector.tensor_tensor(pooled[:, f, 0:few], pooled[:, f, 0:few], h[:, f, P0:P0 + few],
                                            ALU.subtract).then_inc(dve_s.sem, 1)
                    for col, t, n in ((P0 + few, few, SEQ - few), (S0, SEQ, DEC)):
                        nc.vector.scalar_tensor_tensor(pooled[:, f, t:t + n], dst[:, f, col:col + n], 1.0 / w,
                                                       h[:, f, col:col + n], ALU.mult, ALU.subtract) \
                            .then_inc(dve_s.sem, 1)
                    if g:
                        lo_of_input(g - 1)
                lo_of_input(3)
                for c in range(C):
                    dve.wait_ge(pe_s.sem, pe_s.at(c + 1))
                    nc.vector.scalar_tensor_tensor(X[:, c, :], PS[:, c, 0:T], vec("pool_scale", j, c), X[:, c, :],
                                                   ALU.mult, ALU.add)

            @block.scalar
            def _(act):
                for g in range(2):
                    act.wait_ge(S["pe2"].sem, S["pe2"].at(g + 1))
                    nc.scalar.activation(rows[0:HIST, g, :].rearrange("p (b n) -> p b n", b=2),
                                         PS[0:HIST, 2 * g:2 * g + 2, :], ACT.Copy).then_inc(act_s.sem, 1)
                for g in range(4):
                    f = slice(2 * g, 2 * g + 2)
                    act.wait_ge(dve_s.sem, dve_s.at(3 * g + 3))
                    nc.scalar.activation(x_hi[:, f, :], pooled[:, f, :], ACT.Copy).then_inc(in_hi.sem, 1)

            @block.sync
            def _(sp):
                for g in range(2):
                    sp.wait_ge(act_s.sem, act_s.at(g + 1))
                    sp.dma_start(O[2 + g][j, 0], rows[0:HIST, g, :]).then_inc(S["store"].sem, 16)
                sp.wait_ge(S["store"].sem, S["store"].at(32))

            @block.tensor
            def _(pe):
                for g, col in enumerate((P0 + SEQ - HIST, G - HIST)):
                    for c in range(C):
                        mm = nc.tensor.transpose(PS[0:HIST, 2 * g + c // 4, (c % 4) * P:(c % 4 + 1) * P],
                                                 h[:, c, col:col + HIST], ident)
                    mm.then_inc(S["pe2"].sem, 1)
                pe.wait_ge(act_s.sem, act_s.at(2))
                for c in range(C):
                    g, m = c // 2, c % 2
                    pe.wait_ge(in_lo.sem, in_lo.at(g + 1))
                    for k in range(2):
                        hi = pw_hi[:, 2 * g + k, m * P:(m + 1) * P]
                        lo = pw_lo[:, 2 * g + k, m * P:(m + 1) * P]
                        nc.tensor.matmul(PS[:, c, 0:T], hi, x_hi[:, 2 * g + k, :], start=k == 0, stop=False)
                        nc.tensor.matmul(PS[:, c, 0:T], lo, x_hi[:, 2 * g + k, :], start=False, stop=False)
                        mm = nc.tensor.matmul(PS[:, c, 0:T], hi, x_lo[:, 2 * g + k, :], start=False, stop=k == 1)
                    mm.then_inc(pe_s.sem, 1)
        dve_s.close(12)
        in_hi.close(4)
        in_lo.close(4)
        pe_s.close(C)
        S["pe2"].close(2)
        act_s.close(2)
        S["store"].close(32)

    def stage_attn():
        a = first_chunk["attn_in"]
        area = Area(unit(2))
        qk = area.take("qk", [P, HEADS + 1, T])
        vt = area.take("vt", [P, T])
        ix = area.take("ix", [P, 5, T])
        h = area.take("attn_h", [P, C, T])
        rot = area.take("rot", [P, HEADS, T])
        tables = area.take("rope_tables", [P, 4, T])
        swaps = area.take("rope_swaps", [P, 2, P])
        rep4 = area.take("repeat4", [P, P])
        w_wi = area.take("w_wi", [P, C, IHEADS])
        wi = area.take("wi", [P, 3, IHEADS])
        kc = area.take("cache_k_rows", [P, 4, DH])
        vc = area.take("cache_v_rows", [P, 4, DH])
        kic = area.take("cache_ki_rows", [P, 4, 2, DI])
        keys_s = area.take("keys_s", [P, LS])
        ikeys_s = area.take("ikeys_s", [P, LS])
        q_s = area.take("q_s", [P, HEADS, DEC])
        k_tok = area.take("k_tok", [P, 3, DH])
        v_tok = area.take("v_tok", [P, 3, DH])
        ki_tok = area.take("ki_tok", [P, 3, DI])
        tiles = ((0, P, P), (1, P, SEQ), (2, DEC, LS))
        score = [area.take(f"score{q}", [P, L]) for q, nq, L in tiles]
        dots = area.take("dots", [P, 2, LS])
        best = area.take("best", [P, 8])
        prob = [area.take("prob0", [P, HEADS, P]), area.take("prob1", [P, HEADS, SEQ]),
                area.take("prob2", [P, 2, LS])]
        prob_t = [area.take("prob_t0", [P, HEADS, 1, P]), area.take("prob_t1", [P, HEADS, 2, P]),
                  area.take("prob_t2", [P, 2, 5, P])]
        stat = area.take("stat", [P, 3, 3, HEADS])
        o = at("attn_o", unit(2) + 10400 + 1152 + 5760, [P, C, T])
        load, pe_s, dve_s, act_s, pool_s = (S[k] for k in ("stage_load", "stage_pe", "stage_dve", "stage_act",
                                                           "stage_pool"))
        rms1 = rstd[:, :].rearrange("p (a t) -> p a t", a=1)
        WIDTHS = [CW, CW, CW, OFF_WI - 3 * CW + DI]

        with nc.Block() as block:
            @block.sync
            def _(sp):
                def get(dst, src):
                    sp.dma_start(dst, src).then_inc(load.sem, 16)
                get(tables[:, 0, :], const_dram("cos_q"))
                get(tables[:, 1, :], const_dram("sin_q"))
                get(tables[:, 2, :], const_dram("cos_i"))
                get(tables[:, 3, :], const_dram("sin_i"))
                get(swaps[:, 0, :], const_dram("swap_q"))
                get(swaps[:, 1, :], const_dram("swap_i"))
                get(rep4[:, :], const_dram("repeat4"))
                get(w_wi[:, :, :], A["attn_w_in"][0][:, OFF_WI:ATTN_IN].rearrange("(c p) n -> p c n", p=P))
                get(kc[:, :, :], A["cache_k"][0, 0].rearrange("(j p) d -> p j d", p=P))
                get(vc[:, :, :], A["cache_v"][0, 0].rearrange("(j p) d -> p j d", p=P))
                for twice in range(2):
                    get(kic[:, :, twice, :], A["cache_kidx"][0, 0].rearrange("(j p) d -> p j d", p=P))
                load_ahead(sp, a, a + 8)

            @block.scalar
            def _(act):
                start_act(act, "attn", a)
                for n in range(a + 2, a + 8):
                    make_hi(act, n, repeat=DI if n >= a + 6 else 0)
                make_hi(act, a + 8, early=True)

            @block.gpsimd
            def _(pool):
                start_pool(pool, "attn")

            @block.vector
            def _(dve):
                start_dve(dve, "attn", a)

                def evict(g):
                    dve.wait_ge(chunk_used, a + 2 * g + 2)
                    b = 4 * (g % 2)
                    if g < 2:
                        outs = ((qk[:, 4 * g:4 * g + 4, :], 4),)
                    elif g == 2:
                        outs = ((qk[:, HEADS:HEADS + 1, :], 1), (vt[:, :].rearrange("p (a t) -> p a t", a=1), 1),
                                (ix[:, 0:2, :], 2))
                    else:
                        outs = ((ix[:, 2:5, :], 3),)
                    for dst, n in outs:
                        ins = nc.vector.tensor_tensor(dst, PS[:, b:b + n, 0:T], rms1.to_broadcast([P, n, T]), ALU.mult)
                        b += n
                    ins.then_inc(act_s.sem, 1)

                for n in range(a + 2, a + 8):
                    make_lo(dve, n, repeat=DI if n >= a + 6 else 0)
                    if n % 2 == a % 2:
                        evict((n - a) // 2 - 1)
                        for c in range((n - a) - 2, n - a):
                            nc.vector.scalar_tensor_tensor(h[:, c, :], X[:, c, :], vec("ln1_g", 1, c), rstd[:, :],
                                                           ALU.mult, ALU.mult)
                for c in range(6, 8):
                    nc.vector.scalar_tensor_tensor(h[:, c, :], X[:, c, :], vec("ln1_g", 1, c), rstd[:, :],
                                                   ALU.mult, ALU.mult)
                make_lo(dve, a + 8, early=True)
                evict(3)

            @block.tensor
            def _(pe):
                start_pe(pe, "attn", a)
                for g, width in enumerate(WIDTHS):
                    if g == 0:
                        continue
                    if g >= 2:
                        pe.wait_ge(act_s.sem, act_s.at(g - 1))
                    project(pe, a, g, [width])
        start_close("attn")
        act_s.close(4)

        with nc.Block() as block:
            @block.tensor
            def _(pe):
                pe.wait_ge(load.sem, load.at(16 * 12))
                for c in range(HEADS):
                    mm = nc.tensor.matmul(PS[0:32, c, 0:T], swaps[0:32, 0, 0:32], qk[0:32, c, :], start=True,
                                          stop=True)
                mm.then_inc(pe_s.sem, 1)
                pe.wait_ge(dve_s.sem, dve_s.at(1))
                nc.tensor.matmul(PS[0:32, 0, 0:T], swaps[0:32, 0, 0:32], qk[0:32, HEADS, :], start=True, stop=True)
                for c in range(5):
                    mm = nc.tensor.matmul(PS[:, 1 + c, 0:T], swaps[:, 1, :], ix[:, c, :], start=True, stop=True)
                mm.then_inc(pe_s.sem, 1)
                for t, (t0, n) in enumerate(TOK_TILES):
                    for c in range(C):
                        mm = nc.tensor.matmul(PS[0:n, 6, t * 8:t * 8 + 8], h[:, c, t0:t0 + n], w_wi[:, c, :],
                                              start=c == 0, stop=c == C - 1)
                mm.then_inc(pe_s.sem, 1)

            @block.vector
            def _(dve):
                def rotate(x, rotated, bank, cos, sin, done):
                    n, shape = x.shape[1], list(x.shape)
                    nc.vector.tensor_tensor(rot[0:shape[0], 0:n, :], PS[0:shape[0], bank:bank + n, 0:T],
                                            sin.to_broadcast(shape), ALU.mult).then_inc(dve_s.sem, 1)
                    dve_own.step(dve, nc.vector.tensor_tensor(x, x, cos.to_broadcast(shape), ALU.mult))
                    dve.wait_ge(dve_s.sem, dve_s.at(done))
                    dve_own.step(dve, nc.vector.tensor_tensor(x, x, rot[0:shape[0], 0:n, :], ALU.add))

                dve.wait_ge(load.sem, load.at(16 * 12))
                dve.wait_ge(pe_s.sem, pe_s.at(1))
                rotate(qk[0:32, 0:HEADS, :], rot, 0, tables[0:32, 0:1, :], tables[0:32, 1:2, :], 1)
                dve.wait_ge(pe_s.sem, pe_s.at(2))
                rotate(qk[0:32, HEADS:HEADS + 1, :], rot, 0, tables[0:32, 0:1, :], tables[0:32, 1:2, :], 2)
                rotate(ix[:, :, :], rot, 1, tables[:, 2:3, :], tables[:, 3:4, :], 3)
                dve.wait_ge(pe_s.sem, pe_s.at(3))
                for t, (t0, n) in enumerate(TOK_TILES):
                    nc.vector.tensor_scalar(wi[0:n, t, :], PS[0:n, 6, t * 8:t * 8 + 8], IHEADS ** -0.5, None,
                                            ALU.mult)
        load.close(16 * 12)
        pe_s.close(3)
        dve_s.close(3)

        with nc.Block() as block:
            @block.tensor
            def _(pe):
                for t, (t0, n) in enumerate(TOK_TILES):
                    nc.tensor.transpose(PS[0:n, 0, t * DH:(t + 1) * DH], qk[:, HEADS, t0:t0 + n], ident)
                    nc.tensor.transpose(PS[0:n, 1, t * DH:(t + 1) * DH], vt[:, t0:t0 + n], ident)
                    mm = nc.tensor.transpose(PS[0:n, 2, t * DI:(t + 1) * DI], ix[0:DI, 4, t0:t0 + n],
                                             ident[0:DI, 0:DI])
                mm.then_inc(pe_s.sem, 1)
                for j in range(4):
                    nc.tensor.transpose(PS[:, 3, j * P:(j + 1) * P], kc[:, j, :], ident)
                    mm = nc.tensor.transpose(PS[:, 4, j * P:(j + 1) * P],
                                             kic[:, j, :, :].rearrange("p a d -> p (a d)"), ident)
                mm.then_inc(pe_s.sem, 1)

            @block.vector
            def _(dve):
                dve.wait_ge(pe_s.sem, pe_s.at(1))
                for rows, t0, t1 in ((P, 0, 2), (DEC, 2, 3)):
                    for b, (dst, w) in enumerate(((k_tok, DH), (v_tok, DH), (ki_tok, DI))):
                        ins = nc.vector.tensor_copy(
                            dst[0:rows, t0:t1, :],
                            PS[0:rows, b, t0 * w:t1 * w].rearrange("p (t d) -> p t d", d=w))
                ins.then_inc(dve_s.sem, 1)

            @block.scalar
            def _(act):
                act.wait_ge(pe_s.sem, pe_s.at(2))
                nc.scalar.activation(keys_s[:, 0:PAST], PS[:, 3, :], ACT.Copy)
                nc.scalar.activation(ikeys_s[:, 0:PAST], PS[:, 4, :], ACT.Copy)
                nc.scalar.activation(q_s[:, :, :], qk[:, 0:HEADS, SEQ:T], ACT.Copy)
                nc.scalar.activation(keys_s[:, PAST:LS], qk[:, HEADS, SEQ:T], ACT.Copy)
                nc.scalar.activation(ikeys_s[:, PAST:LS], ix[:, 4, SEQ:T], ACT.Copy)

            @block.sync
            def _(sp):
                sp.wait_ge(dve_s.sem, dve_s.at(1))
                for k, tok in enumerate((k_tok, v_tok, ki_tok)):
                    sp.dma_start(O[4 + 2 * k][0, 0].rearrange("(t p) d -> p t d", p=P), tok[:, 0:2, :]) \
                        .then_inc(S["store"].sem, 16)
                    sp.dma_start(O[5 + 2 * k][0, 0], tok[0:DEC, 2, :]).then_inc(S["store"].sem, 16)
        pe_s.close(2)
        dve_s.close(1)
        S["store"].close(16 * 6)

        LOGIT_JOBS = ((2, 0, 1), (2, 1, 2), (1, 0, 4), (1, 4, 8), (0, 0, 8))
        TURN = (2, 1, 0)
        max_ready, exp_ready, prob_ready, turned, turned_out, value_ready, value_out, taken, repeated = (
            S[n] for n in ("max_ready", "exp_ready", "prob_ready", "turned", "turned_out", "value_ready",
                           "value_out", "taken", "repeated"))
        with nc.Block() as block:
            @block.tensor
            def _(pe):
                u = 0
                for q, nq, L in reversed(tiles):
                    t0 = TOK_TILES[q][0]
                    for hd in range(IHEADS):
                        if u >= 2:
                            pe.wait_ge(act_s.sem, act_s.at(u - 1))
                        lo = DI * (hd % 2)
                        keys = ikeys_s[lo:lo + DI, :] if q == 2 else ix[lo:lo + DI, 4, :]
                        for k0 in range(0, L, 512):
                            k1 = min(L, k0 + 512)
                            mm = nc.tensor.matmul(PS[0:nq, 2 * (u % 2) + k0 // 512, 0:k1 - k0],
                                                  ix[lo:lo + DI, hd // 2, t0:t0 + nq], keys[:, k0:k1],
                                                  start=True, stop=True)
                        mm.then_inc(pe_s.sem, 1)
                        u += 1
                for i, (q, g0, g1) in enumerate(LOGIT_JOBS):
                    b = 4 + 2 * (i % 2)
                    if i >= 2:
                        pe.wait_ge(act_s.sem, act_s.at(24 + i - 1))
                    for g in range(g0, g1):
                        if q == 2:
                            lhs = q_s[:, 4 * g:4 * g + 4, :].rearrange("p a b -> p (a b)")
                            for k0, k1 in ((0, 512), (512, LS)):
                                mm = nc.tensor.matmul(PS[:, b + k0 // 512, 0:k1 - k0], lhs, keys_s[:, k0:k1],
                                                      start=True, stop=True)
                        else:
                            L = P * (q + 1)
                            col = (g - g0) * L
                            mm = nc.tensor.matmul(PS[:, b + col // 512, col % 512:col % 512 + L],
                                                  qk[:, g, q * P:(q + 1) * P], qk[:, HEADS, 0:L],
                                                  start=True, stop=True)
                    mm.then_inc(pe_s.sem, 1)

                def turn(q):
                    pe.wait_ge(prob_ready.sem, prob_ready.at(TURN[q] + 1))
                    if TURN[q]:
                        pe.wait_ge(turned_out.sem, turned_out.at(TURN[q]))
                    for g in range(HEADS if q < 2 else 2):
                        for k in range(q + 1 if q < 2 else 4):
                            col = (g * (q + 1 if q < 2 else 4) + k) * P
                            mm = nc.tensor.transpose(PS[:, col // 512, col % 512:col % 512 + P],
                                                     prob[q][:, g, k * P:(k + 1) * P], ident)
                        if q == 2:
                            mm = nc.tensor.transpose(PS[0:DEC, 2, g * P:(g + 1) * P], prob[2][:, g, PAST:LS], ident)
                    mm.then_inc(turned.sem, 1)

                def values(q):
                    pe.wait_ge(turned_out.sem, turned_out.at(TURN[q] + 1))
                    if TURN[q] == 1:
                        pe.wait_ge(value_out.sem, value_out.at(1))
                    nk = q + 1 if q < 2 else 5
                    for g in range(HEADS if q < 2 else 2):
                        for k in range(nk):
                            w = DEC if k == 4 else P
                            val = v_tok[:, k, :] if q < 2 else (vc[:, k, :] if k < 4 else v_tok[0:DEC, 2, :])
                            b = (4, 6, 6)[q] + g // 4
                            mm = nc.tensor.matmul(PS[:, b, (g % 4) * P:(g % 4 + 1) * P], val,
                                                  prob_t[q][0:w, g, k, :], start=k == 0, stop=k == nk - 1)
                    mm.then_inc(value_ready.sem, 1)

                pe.wait_ge(act_s.sem, act_s.at(29))
                pe.wait_ge(taken.sem, taken.at(1))
                for k0, k1 in ((0, 512), (512, LS)):
                    mm = nc.tensor.matmul(PS[:, 4 + k0 // 512, 0:k1 - k0], rep4[0:DEC, :], score[2][0:DEC, k0:k1],
                                          start=True, stop=True)
                mm.then_inc(repeated.sem, 1)
                for q in (2, 1, 0):
                    turn(q)
                    values(q)

            @block.scalar
            def _(act):
                u = 0
                for q, nq, L in reversed(tiles):
                    for hd in range(IHEADS):
                        act.wait_ge(pe_s.sem, pe_s.at(u + 1))
                        if u >= 2:
                            act.wait_ge(dve_s.sem, dve_s.at(u - 1))
                        for k0 in range(0, L, 512):
                            k1 = min(L, k0 + 512)
                            ins = nc.scalar.activation(dots[0:nq, u % 2, k0:k1],
                                                       PS[0:nq, 2 * (u % 2) + k0 // 512, 0:k1 - k0], ACT.Relu,
                                                       scale=DI ** -0.5)
                        ins.then_inc(act_s.sem, 1)
                        u += 1
                for i, (q, g0, g1) in enumerate(LOGIT_JOBS):
                    b = 4 + 2 * (i % 2)
                    act.wait_ge(pe_s.sem, pe_s.at(25 + i))
                    if q == 2:
                        nc.scalar.activation(prob[2][:, g0, 0:512], PS[:, b, :], ACT.Copy)
                        ins = nc.scalar.activation(prob[2][:, g0, 512:LS], PS[:, b + 1, 0:LS - 512], ACT.Copy)
                    else:
                        ins = nc.scalar.activation(
                            prob[q][:, g0:g1, :].rearrange("p (b g) k -> p b (g k)", b=2), PS[:, b:b + 2, :],
                            ACT.Copy)
                    ins.then_inc(act_s.sem, 1)

                def exps(q):
                    act.wait_ge(max_ready.sem, max_ready.at(TURN[q] + 1))
                    for g in range(HEADS if q < 2 else 2):
                        ins = nc.scalar.activation(prob[q][:, g, :], prob[q][:, g, :], ACT.Exp,
                                                   bias=stat[:, q, 0, g:g + 1], scale=DH ** -0.5,
                                                   accum_out=stat[:, q, 1, g:g + 1])
                    ins.then_inc(exp_ready.sem, 1)

                def turn_out(q):
                    act.wait_ge(turned.sem, turned.at(TURN[q] + 1))
                    if q == 2:
                        nc.scalar.activation(prob_t[2][0:DEC, :, 4, :],
                                             PS[0:DEC, 2, 0:2 * P].rearrange("p (g n) -> p g n", n=P), ACT.Copy)
                        for g in range(2):
                            ins = nc.scalar.activation(prob_t[2][:, g, 0:4, :],
                                                       PS[:, g, :].rearrange("p (k n) -> p k n", n=P), ACT.Copy)
                    else:
                        nb = 2 * (q + 1)
                        ins = nc.scalar.activation(
                            prob_t[q][:, :, :, :].rearrange("p g k n -> p (g k n)").rearrange(
                                "p (b n) -> p b n", b=nb), PS[:, 0:nb, :], ACT.Copy)
                    ins.then_inc(turned_out.sem, 1)

                def value_copy(q):
                    act.wait_ge(value_ready.sem, value_ready.at(TURN[q] + 1))
                    if q == 2:
                        ins = nc.scalar.activation(
                            o[:, :, SEQ:T], PS[:, 6, 0:2 * P].rearrange("p (h n) -> p h n", n=DEC), ACT.Copy)
                    else:
                        b = (4, 6)[q]
                        ins = nc.scalar.activation(
                            o[:, :, q * P:(q + 1) * P].rearrange("p (b g) n -> p b g n", b=2),
                            PS[:, b:b + 2, :].rearrange("p b (g n) -> p b g n", n=P), ACT.Copy)
                    ins.then_inc(value_out.sem, 1)

                exps(2)
                exps(1)
                turn_out(2)
                value_copy(2)
                turn_out(1)
                exps(0)
                value_copy(1)
                turn_out(0)
                value_copy(0)

            @block.vector
            def _(dve):
                V = nc.vector
                u = 0
                for q, nq, L in reversed(tiles):
                    s = score[q]
                    for hd in range(IHEADS):
                        dve.wait_ge(act_s.sem, act_s.at(u + 1))
                        w = wi[0:nq, q, hd:hd + 1]
                        if hd == 0:
                            V.tensor_scalar(s[0:nq, 0:L], dots[0:nq, u % 2, 0:L], w, None, ALU.mult) \
                                .then_inc(dve_s.sem, 1)
                        else:
                            dve.wait_ge(dve_s.sem, dve_s.at(u))
                            V.scalar_tensor_tensor(s[0:nq, 0:L], dots[0:nq, u % 2, 0:L], w, s[0:nq, 0:L],
                                                   ALU.mult, ALU.add).then_inc(dve_s.sem, 1)
                        u += 1
                dve.wait_ge(dve_s.sem, dve_s.at(u))
                dve_own.step(dve, V.memset(score[0][0:CHUNK, CHUNK:P], NEG))
                dve_own.step(dve, V.memset(score[1][0:CHUNK, 3 * CHUNK:SEQ], NEG))

                def select(q):
                    _, nq, L = tiles[q]
                    s = score[q]
                    for _ in range((TOPK_S if q == 2 else TOPK_P) // 8):
                        dve_own.step(dve, V.max(best[0:nq, :], s[0:nq, 0:L]))
                        dve_own.step(dve, V.match_replace(s[0:nq, 0:L], best[0:nq, :], s[0:nq, 0:L], TAKEN))
                    return V.tensor_scalar(s[0:nq, 0:L], s[0:nq, 0:L], 0.5 * (NEG + TAKEN), NEG, ALU.is_gt, ALU.mult)

                def maxima(q):
                    n = HEADS if q < 2 else 2
                    dve.wait_ge(act_s.sem, act_s.at(29))
                    if q < 2:
                        L = P * (q + 1)
                        dve_own.step(dve, V.tensor_tensor(prob[q][:, :, :], prob[q][:, :, :],
                                                          score[q][:, :].unsqueeze(1).to_broadcast([P, n, L]),
                                                          ALU.add))
                    else:
                        dve.wait_ge(repeated.sem, repeated.at(1))
                        for k0, k1 in ((0, 512), (512, LS)):
                            dve_own.step(dve, V.tensor_tensor(
                                prob[2][:, :, k0:k1], prob[2][:, :, k0:k1],
                                PS[:, 4 + k0 // 512:5 + k0 // 512, 0:k1 - k0].to_broadcast([P, 2, k1 - k0]), ALU.add))
                    dve_own.step(dve, V.tensor_reduce(stat[:, q, 0, 0:n], prob[q][:, :, :], AX.X, ALU.max))
                    V.tensor_scalar(stat[:, q, 0, 0:n], stat[:, q, 0, 0:n], -DH ** -0.5, None, ALU.mult) \
                        .then_inc(max_ready.sem, 1)

                def normalise(q):
                    n = HEADS if q < 2 else 2
                    L = P * (q + 1) if q < 2 else LS
                    dve.wait_ge(exp_ready.sem, exp_ready.at(TURN[q] + 1))
                    dve_own.step(dve, V.reciprocal(stat[:, q, 2, 0:n], stat[:, q, 1, 0:n]))
                    V.tensor_tensor(prob[q][:, :, :], prob[q][:, :, :],
                                    stat[:, q, 2, 0:n].unsqueeze(2).to_broadcast([P, n, L]), ALU.mult) \
                        .then_inc(prob_ready.sem, 1)

                select(2).then_inc(taken.sem, 1)
                dve_own.step(dve, select(1))
                maxima(2)
                maxima(1)
                dve_own.step(dve, select(0))
                normalise(2)
                maxima(0)
                normalise(1)
                normalise(0)
        pe_s.close(29)
        act_s.close(29)
        dve_s.close(24)
        for sig, n in ((max_ready, 3), (exp_ready, 3), (prob_ready, 3), (turned, 3), (turned_out, 3),
                       (value_ready, 3), (value_out, 3), (taken, 1), (repeated, 1)):
            sig.close(n)
        project_residual("attn", "attn_out", o)
        with nc.Block() as block:
            @block.sync
            def _(sp):
                sp.wait_ge(S["store"].sem, S["store"].at(0))

    def stage_rwkv():
        a0 = first_chunk["rwkv_w_r"]
        load, pe_s, dve_s, act_s, pool_s = (S[k] for k in ("stage_load", "stage_pe", "stage_dve", "stage_act",
                                                           "stage_pool"))
        ARC = [P, C, T]
        H = P // N
        y_hi, y_lo = at("lerp_hi", unit(2), ARC, F32R), at("lerp_lo", unit(3), ARC, F32R)
        logw = at("log_decay", unit(3), ARC)
        r, k, v = at("r", unit(4), ARC), at("k", unit(5), ARC), at("v", unit(6), ARC)
        rate = at("rate", unit(7), ARC)
        gate = at("gate", unit(8), ARC)
        bonus = at("bonus", unit(9), ARC)
        t1, t2 = at("t1", unit(10), ARC), at("t2", unit(11), ARC)
        ar = at("ar", unit(12), [P, 2, C, T])
        bt = at("bt", unit(4), ARC)
        temp = at("rwkv_temp", unit(2), ARC)
        HS = T + 2
        hs = at("rwkv_h", unit(11), [P, C, HS])
        delta = at("delta", unit(13), ARC)
        lerp = at("lerp", unit(10), ARC)
        sq = at("rwkv_sq", unit(9), ARC)
        lora = Area(unit(8))
        w1 = lora.take("decay_w1", [P, C, N])
        a1 = lora.take("rate_w1", [P, C, N])
        g1 = lora.take("gate_w1", [P, C, P])
        shift_row = at("shift_row", unit(8) + 8192, [P, P])
        shift_out = at("shift_out", unit(8) + 8192, [P, 2, P])
        scan_keep = at("scan_keep", unit(8), [P, T])
        w2, a2 = at("decay_w2", unit(9), [P, D]), at("rate_w2", unit(9) + 4096, [P, D])
        HN = D // N
        to_head = at("to_head", unit(9) + 8192, [P, C, HN])
        g2 = at("gate_w2", hi_at, [P, D])
        inner = at("lora_inner", unit(14), [P, 3, T])
        last_decay = at("last_decay", unit(14) + 3456, [P, C, NCH])
        LAST = (SEQ, HS - 1)
        parts = ((1, 0, SEQ), (SEQ + 2, SEQ, DEC))

        lerp_s, in_hi, in_lo = S["lerp_ready"], S["in_hi"], S["in_lo"]
        inner_s, inner_out, lora_s, lora_out, proj_out = (S[n] for n in ("inner_done", "inner_out", "lora_done",
                                                                         "lora_out", "proj_out"))
        lora_lerps = (at("lerp_a", unit(2), ARC), at("lerp_g", unit(3), ARC), at("lerp_w", unit(9), ARC))
        splits = ((x_hi, x_lo), (y_hi, y_lo), (x_hi, x_lo))
        with nc.Block() as block:
            @block.sync
            def _(sp):
                sp.dma_start(shift_row[0:C, :], A["state_shift"][0, 0].rearrange("a (c p) -> (a c) p", p=P)) \
                    .then_inc(load.sem, 16)
                for dst, name in ((w1, "rwkv_w1"), (a1, "rwkv_a1"), (g1, "rwkv_g1")):
                    sp.dma_start(dst[:, :, :], A[name][0].rearrange("(c p) n -> p c n", p=P)).then_inc(load.sem, 16)
                load_ahead(sp, a0, a0 + 5)
                sp.wait_ge(inner_s.sem, inner_s.at(3))
                for dst, name in ((w2, "rwkv_w2"), (a2, "rwkv_a2")):
                    sp.dma_start(dst[0:N, :], A[name][0]).then_inc(S["load2"].sem, 16)
                sp.dma_start(scan_keep[:, :], const_dram("scan_keep")).then_inc(S["load2"].sem, 16)
                sp.dma_start(to_head[:, :, :].rearrange("p c n -> p (c n)"), const_dram("to_head")) \
                    .then_inc(S["load2"].sem, 16)
                sp.wait_ge(inner_out.sem, inner_out.at(3))
                for g in range(2):
                    sp.dma_start(O[10 + g][0, 0].rearrange("a (c p) -> (a c) p", p=P), shift_out[0:C, g, :]) \
                        .then_inc(S["store"].sem, 16)
                load_ahead(sp, a0 + 5, a0 + 12)
                sp.wait_ge(S["store"].sem, S["store"].at(32))

            @block.gpsimd
            def _(pool):
                nc.gpsimd.memset(hs[:, :, 0:1], 0.0).then_inc(pool_s.sem, 1)

            @block.tensor
            def _(pe):
                pe.wait_ge(load.sem, load.at(64))
                nc.tensor.transpose(PS[:, 0, 0:C], shift_row[0:C, :], ident[0:C, 0:C]).then_inc(pe_s.sem, 1)
                norm_pe(pe, sq)
                for p in range(3):
                    hi, lo = splits[p]
                    for g in range(2):
                        if p == 1:
                            pe.wait_ge(*((inner_out.sem, inner_out.at(4)), (proj_out.sem, proj_out.at(2)))[g])
                        if p == 2:
                            pe.wait_ge(lora_out.sem, lora_out.at(3 + g))
                        for half in range(2):
                            n = a0 + 4 * p + 2 * g + half
                            pe.wait_ge(lo_made, n + 1)
                            if g == 0:
                                pe.wait_ge(in_lo.sem, in_lo.at(2 * p + half + 1))
                            use_chunk(n % 2, lambda k: hi[:, half * KT + k, :], lambda k: lo[:, half * KT + k, :],
                                      4 * g, half == 0, half == 1).then_inc(chunk_used, 1)
                    if p == 0:
                        pe.wait_ge(proj_out.sem, proj_out.at(1))
                        for j, w in enumerate((a1, g1, w1)):
                            n = w.shape[2]
                            if j == 2:
                                for g in range(2):
                                    nc.tensor.transpose(PS[0:C, 3, g * P:(g + 1) * P], hs[:, :, LAST[g]], ident)
                            for c in range(C):
                                pe.wait_ge(lerp_s.sem, lerp_s.at(C * (j + 1) + c + 1))
                                mm = nc.tensor.matmul(PS[0:n, j, 0:T], w[:, c, :], lora_lerps[j][:, c, :],
                                                      start=c == 0, stop=c == C - 1)
                            mm.then_inc(inner_s.sem, 1)
                    if p == 1:
                        pe.wait_ge(S["load2"].sem, S["load2"].at(64))
                        for s in range(4):
                            j, b = s // 2, 4 * (s % 2)
                            pe.wait_ge(*((proj_out.sem, proj_out.at(3 + s)) if s < 2 else
                                         (lora_out.sem, lora_out.at(s - 1))))
                            for m in range(4):
                                c = 4 * (s % 2) + m
                                mm = nc.tensor.matmul(PS[:, b + m, 0:T], (w2, a2)[j][0:N, c * P:(c + 1) * P],
                                                      inner[0:N, (2, 0)[j], :], start=True, stop=True)
                            mm.then_inc(lora_s.sem, 1)
                pe.wait_ge(act_s.sem, act_s.at(1))
                pe.wait_ge(proj_out.sem, proj_out.at(5))
                for c in range(C):
                    nc.tensor.matmul(PS[0:HN, 0, 0:T], to_head[:, c, :], t2[:, c, :], start=c == 0, stop=c == C - 1)

            @block.scalar
            def _(act):
                norm_act(act, sq)

                def evict(p, g):
                    act.wait_ge(chunk_used, a0 + 4 * p + 2 * g + 2)
                    nc.scalar.activation((r, k, v)[p][:, 4 * g:4 * g + 4, :], PS[:, 4 * g:4 * g + 4, 0:T], ACT.Copy) \
                        .then_inc(proj_out.sem, 1)

                def hi_of_input(p):
                    for half in range(2):
                        act.wait_ge(lerp_s.sem, lerp_s.at((0, 32, 40)[p] + KT * half + KT))
                        nc.scalar.activation(splits[p][0][:, KT * half:KT * half + KT, :],
                                             lerp[:, KT * half:KT * half + KT, :], ACT.Copy).then_inc(in_hi.sem, 1)

                def inner_evict(j, fn, n):
                    act.wait_ge(inner_s.sem, inner_s.at(j + 1))
                    nc.scalar.activation(inner[0:n, j, :], PS[0:n, j, 0:T], fn).then_inc(inner_out.sem, 1)

                hi_of_input(0)
                for n in range(a0, a0 + 4):
                    make_hi(act, n)
                evict(0, 0)
                make_hi(act, a0 + 4)
                evict(0, 1)
                make_hi(act, a0 + 5)
                inner_evict(0, ACT.Copy, N)
                hi_of_input(1)
                inner_evict(1, ACT.Sigmoid, P)
                act.wait_ge(inner_s.sem, inner_s.at(3))
                nc.scalar.activation(shift_out[0:C, :, :], PS[0:C, 3, 0:2 * P].rearrange("p (a b) -> p a b", a=2),
                                     ACT.Copy).then_inc(inner_out.sem, 1)
                inner_evict(2, ACT.Tanh, N)
                make_hi(act, a0 + 6)
                hi_of_input(2)
                make_hi(act, a0 + 7)
                evict(1, 0)
                make_hi(act, a0 + 8)
                evict(1, 1)
                for s in range(4):
                    act.wait_ge(lora_s.sem, lora_s.at(s + 1))
                    j, b, c0 = s // 2, 4 * (s % 2), 4 * (s % 2)
                    for m in range(4):
                        ins = nc.scalar.activation((logw, rate)[j][:, c0 + m, :], PS[:, b + m, 0:T], ACT.Sigmoid,
                                                   bias=vec(("rwkv_w0", "rwkv_a0")[j], 0, c0 + m))
                    ins.then_inc(lora_out.sem, 1)
                make_hi(act, a0 + 9)
                make_hi(act, a0 + 10)
                act.wait_ge(proj_out.sem, proj_out.at(4))
                act.wait_ge(in_lo.sem, in_lo.at(6))
                for c in range(C):
                    nc.scalar.activation(t2[:, c, :], k[:, c, :], ACT.Square, scale=vec("rwkv_k_k", 0, c))
                make_hi(act, a0 + 11)
                for c in range(C):
                    ins = nc.scalar.activation(t1[:, c, :], k[:, c, :], ACT.Copy, scale=vec("rwkv_k_k", 0, c))
                ins.then_inc(act_s.sem, 1)
                evict(2, 0)
                evict(2, 1)

            @block.vector
            def _(dve):
                V = nc.vector
                dve.wait_ge(pe_s.sem, pe_s.at(1))
                V.tensor_copy(hs[:, :, SEQ + 1], PS[:, 0, 0:C]).then_inc(dve_s.sem, 1)
                norm_dve(dve, "ln1_g", 2, lambda c: [(hs[:, c, 1:SEQ + 1], (0, SEQ)),
                                                     (hs[:, c, SEQ + 2:HS], (SEQ, T))])
                dve.wait_ge(S["h_ready"].sem, S["h_ready"].at(C))
                dve.wait_ge(dve_s.sem, dve_s.at(1))
                dve.wait_ge(pool_s.sem, pool_s.at(1))
                for col, t, n in parts:
                    V.tensor_tensor(delta[:, :, t:t + n], hs[:, :, col - 1:col - 1 + n], hs[:, :, col:col + n],
                                    ALU.subtract).then_inc(dve_s.sem, 1)
                dve.wait_ge(dve_s.sem, dve_s.at(3))

                def interpolate(dst, mix):
                    for c in range(C):
                        for col, t, n in parts:
                            ins = V.scalar_tensor_tensor(dst[:, c, t:t + n], delta[:, c, t:t + n],
                                                         vec("rwkv_mix", mix, c), hs[:, c, col:col + n],
                                                         ALU.mult, ALU.add)
                        ins.then_inc(lerp_s.sem, 1)

                def lo_of_input(p, half):
                    dve.wait_ge(in_hi.sem, in_hi.at(2 * p + half + 1))
                    c4 = slice(KT * half, KT * half + KT)
                    V.tensor_tensor(splits[p][1][:, c4, :], lerp[:, c4, :], splits[p][0][:, c4, :].bitcast(F32),
                                    ALU.subtract).then_inc(in_lo.sem, 1)

                interpolate(lerp, 0)
                lo_of_input(0, 0)
                make_lo(dve, a0)
                lo_of_input(0, 1)
                make_lo(dve, a0 + 1)
                dve.wait_ge(in_lo.sem, in_lo.at(2))
                interpolate(lora_lerps[0], 4)
                make_lo(dve, a0 + 2)
                interpolate(lora_lerps[1], 5)
                make_lo(dve, a0 + 3)
                interpolate(lora_lerps[2], 1)
                interpolate(lerp, 2)
                make_lo(dve, a0 + 4)
                dve.wait_ge(inner_s.sem, inner_s.at(2))
                lo_of_input(1, 0)
                lo_of_input(1, 1)
                make_lo(dve, a0 + 5)
                dve.wait_ge(in_lo.sem, in_lo.at(4))
                interpolate(lerp, 3)
                make_lo(dve, a0 + 6)
                dve.wait_ge(chunk_used, a0 + 4)
                lo_of_input(2, 0)
                lo_of_input(2, 1)
                for n in range(a0 + 7, a0 + 10):
                    make_lo(dve, n)
                dve.wait_ge(lora_out.sem, lora_out.at(2))
                dve.wait_ge(lerp_s.sem, lerp_s.at(6 * C))
                dve_own.step(dve, V.tensor_scalar(logw[:, :, :], logw[:, :, :], -float(np.exp(-0.5)), None, ALU.mult))
                for c in range(C):
                    V.tensor_tensor_scan(ar[:, 1, c, :], scan_keep[:, :], logw[:, c, :], 0.0, ALU.mult, ALU.add) \
                        .then_inc(dve_own.sem, 1)
                dve_own.n += C
                dve.wait_ge(dve_own.sem, dve_own.n)
                make_lo(dve, a0 + 10)
                V.tensor_tensor(logw[:, :, :], ar[:, 1, :, :], logw[:, :, :], ALU.subtract)
                dve.wait_ge(lora_out.sem, lora_out.at(4))
                for c in range(C):
                    V.tensor_scalar(temp[:, c, :], rate[:, c, :], 1.0, vec("rwkv_k_a", 0, c), ALU.subtract, ALU.mult) \
                        .then_inc(dve_own.sem, 1)
                dve_own.n += C
                make_lo(dve, a0 + 11)
                dve.wait_ge(dve_own.sem, dve_own.n)
                dve.wait_ge(act_s.sem, act_s.at(1))
                dve_own.step(dve, V.scalar_tensor_tensor(k[:, :, :], temp[:, :, :], 1.0, k[:, :, :], ALU.add, ALU.mult))
                for c in range(C):
                    V.scalar_tensor_tensor(temp[:, c, :], r[:, c, :], vec("rwkv_r_k", 0, c), k[:, c, :],
                                           ALU.mult, ALU.mult)
        norm_close()
        for sig, n in ((load, 64), (pool_s, 1), (pe_s, 1), (dve_s, 3), (act_s, 1), (S["load2"], 64), (lerp_s, 6 * C),
                       (in_hi, 6), (in_lo, 6), (inner_s, 3), (inner_out, 4), (lora_s, 4), (lora_out, 4),
                       (proj_out, 6), (S["store"], 32)):
            sig.close(n)

        tri = at("triangles", hi_at + 31232, [P, 4, TT])
        from_head = at("from_head", hi_at + 4096, [P, C, P])
        norm_inv = at("key_norm_inverse", hi_at + 8192, [P, T])
        grown, shrunk = at("decay_to_token", unit(0), ARC), at("decay_inverse", unit(1), ARC)
        seg = "p c (j s) -> p (c j) s"
        LAST_DECAY = last_decay[:, :, :].rearrange("p c j -> p (c j)").unsqueeze(2).to_broadcast([P, C * NCH, CH])
        with nc.Block() as block:
            @block.sync
            def _(sp):
                sp.dma_start(from_head[0:HN, :, :].rearrange("p c n -> p (c n)"), const_dram("from_head", HN)) \
                    .then_inc(load.sem, 16)
                sp.dma_start(g2[:, :], A["rwkv_g2"][0]).then_inc(load.sem, 16)
                o0 = const_order["row_after_col"][0]
                sp.dma_start(tri[:, :, :].rearrange("p a b -> p (a b)"), consts[:, o0:o0 + 4 * TT]) \
                    .then_inc(S["load2"].sem, 16)

            @block.scalar
            def _(act):
                act.wait_ge(dve_s.sem, dve_s.at(1))
                nc.scalar.activation(norm_inv[0:HN, :], norm_inv[0:HN, :], ACT.Sqrt).then_inc(act_s.sem, 1)
                nc.scalar.activation(logw[:, :, :], logw[:, :, :], ACT.Exp).then_inc(act_s.sem, 1)
                nc.scalar.activation(grown[:, :, :], ar[:, 1, :, :], ACT.Exp).then_inc(act_s.sem, 1)
                nc.scalar.activation(shrunk[:, :, :], ar[:, 1, :, :], ACT.Exp, scale=-1.0).then_inc(act_s.sem, 1)
                for i, c0 in enumerate((4, 0)):
                    act.wait_ge(pe_s.sem, pe_s.at(5 + i))
                    nc.scalar.activation(gate[:, c0:c0 + 4, :], PS[:, c0:c0 + 4, 0:T], ACT.Copy)

            @block.tensor
            def _(pe):
                def four(bank, c0, lhs, rhs):
                    for m in range(4):
                        mm = nc.tensor.matmul(PS[:, bank + m, 0:T], lhs(c0 + m), rhs(c0 + m), start=True, stop=True)
                    mm.then_inc(pe_s.sem, 1)

                def head_sums(bank, c0):
                    four(bank, c0, lambda c: head_ones, lambda c: temp[:, c, :])

                def spread_norms(bank, c0):
                    four(bank, c0, lambda c: from_head[0:HN, c, :], lambda c: norm_inv[0:HN, :])

                def gates(bank, c0):
                    four(bank, c0, lambda c: g2[:, c * P:(c + 1) * P], lambda c: inner[:, 1, :])

                head_sums(4, 0)
                pe.wait_ge(load.sem, load.at(32))
                pe.wait_ge(act_s.sem, act_s.at(1))
                spread_norms(0, 0)
                pe.wait_ge(dve_s.sem, dve_s.at(2))
                spread_norms(4, 4)
                pe.wait_ge(dve_s.sem, dve_s.at(3))
                head_sums(0, 4)
                pe.wait_ge(dve_s.sem, dve_s.at(4))
                gates(4, 4)
                pe.wait_ge(dve_s.sem, dve_s.at(5))
                gates(0, 0)

            @block.gpsimd
            def _(pool):
                pool.wait_ge(act_s.sem, act_s.at(4))
                nc.gpsimd.tensor_tensor(k[:, :, :], k[:, :, :], shrunk[:, :, :], ALU.mult).then_inc(pool_s.sem, 1)
                pool.wait_ge(pool_s.sem, pool_s.at(1))
                pool.wait_ge(dve_s.sem, dve_s.at(6))
                nc.gpsimd.tensor_tensor(t2[:, :, :].rearrange(seg, s=CH), k[:, :, :].rearrange(seg, s=CH), LAST_DECAY,
                                        ALU.mult).then_inc(pool_s.sem, 1)

            @block.vector
            def _(dve):
                def step(ins):
                    dve_own.step(dve, ins)
                V = nc.vector
                step(V.tensor_scalar(norm_inv[0:HN, :], PS[0:HN, 0, 0:T], 1e-24, None, ALU.max))
                V.reciprocal(norm_inv[0:HN, :], norm_inv[0:HN, :]).then_inc(dve_s.sem, 1)

                def bonuses(done, bank, c0):
                    dve.wait_ge(pe_s.sem, pe_s.at(done))
                    V.tensor_tensor(bonus[:, c0:c0 + 4, :], PS[:, bank:bank + 4, 0:T], v[:, c0:c0 + 4, :], ALU.mult) \
                        .then_inc(dve_s.sem, 1)

                bonuses(1, 4, 0)
                for q in range(2):
                    c4 = slice(4 * q, 4 * q + 4)
                    dve.wait_ge(pe_s.sem, pe_s.at(q + 2))
                    V.tensor_tensor(t1[:, c4, :], t1[:, c4, :], PS[:, c4, 0:T], ALU.mult).then_inc(dve_s.sem, 1)
                bonuses(4, 0, 4)
                dve.wait_ge(dve_s.sem, dve_s.at(4))
                dve.wait_ge(act_s.sem, act_s.at(2))
                step(V.scalar_tensor_tensor(ar[:, 0, :, :], t1[:, :, :], -1.0, logw[:, :, :], ALU.mult, ALU.mult))
                V.tensor_tensor(t1[:, :, :], t1[:, :, :], rate[:, :, :], ALU.mult).then_inc(dve_own.sem, 1)
                dve_own.n += 1
                dve.wait_ge(act_s.sem, act_s.at(3))
                V.tensor_copy(last_decay[:, :, :], grown[:, :, :].rearrange("p c (j s) -> p c j s", s=CH)[:, :, :, CH - 1]) \
                    .then_inc(dve_s.sem, 1)
                dve.wait_ge(act_s.sem, act_s.at(4))
                step(V.tensor_tensor(ar[:, 1, :, :], r[:, :, :], grown[:, :, :], ALU.mult))
                dve.wait_ge(dve_s.sem, dve_s.at(6))
                step(V.tensor_tensor(bt[:, :, :], t1[:, :, :], shrunk[:, :, :], ALU.mult))
                step(V.tensor_tensor(t1[:, :, :].rearrange(seg, s=CH), bt[:, :, :].rearrange(seg, s=CH), LAST_DECAY,
                                     ALU.mult))
        load.close(32)
        S["load2"].close(16)
        act_s.close(4)
        pe_s.close(6)
        dve_s.close(6)
        pool_s.close(2)

        TOK = [P, NT, D]
        a_tok = at("a_tok", unit(0), TOK)
        b_tok = at("b_tok", unit(0) + 12288, TOK)
        k_tok = at("k_tokens", unit(0) + 24576, TOK)
        v_tok = at("v_tokens", unit(10), TOK)
        sources = ((t1[:, :, :], b_tok), (t2[:, :, :], k_tok), (ar[:, 0, :, :], a_tok), (v[:, :, :], v_tok))
        jobs = [(src, dst, t) for src, dst in sources for t in range(NT)]
        with nc.Block() as block:
            @block.tensor
            def _(pe):
                for i, (src, dst, t) in enumerate(jobs):
                    if i >= 4:
                        s = (act_s, dve_s)[i % 2]
                        pe.wait_ge(s.sem, s.at((i - 4) // 2 + 1))
                    for c in range(C):
                        mm = nc.tensor.transpose(PS[0:TT, 2 * (i % 4) + c // 4, (c % 4) * P:(c % 4 + 1) * P],
                                                 src[:, c, t * TT:(t + 1) * TT], ident)
                    mm.then_inc(pe_s.sem, 1)

            def copy_out(eng, odd, sig):
                for i, (src, dst, t) in enumerate(jobs):
                    if i % 2 == odd:
                        eng.wait_ge(pe_s.sem, pe_s.at(i + 1))
                        out = dst[0:TT, t, :].rearrange("p (b n) -> p b n", b=2)
                        ps = PS[0:TT, 2 * (i % 4):2 * (i % 4) + 2, :]
                        ins = nc.vector.tensor_copy(out, ps) if odd else nc.scalar.activation(out, ps, ACT.Copy)
                        ins.then_inc(sig.sem, 1)

            @block.scalar
            def _(act):
                copy_out(act, 0, act_s)

            @block.vector
            def _(dve):
                copy_out(dve, 1, dve_s)
        pe_s.close(12)
        act_s.close(6)
        dve_s.close(6)

        scratch = Area(hi_at)
        gram = scratch.take("gram", [P, H, 3, NT * TT])
        power = [scratch.take(f"power{i}", [P, H, 2, NT * TT]) for i in range(2)]
        inv = [scratch.take(f"inverse{i}", [P, 6, TT]) for i in range(2)]
        lv = scratch.take("lv", [P, 6, N])
        wt = at("wt", unit(6), ARC)
        state_rows = at("state_rows", unit(10) + 12288, [P, D // N, N])
        LEVELS = 5
        with nc.Block() as block:
            @block.sync
            def _(sp):
                sp.dma_start(state_rows[0:N, :, :], A["state_wkv"][0, 0].rearrange("h v k -> v h k")) \
                    .then_inc(load.sem, 16)

            def systems(half):
                return [(3 * half + t, t) for t in range(NT)]

            def head(x, c, half, t):
                return x[N * half:N * half + N, c, t * TT:(t + 1) * TT]

            def pair(level, half, t):
                m = gram if level == 0 else power[level % 2]
                return (m[0:TT, half, kind, t * TT:(t + 1) * TT] for kind in range(2))

            def bank(half, kind, t):
                return PS[0:TT, 3 * half + kind, t * TT:(t + 1) * TT]

            PE_N, ACT_N, DVE_N = 2 * (LEVELS + 1), 2 * (LEVELS - 1), 2 * LEVELS

            @block.tensor
            def _(pe):
                def grams(c):
                    for half in range(H):
                        if c:
                            pe.wait_ge(dve_s.sem, dve_s.at(DVE_N * c - 1 + half))
                        for s, t in systems(half):
                            a_, b_, k_ = head(ar[:, 0, :, :], c, half, t), head(bt, c, half, t), head(k, c, half, t)
                            nc.tensor.matmul(bank(half, 0, t), a_, b_, start=True, stop=True)
                            nc.tensor.matmul(bank(half, 1, t), b_, a_, start=True, stop=True)
                            mm = nc.tensor.matmul(bank(half, 2, t), k_, a_, start=True, stop=True)
                        mm.then_inc(pe_s.sem, 1)

                def powers(c):
                    for level in range(1, LEVELS + 1):
                        for half in range(H):
                            pe.wait_ge(dve_s.sem, dve_s.at(DVE_N * c + 2 * max(0, level - 2) + half + 1))
                            if level >= 2:
                                pe.wait_ge(act_s.sem, act_s.at(ACT_N * c + 2 * (level - 2) + half + 1))
                            for s, t in systems(half):
                                m, mt = pair(level - 1, half, t)
                                if level < LEVELS:
                                    mm = nc.tensor.matmul(bank(half, 0, t), mt, m, start=True, stop=True)
                                if level < LEVELS - 1:
                                    mm = nc.tensor.matmul(bank(half, 1, t), m, mt, start=True, stop=True)
                                if level >= 2:
                                    mm = nc.tensor.matmul(bank(half, 2, t), m,
                                                          inv[(level - 1 + c) % 2][0:TT, s, :], start=True, stop=True)
                            mm.then_inc(pe_s.sem, 1)
                        if level == 1:
                            if c:
                                pe.wait_ge(S["dve2"].sem, S["dve2"].at(c))
                            for half in range(H):
                                for s, t in systems(half):
                                    mm = nc.tensor.matmul(PS[0:TT, 7, s * N:(s + 1) * N],
                                                          gram[0:TT, half, 2, t * TT:(t + 1) * TT],
                                                          v_tok[0:TT, t, c * P + half * N:c * P + (half + 1) * N],
                                                          start=True, stop=True)
                            mm.then_inc(S["pe2"].sem, 1)

                def results(c):
                    z = inv[(LEVELS + c) % 2]
                    pe.wait_ge(dve_s.sem, dve_s.at(DVE_N * (c + 1)))
                    if c:
                        pe.wait_ge(S["act2"].sem, S["act2"].at(2 * c))
                    for half in range(H):
                        for s, t in systems(half):
                            nc.tensor.matmul(PS[N * half:N * half + N, 6, t * TT:(t + 1) * TT],
                                             a_tok[0:TT, t, c * P + half * N:c * P + (half + 1) * N], z[0:TT, s, :],
                                             start=True, stop=True)
                    pe.wait_ge(S["act2"].sem, S["act2"].at(2 * c + 1))
                    for half in range(H):
                        for s, t in systems(half):
                            mm = nc.tensor.matmul(PS[0:TT, 7, s * N:(s + 1) * N], z[0:TT, s, :], lv[0:TT, s, :],
                                                  start=True, stop=True)
                    mm.then_inc(S["pe2"].sem, 1)

                grams(0)
                for c in range(C):
                    powers(c)
                    if c + 1 < C:
                        grams(c + 1)
                    results(c)

            @block.scalar
            def _(act):
                for c in range(C):
                    for level in range(1, LEVELS):
                        for half in range(H):
                            act.wait_ge(pe_s.sem, pe_s.at(PE_N * c + 2 * level + half + 1))
                            w = 2 if level < LEVELS - 1 else 1
                            nc.scalar.activation(power[level % 2][0:TT, half, 0:w, :],
                                                 PS[0:TT, 3 * half:3 * half + w, 0:NT * TT], ACT.Copy) \
                                .then_inc(act_s.sem, 1)
                        if level == 1:
                            act.wait_ge(S["pe2"].sem, S["pe2"].at(2 * c + 1))
                            nc.scalar.activation(lv[0:TT, :, :],
                                                 PS[0:TT, 7, 0:6 * N].rearrange("p (s n) -> p s n", n=N), ACT.Copy) \
                                .then_inc(S["act2"].sem, 1)
                    act.wait_ge(S["pe2"].sem, S["pe2"].at(2 * c + 2))
                    nc.scalar.activation(wt[:, c, :], PS[:, 6, 0:T], ACT.Copy).then_inc(S["act2"].sem, 1)

            @block.vector
            def _(dve):
                dve.wait_ge(S["load2"].sem, S["load2"].at(0))
                eye = ident[0:TT, 0:TT].unsqueeze(1)
                def triangles(c):
                    for half in range(H):
                        s3 = slice(3 * half, 3 * half + 3)
                        dve.wait_ge(pe_s.sem, pe_s.at(PE_N * c + half + 1))
                        split_t = "p k (t n) -> p k t n"
                        dve_own.step(dve, nc.vector.tensor_tensor(
                            gram[0:TT, half, :, :].rearrange(split_t, n=TT),
                            PS[0:TT, 3 * half:3 * half + 3, 0:NT * TT].rearrange(split_t, n=TT),
                            tri[0:TT, 0:3, :].unsqueeze(2).to_broadcast([TT, 3, NT, TT]), ALU.mult))
                        nc.vector.tensor_tensor(inv[(1 + c) % 2][0:TT, s3, :],
                                                gram[0:TT, half, 1, :].rearrange("p (t n) -> p t n", n=TT),
                                                eye.to_broadcast([TT, NT, TT]), ALU.add).then_inc(dve_s.sem, 1)

                triangles(0)
                for c in range(C):
                    for level in range(2, LEVELS + 1):
                        for half in range(H):
                            s3 = slice(3 * half, 3 * half + 3)
                            dve.wait_ge(pe_s.sem, pe_s.at(PE_N * c + 2 * level + half + 1))
                            dve.wait_ge(dve_s.sem, dve_s.at(DVE_N * c + 2 * (level - 2) + half + 1))
                            nc.vector.tensor_tensor(inv[(level + c) % 2][0:TT, s3, :], inv[(level - 1 + c) % 2][0:TT, s3, :],
                                                    PS[0:TT, 3 * half + 2, 0:NT * TT]
                                                    .rearrange("p (t n) -> p t n", n=TT), ALU.add).then_inc(dve_s.sem, 1)
                    if c + 1 < C:
                        triangles(c + 1)
                    dve.wait_ge(S["pe2"].sem, S["pe2"].at(2 * c + 2))
                    nc.vector.tensor_copy(
                        a_tok[0:TT, :, c * P:(c + 1) * P].rearrange("p t (h n) -> p h t n", n=N),
                        PS[0:TT, 7, 0:6 * N].rearrange("p (h t n) -> p h t n", h=H, n=N)).then_inc(S["dve2"].sem, 1)
        load.close(16)
        pe_s.close(C * 2 * (LEVELS + 1))
        act_s.close(C * 2 * (LEVELS - 1))
        dve_s.close(C * 2 * LEVELS)
        S["pe2"].close(2 * C)
        S["act2"].close(2 * C)
        S["dve2"].close(C)

        u_tok = a_tok
        chain = Area(hi_at)
        states = chain.take("states", [P, C, NCH + 2, N])
        state_out = chain.take("state_out", [P, 2, D])
        decayed = at("decayed", unit(10) + 12288 + 4096, [P, C, N])
        SLOTS = [(n, n + 1) for n in range(NCH - 2)] + [(NCH - 2, NCH), (NCH - 1, NCH + 1)]
        with nc.Block() as block:
            def cols(c, half):
                return slice(c * P + half * N, c * P + (half + 1) * N)

            @block.tensor
            def _(pe):
                pe.wait_ge(load.sem, load.at(0))
                for c in range(C):
                    mm = nc.tensor.transpose(PS[:, 6, c * N:(c + 1) * N],
                                             state_rows[0:N, 2 * c:2 * c + 2, :].rearrange("v h k -> v (h k)"),
                                             ident[0:N, 0:N])
                mm.then_inc(S["pe2"].sem, 1)
                for n, (cur, nxt) in enumerate(SLOTS):
                    t, p0 = n // 3, CH * (n % 3)
                    rows = slice(p0, p0 + CH)
                    for q in range(2):
                        pe.wait_ge(dve_s.sem, dve_s.at(1 + (4 * (n - 1) + 3 + q if n else 0)))
                        for c in range(4 * q, 4 * q + 4):
                            for half in range(H):
                                f = slice(N * half, N * half + N)
                                mm = nc.tensor.matmul(PS[rows, 2 * q + half, (c % 4) * N:(c % 4 + 1) * N],
                                                      wt[f, c, n * CH:(n + 1) * CH], states[f, c, cur, :],
                                                      start=True, stop=True)
                        mm.then_inc(pe_s.sem, 1)
                        for c in range(4 * q, 4 * q + 4):
                            for half in range(H):
                                nc.tensor.matmul(PS[N * half:N * half + N, 4 + q, (c % 4) * N:(c % 4 + 1) * N],
                                                 k_tok[rows, t, cols(c, half)], v_tok[rows, t, cols(c, half)],
                                                 start=c % 4 == 0, stop=False, skip_group_check=True)
                    for q in range(2):
                        pe.wait_ge(dve_s.sem, dve_s.at(1 + 4 * n + q + 1))
                        for c in range(4 * q, 4 * q + 4):
                            for half in range(H):
                                mm = nc.tensor.matmul(PS[N * half:N * half + N, 4 + q, (c % 4) * N:(c % 4 + 1) * N],
                                                      b_tok[rows, t, cols(c, half)], u_tok[rows, t, cols(c, half)],
                                                      start=False, stop=c % 4 == 3, skip_group_check=True)
                        mm.then_inc(pe_s.sem, 1)
                pe.wait_ge(dve_s.sem, dve_s.at(1 + 4 * NCH))
                for g in range(2):
                    for c in range(C):
                        mm = nc.tensor.transpose(PS[0:N, 2 * g + c // 4, (c % 4) * P:(c % 4 + 1) * P],
                                                 states[:, c, NCH + g, :], ident)
                    mm.then_inc(S["pe2"].sem, 1)

            @block.gpsimd
            def _(pool):
                nc.gpsimd.memset(states[:, :, 0, :], 0.0).then_inc(pool_s.sem, 1)
                for n, (cur, nxt) in enumerate(SLOTS):
                    for q in range(2):
                        pool.wait_ge(dve_s.sem, dve_s.at(1 + (4 * (n - 1) + 3 + q if n else 0)))
                        if n == 0:
                            pool.wait_ge(pool_s.sem, pool_s.at(1))
                        c4 = slice(4 * q, 4 * q + 4)
                        nc.gpsimd.tensor_tensor(decayed[:, c4, :], states[:, c4, cur, :],
                                                last_decay[:, c4, n:n + 1].to_broadcast([P, 4, N]), ALU.mult) \
                            .then_inc(pool_s.sem, 1)

            @block.vector
            def _(dve):
                dve.wait_ge(S["pe2"].sem, S["pe2"].at(1))
                dve.wait_ge(pool_s.sem, pool_s.at(1))
                nc.vector.tensor_copy(states[:, :, NCH - 1, :], PS[:, 6, :].rearrange("p (c n) -> p c n", n=N)) \
                    .then_inc(dve_s.sem, 1)
                for n, (cur, nxt) in enumerate(SLOTS):
                    t, p0 = n // 3, CH * (n % 3)
                    rows = slice(p0, p0 + CH)
                    for q in range(2):
                        dve.wait_ge(pe_s.sem, pe_s.at(4 * n + q + 1))
                        u = u_tok[rows, t, q * 4 * P:(q + 1) * 4 * P].rearrange("p (c h n) -> p h c n", h=H, n=N)
                        nc.vector.tensor_tensor(u, u, PS[rows, 2 * q:2 * q + 2, 0:4 * N]
                                                .rearrange("p h (c n) -> p h c n", n=N), ALU.add) \
                            .then_inc(dve_s.sem, 1)
                    for q in range(2):
                        dve.wait_ge(pe_s.sem, pe_s.at(4 * n + 3 + q))
                        dve.wait_ge(pool_s.sem, pool_s.at(2 + 2 * n + q))
                        nc.vector.tensor_tensor(states[:, 4 * q:4 * q + 4, nxt, :], decayed[:, 4 * q:4 * q + 4, :],
                                                PS[:, 4 + q, 0:4 * N].rearrange("p (c n) -> p c n", n=N), ALU.add) \
                            .then_inc(dve_s.sem, 1)

            @block.scalar
            def _(act):
                for g in range(2):
                    act.wait_ge(S["pe2"].sem, S["pe2"].at(2 + g))
                    nc.scalar.activation(state_out[0:N, g, :].rearrange("p (b n) -> p b n", b=2),
                                         PS[0:N, 2 * g:2 * g + 2, :], ACT.Copy).then_inc(act_s.sem, 1)

            @block.sync
            def _(sp):
                for g in range(2):
                    sp.wait_ge(act_s.sem, act_s.at(g + 1))
                    sp.dma_start(O[12 + g][0, 0].rearrange("h v k -> v h k"),
                                 state_out[0:N, g, :].rearrange("v (h k) -> v h k", k=N)).then_inc(S["store"].sem, 16)
        pe_s.close(4 * NCH)
        dve_s.close(1 + 4 * NCH)
        pool_s.close(1 + 2 * NCH)
        act_s.close(2)
        S["pe2"].close(3)
        S["store"].close(32)

        y = at("y", unit(2), ARC)
        cross = at("cross", unit(3), [P, 2, 2 * H, NT * TT])
        out_hi, out_lo = at("mixed_hi", unit(6), ARC, F32R), at("mixed_lo", unit(7), ARC, F32R)
        norm_area = Area(unit(11) + 3072)
        ysq = norm_area.take("y_squared", [P, 2, T])
        yinv = norm_area.take("y_inv_deviation", [P, 2, T])
        copied, mean_s, centred, squared_s, spread_s, inv_s, root_s, mixed_s = (S[n] for n in (
            "y_copied", "mean_ready", "centred", "centred_sq", "spread_ready", "spread_inv", "root_ready",
            "mixed_ready"))
        with nc.Block() as block:
            def head(x, c, half, t):
                return x[N * half:N * half + N, c, t * TT:(t + 1) * TT]

            @block.tensor
            def _(pe):
                def grams(c):
                    if c:
                        pe.wait_ge(dve_s.sem, dve_s.at(c))
                    for half in range(H):
                        for t in range(NT):
                            rr = head(ar[:, 1, :, :], c, half, t)
                            for kind, x in enumerate((bt, k)):
                                mm = nc.tensor.matmul(PS[0:TT, 2 * half + kind, t * TT:(t + 1) * TT],
                                                      head(x, c, half, t), rr, start=True, stop=True)
                    mm.then_inc(pe_s.sem, 1)

                def outputs(c):
                    pe.wait_ge(dve_s.sem, dve_s.at(c + 1))
                    if c >= 2:
                        pe.wait_ge(copied.sem, copied.at(c - 1))
                    bank = 4 + c % 2
                    for half in range(H):
                        f = slice(N * half, N * half + N)
                        hc = slice(c * P + half * N, c * P + (half + 1) * N)
                        for t in range(NT):
                            for kind, x in enumerate((u_tok, v_tok)):
                                nc.tensor.matmul(PS[f, bank, t * TT:(t + 1) * TT], x[0:TT, t, hc],
                                                 cross[0:TT, c % 2, 2 * half + kind, t * TT:(t + 1) * TT],
                                                 start=kind == 0, stop=False)
                            for n in range(3 * t, 3 * t + 3):
                                mm = nc.tensor.matmul(PS[f, bank, n * CH:(n + 1) * CH], states[f, c, n, :],
                                                      ar[f, 1, c, n * CH:(n + 1) * CH], start=False,
                                                      stop=n == 3 * t + 2)
                    mm.then_inc(S["pe2"].sem, 1)

                grams(0)
                for c in range(C + 2):
                    if c + 1 < C:
                        grams(c + 1)
                    if c < C:
                        outputs(c)
                    if 1 <= c <= C:
                        pe.wait_ge(copied.sem, copied.at(c))
                        if c >= 2:
                            pe.wait_ge(centred.sem, centred.at(c - 1))
                        nc.tensor.matmul(PS[:, 6, 0:T], head_ones, y[:, c - 1, :], start=True, stop=True) \
                            .then_inc(mean_s.sem, 1)
                    if c >= 2:
                        pe.wait_ge(squared_s.sem, squared_s.at(c - 1))
                        if c >= 3:
                            pe.wait_ge(inv_s.sem, inv_s.at(c - 2))
                        nc.tensor.matmul(PS[:, 7, 0:T], head_ones, ysq[:, c % 2, :], start=True, stop=True) \
                            .then_inc(spread_s.sem, 1)

            @block.vector
            def _(dve):
                V = nc.vector

                def mask(c):
                    dve.wait_ge(pe_s.sem, pe_s.at(c + 1))
                    if c >= 2:
                        dve.wait_ge(S["pe2"].sem, S["pe2"].at(c - 1))
                    V.tensor_tensor(cross[0:TT, c % 2, :, :].rearrange("p b (t n) -> p b t n", n=TT),
                                    PS[0:TT, 0:2 * H, 0:NT * TT].rearrange("p b (t n) -> p b t n", n=TT),
                                    tri[0:TT, 3:4, :].unsqueeze(1).to_broadcast([TT, 2 * H, NT, TT]), ALU.mult) \
                        .then_inc(dve_s.sem, 1)

                mask(0)
                for c in range(C + 2):
                    if c + 1 < C:
                        mask(c + 1)
                    if 1 <= c <= C:
                        dve.wait_ge(mean_s.sem, mean_s.at(c))
                        V.scalar_tensor_tensor(y[:, c - 1, :], PS[:, 6, 0:T], -1.0 / N, y[:, c - 1, :], ALU.mult,
                                               ALU.add).then_inc(centred.sem, 1)
                    if c >= 2:
                        d, inv = c - 2, yinv[:, c % 2, :]
                        dve.wait_ge(spread_s.sem, spread_s.at(d + 1))
                        dve_own.step(dve, V.tensor_scalar(inv, PS[:, 7, 0:T], 1.0 / N, LNX_EPS, ALU.mult, ALU.add))
                        V.reciprocal(inv, inv).then_inc(inv_s.sem, 1)
                        dve.wait_ge(root_s.sem, root_s.at(d + 1))
                        dve_own.step(dve, V.scalar_tensor_tensor(y[:, d, :], y[:, d, :], vec("rwkv_lnx_g", 0, d), inv,
                                                                 ALU.mult, ALU.mult))
                        dve_own.step(dve, V.scalar_tensor_tensor(y[:, d, :], y[:, d, :], vec("rwkv_lnx_b", 0, d),
                                                                 bonus[:, d, :], ALU.add, ALU.add))
                        V.tensor_tensor(y[:, d, :], y[:, d, :], gate[:, d, :], ALU.mult).then_inc(mixed_s.sem, 1)
                        dve.wait_ge(in_hi.sem, in_hi.at(d + 1))
                        V.tensor_tensor(out_lo[:, d, :], y[:, d, :], out_hi[:, d, :].bitcast(F32), ALU.subtract) \
                            .then_inc(in_lo.sem, 1)

            @block.scalar
            def _(act):
                for c in range(C + 2):
                    if c < C:
                        act.wait_ge(S["pe2"].sem, S["pe2"].at(c + 1))
                        nc.scalar.activation(y[:, c, :], PS[:, 4 + c % 2, 0:T], ACT.Copy).then_inc(copied.sem, 1)
                    if 1 <= c <= C:
                        act.wait_ge(centred.sem, centred.at(c))
                        nc.scalar.activation(ysq[:, (c - 1) % 2, :], y[:, c - 1, :], ACT.Square) \
                            .then_inc(squared_s.sem, 1)
                    if c >= 2:
                        act.wait_ge(inv_s.sem, inv_s.at(c - 1))
                        nc.scalar.activation(yinv[:, c % 2, :], yinv[:, c % 2, :], ACT.Sqrt).then_inc(root_s.sem, 1)
                        act.wait_ge(mixed_s.sem, mixed_s.at(c - 1))
                        nc.scalar.activation(out_hi[:, c - 2, :], y[:, c - 2, :], ACT.Copy).then_inc(in_hi.sem, 1)

            @block.sync
            def _(sp):
                sp.wait_ge(S["store"].sem, S["store"].at(0))
        for sig in (pe_s, S["pe2"], dve_s, copied, mean_s, centred, squared_s, spread_s, inv_s, root_s, mixed_s,
                    in_hi, in_lo):
            sig.close(C)
        project_residual("rwkv", "rwkv_w_o", halves=(out_hi, out_lo))
    STAGE = {"input": stage_input, "mlp": stage_mlp, "output": stage_output, "pool": stage_pool, "attn": stage_attn, "rwkv": stage_rwkv}
    for stage in STAGES:
        key = stage.rstrip("0123")
        STAGE[key](*([int(stage[len(key):])] if key in ("mlp", "pool") else []))


_INS = ["x_prompt", "x_sample", "state_pool", "cache_k", "cache_v", "cache_kidx", "state_shift", "state_wkv",
        "ln1_g", "ln2_g", "w_up", "w_down", "ln_f_g", "pool_w", "pool_scale", "attn_w_in", "attn_w_out",
        "rwkv_mix", "rwkv_w0", "rwkv_w1", "rwkv_w2", "rwkv_a0", "rwkv_a1", "rwkv_a2", "rwkv_g1", "rwkv_g2",
        "rwkv_k_k", "rwkv_k_a", "rwkv_r_k", "rwkv_w_r", "rwkv_w_k", "rwkv_w_v", "rwkv_w_o", "rwkv_lnx_g",
        "rwkv_lnx_b"]
_OUTS = [(1, SEQ, D), (1, DEC, D), (2, 1, HIST, D), (2, 1, HIST, D), (1, 1, SEQ, DH), (1, 1, DEC, DH),
         (1, 1, SEQ, DH), (1, 1, DEC, DH), (1, 1, SEQ, DI), (1, 1, DEC, DI), (1, 1, 1, D), (1, 1, 1, D),
         (1, 1, D // N, N, N), (1, 1, D // N, N, N)]


def kernel(**inputs):
    import concourse.bacc as bacc
    from concourse.bass_utils import run_bass_kernel_spmd

    nc = bacc.Bacc("TRN2", target_bir_lowering=False, num_devices=1)
    constants, order = shape_constants()
    arrays, views = {}, {}
    for name in _INS:
        arrays[f"in_{name}"] = np.ascontiguousarray(inputs[name])
    arrays["in_shape_constants"] = constants
    for key, a in arrays.items():
        views[key[3:]] = nc.dram_tensor(key, a.shape, mybir.dt.from_np(a.dtype), kind="ExternalInput").ap()
    outs = [nc.dram_tensor(f"out_{i}", shape, F32, kind="ExternalOutput").ap() for i, shape in enumerate(_OUTS)]
    build(nc, views, outs, order)
    r = run_bass_kernel_spmd(nc, [arrays], core_ids=[0])
    return tuple(r.results[0][f"out_{i}"] for i in range(len(_OUTS)))
```
